# Optimizing a Trainium2 kernel written in Bass

```python
import jax, jax.numpy as jnp
from jax import lax
import numpy as np

D_MODEL = 1024
BATCH = 1
SEQ = 256
DEPTH = 2

ROPE_THETA = 10000.0
Q_BLOCK = 128
NORM_EPS = 1e-6
SUBLN_EPS = 1e-5

DA_HEAD_DIM = 64
DA_V_DIM = 2 * DA_HEAD_DIM
DA_WIDTH = D_MODEL // 2
DA_HEADS = DA_WIDTH // DA_V_DIM

MLA_V_DIM = 128
MLA_WIDTH = D_MODEL - DA_WIDTH
MLA_HEADS = MLA_WIDTH // MLA_V_DIM
MLA_Q_RANK = D_MODEL // 4
MLA_KV_RANK = D_MODEL // 8
MLA_NOPE_DIM = 64
MLA_ROPE_DIM = 32
MLA_QK_DIM = MLA_NOPE_DIM + MLA_ROPE_DIM

MIX_WIDTH = DA_WIDTH + MLA_WIDTH

IN_SIZES = (
    DA_HEADS * 2 * DA_HEAD_DIM,
    DA_HEADS * 2 * DA_HEAD_DIM,
    DA_HEADS * DA_V_DIM,
    MLA_Q_RANK,
    MLA_KV_RANK,
    MLA_ROPE_DIM,
)
IN_COLS = sum(IN_SIZES)
IN_SPLITS = [int(v) for v in np.cumsum(IN_SIZES)[:-1]]

FF_DENSE = 2816
N_EXPERTS = 8
TOP_K = 2
FF_EXPERT = (7 * D_MODEL) // 2
N_DENSE = (DEPTH + 1) // 2
N_MOE = DEPTH // 2

kernel_name = "hybrid_diffattn_mla_moe_encoder"

def rmsnorm(x, g, eps=NORM_EPS):
    xf = x.astype(jnp.float32)
    y = xf * lax.rsqrt(jnp.mean(xf * xf, axis=-1, keepdims=True) + eps)
    return (y * g.astype(jnp.float32)).astype(x.dtype)

def rope_tables(positions, dim):
    inv = 1.0 / (ROPE_THETA ** (jnp.arange(0, dim, 2, dtype=jnp.float32) / dim))
    ang = positions.astype(jnp.float32)[..., None] * inv
    return jnp.cos(ang), jnp.sin(ang)

def apply_rope(x, cos, sin):
    extra = x.ndim - 3
    shp = cos.shape[:2] + (1,) * extra + cos.shape[-1:]
    c, s = cos.reshape(shp), sin.reshape(shp)
    xf = x.astype(jnp.float32)
    half = x.shape[-1] // 2
    x1, x2 = xf[..., :half], xf[..., half:]
    return jnp.concatenate([x1 * c - x2 * s, x1 * s + x2 * c], axis=-1).astype(x.dtype)

def map_query_blocks(fn, q):
    b, s = q.shape[:2]
    nb = s // Q_BLOCK
    qb = jnp.moveaxis(q.reshape((b, nb, Q_BLOCK) + q.shape[2:]), 1, 0)
    out = lax.map(fn, qb)
    out = jnp.moveaxis(out, 0, 1)
    return out.reshape((b, s) + out.shape[3:])

def diff_attention(q, k, v, lam):
    scale = DA_HEAD_DIM ** -0.5
    kf = k.astype(jnp.float32)
    vf = v.astype(jnp.float32)

    def block(qb):
        s = jnp.einsum('bqhcd,bkhcd->bhcqk', qb.astype(jnp.float32), kf) * scale
        p = jax.nn.softmax(s, axis=-1)
        w = p[:, :, 0] - lam * p[:, :, 1]
        return jnp.einsum('bhqk,bkhd->bqhd', w, vf)

    return map_query_blocks(block, q)

def softmax_attention(q, k, v, scale):
    kf = k.astype(jnp.float32)
    vf = v.astype(jnp.float32)

    def block(qb):
        s = jnp.einsum('bqhd,bkhd->bhqk', qb.astype(jnp.float32), kf) * scale
        p = jax.nn.softmax(s, axis=-1)
        return jnp.einsum('bhqk,bkhd->bqhd', p, vf)

    return map_query_blocks(block, q)

def swiglu(h, w_gate, w_up, w_down):
    return (jax.nn.silu(h @ w_gate) * (h @ w_up)) @ w_down

def moe_swiglu(h, router, w_gate, w_up, w_down):
    b, s, d = h.shape
    t = h.reshape(b * s, d)
    logits = (t @ router).astype(jnp.float32)
    top_v, top_i = lax.top_k(logits, TOP_K)
    gates = jax.nn.softmax(top_v, axis=-1)
    combine = jnp.sum(jax.nn.one_hot(top_i, N_EXPERTS, dtype=jnp.float32)
                      * gates[..., None], axis=1)
    y = jnp.zeros((b * s, d), jnp.float32)
    for e in range(N_EXPERTS):
        ye = swiglu(t, w_gate[e], w_up[e], w_down[e]).astype(jnp.float32)
        y = y + combine[:, e:e + 1] * ye
    return y.reshape(b, s, d).astype(h.dtype)

def setup_inputs(seed: int = 0) -> dict:
    key = jax.random.key(seed)
    ks = jax.random.split(key, 24)
    f32 = jnp.float32

    def nrm(k, shape, fan_in):
        return jax.random.normal(k, shape, f32) * (fan_in ** -0.5)

    def gain(k, shape):
        return 1.0 + 0.01 * jax.random.normal(k, shape, f32)

    return {
        "x": jax.random.normal(ks[0], (BATCH, SEQ, D_MODEL), f32),
        "positions": jnp.tile(jnp.arange(SEQ, dtype=jnp.int32)[None, :], (BATCH, 1)),
        "w_in": nrm(ks[1], (DEPTH, D_MODEL, IN_COLS), D_MODEL),
        "w_out": nrm(ks[2], (DEPTH, MIX_WIDTH, D_MODEL), MIX_WIDTH),
        "norm_mix": gain(ks[3], (DEPTH, D_MODEL)),
        "norm_ffn": gain(ks[4], (DEPTH, D_MODEL)),
        "da_lambda_q1": 0.1 * jax.random.normal(ks[5], (DEPTH, DA_HEAD_DIM), f32),
        "da_lambda_k1": 0.1 * jax.random.normal(ks[6], (DEPTH, DA_HEAD_DIM), f32),
        "da_lambda_q2": 0.1 * jax.random.normal(ks[7], (DEPTH, DA_HEAD_DIM), f32),
        "da_lambda_k2": 0.1 * jax.random.normal(ks[8], (DEPTH, DA_HEAD_DIM), f32),
        "da_subln": gain(ks[9], (DEPTH, DA_V_DIM)),
        "mla_q_norm": gain(ks[10], (DEPTH, MLA_Q_RANK)),
        "mla_w_uq": nrm(ks[11], (DEPTH, MLA_Q_RANK, MLA_HEADS * MLA_QK_DIM), MLA_Q_RANK),
        "mla_kv_norm": gain(ks[12], (DEPTH, MLA_KV_RANK)),
        "mla_w_ukv": nrm(ks[13], (DEPTH, MLA_KV_RANK, MLA_HEADS * (MLA_NOPE_DIM + MLA_V_DIM)), MLA_KV_RANK),
        "ffn_w_gate": nrm(ks[14], (N_DENSE, D_MODEL, FF_DENSE), D_MODEL),
        "ffn_w_up": nrm(ks[15], (N_DENSE, D_MODEL, FF_DENSE), D_MODEL),
        "ffn_w_down": nrm(ks[16], (N_DENSE, FF_DENSE, D_MODEL), FF_DENSE),
        "moe_router": nrm(ks[17], (N_MOE, D_MODEL, N_EXPERTS), D_MODEL),
        "moe_w_gate": nrm(ks[18], (N_MOE, N_EXPERTS, D_MODEL, FF_EXPERT), D_MODEL),
        "moe_w_up": nrm(ks[19], (N_MOE, N_EXPERTS, D_MODEL, FF_EXPERT), D_MODEL),
        "moe_w_down": nrm(ks[20], (N_MOE, N_EXPERTS, FF_EXPERT, D_MODEL), FF_EXPERT),
        "norm_final": gain(ks[21], (D_MODEL,)),
    }

def reference(x, positions, w_in, w_out, norm_mix, norm_ffn,
              da_lambda_q1, da_lambda_k1, da_lambda_q2, da_lambda_k2, da_subln,
              mla_q_norm, mla_w_uq, mla_kv_norm, mla_w_ukv,
              ffn_w_gate, ffn_w_up, ffn_w_down,
              moe_router, moe_w_gate, moe_w_up, moe_w_down, norm_final):
    b, s, _ = x.shape
    cos_da, sin_da = rope_tables(positions, DA_HEAD_DIM)
    cos_ml, sin_ml = rope_tables(positions, MLA_ROPE_DIM)

    for l in range(DEPTH):
        h = rmsnorm(x, norm_mix[l])
        proj = h @ w_in[l]
        da_q, da_k, da_v, c_q, c_kv, k_rope = jnp.split(proj, IN_SPLITS, axis=-1)

        da_q = apply_rope(da_q.reshape(b, s, DA_HEADS, 2, DA_HEAD_DIM), cos_da, sin_da)
        da_k = apply_rope(da_k.reshape(b, s, DA_HEADS, 2, DA_HEAD_DIM), cos_da, sin_da)
        da_v = da_v.reshape(b, s, DA_HEADS, DA_V_DIM)
        lambda_init = 0.8 - 0.6 * float(np.exp(-0.3 * l))
        lam = (jnp.exp(jnp.sum(da_lambda_q1[l].astype(jnp.float32) * da_lambda_k1[l].astype(jnp.float32)))
               - jnp.exp(jnp.sum(da_lambda_q2[l].astype(jnp.float32) * da_lambda_k2[l].astype(jnp.float32)))
               + lambda_init)
        o_da = diff_attention(da_q, da_k, da_v, lam)
        o_da = rmsnorm(o_da, da_subln[l], SUBLN_EPS) * (1.0 - lambda_init)
        o_da = o_da.reshape(b, s, DA_WIDTH).astype(x.dtype)

        q = (rmsnorm(c_q, mla_q_norm[l]) @ mla_w_uq[l]).reshape(b, s, MLA_HEADS, MLA_QK_DIM)
        q = jnp.concatenate([q[..., :MLA_NOPE_DIM],
                             apply_rope(q[..., MLA_NOPE_DIM:], cos_ml, sin_ml)], axis=-1)
        kv = (rmsnorm(c_kv, mla_kv_norm[l]) @ mla_w_ukv[l]).reshape(
            b, s, MLA_HEADS, MLA_NOPE_DIM + MLA_V_DIM)
        k_nope, v_ml = kv[..., :MLA_NOPE_DIM], kv[..., MLA_NOPE_DIM:]
        k_pe = apply_rope(k_rope[:, :, None, :], cos_ml, sin_ml)
        k = jnp.concatenate([k_nope, jnp.broadcast_to(k_pe, (b, s, MLA_HEADS, MLA_ROPE_DIM))], axis=-1)
        o_ml = softmax_attention(q, k, v_ml, MLA_QK_DIM ** -0.5)
        o_ml = o_ml.reshape(b, s, MLA_WIDTH).astype(x.dtype)

        x = x + jnp.concatenate([o_da, o_ml], axis=-1) @ w_out[l]

        h = rmsnorm(x, norm_ffn[l])
        if l % 2 == 0:
            i = l // 2
            x = x + swiglu(h, ffn_w_gate[i], ffn_w_up[i], ffn_w_down[i])
        else:
            i = l // 2
            x = x + moe_swiglu(h, moe_router[i], moe_w_gate[i], moe_w_up[i], moe_w_down[i])

    return rmsnorm(x, norm_final)


_drawn_inputs = setup_inputs


def setup_inputs(seed=0):
    import zlib

    import numpy as np

    out = dict(_drawn_inputs(seed))
    spreads = {}
    factors = {'norm_ffn': 6.272,
     'da_subln': 4.694,
     'mla_q_norm': 8.0,
     'mla_kv_norm': 8.0,
     'norm_final': 5.486}
    for name, (base, spread) in spreads.items():
        noise = np.random.default_rng([zlib.crc32(name.encode()), seed]).standard_normal(out[name].shape)
        drawn = base * np.exp(spread * noise) if base else spread * noise
        out[name] = __import__('jax').numpy.asarray(drawn.astype(out[name].dtype))
    for name, factor in factors.items():
        out[name] = (out[name] * factor).astype(out[name].dtype)
    return out
```

```python
from contextlib import ExitStack

import numpy as np

import concourse.bass as bass
from concourse import mybir

P = 128
D = 1024
S = 256
TOKS = S // P
KC = D // P
DEPTH = 2
NORM_EPS, SUBLN_EPS = 1e-6, 1e-5

DA_HEADS, DA_DIM, DA_V = 4, 64, 128
DA_COLS = DA_HEADS * 2 * DA_DIM
HALF = DA_DIM // 2
ML_HEADS, NOPE, ROPE, ML_V = 4, 64, 32, 128
ML_QK = NOPE + ROPE
Q_RANK, KV_RANK = 256, 128
ML_Q_COLS = ML_HEADS * ML_QK
KV_HEAD = NOPE + ML_V
KV_COLS = ML_HEADS * KV_HEAD
REST = Q_RANK + KV_RANK + ROPE
IN_COLS = 3 * DA_COLS + REST
FREQS = HALF + ROPE // 2

FF_DENSE, FF_EXPERT = 2816, 3584
EXPERTS = 8
FB = 512
DENSE_STEPS = -(-FF_DENSE // FB)
DENSE_LAST = FF_DENSE - (DENSE_STEPS - 1) * FB
STEPS = FF_EXPERT // FB

UNIT = 1024
TILE_UNITS = 4
SLOTS = 3
RING = 6
AHEAD = 5
LAYER_UNITS = (4 + 2) * TILE_UNITS
DENSE_UNITS = 2 * TILE_UNITS * DENSE_STEPS + TILE_UNITS * (DENSE_STEPS - 1) + DENSE_LAST // P
DENSE_TILES = 3 * DENSE_STEPS
STEP_UNITS, STEP_TILES = 3 * TILE_UNITS, 3
EXPERT_UNITS, EXPERT_TILES = STEPS * STEP_UNITS, STEPS * STEP_TILES
LAYER_TILES = 6
UNIT0 = (0, LAYER_UNITS + DENSE_UNITS)
TILE0 = (0, LAYER_TILES + DENSE_TILES)
MOE_UNIT, MOE_TILE = UNIT0[1] + LAYER_UNITS, TILE0[1] + LAYER_TILES
DENSE_UNIT, DENSE_TILE = LAYER_UNITS, LAYER_TILES
SHORT_TILE = DENSE_TILE + DENSE_TILES - 1
SHORT_BY = TILE_UNITS - DENSE_LAST // P
assert STEP_UNITS % RING == 0 and STEP_TILES % SLOTS == 0

JOBS = 12
DA_JOBS = DA_HEADS * TOKS

TWO_PI = 2 * np.pi
_C1 = float(np.float32(np.round(TWO_PI * 2**7) / 2**7))
_C2 = float(np.float32(np.round((TWO_PI - _C1) * 2**19) / 2**19))
_C3 = float(np.float32(TWO_PI - _C1 - _C2))
PI_DOWN = 3.1415925


def lambda_init(layer):
    return 0.8 - 0.6 * float(np.exp(-0.3 * layer))


def rope_freqs():
    f = [1.0 / (np.float32(10000.0) ** (np.arange(0, d, 2, dtype=np.float32) / np.float32(d))) for d in (DA_DIM, ROPE)]
    return np.concatenate(f).astype(np.float32)[None, :]


class Place:

    def __init__(self, unit, tile, e=None, fb=None):
        self.unit, self.tile, self.e, self.fb = unit, tile, e, fb

    def plus(self, units, tiles):
        return Place(self.unit + units, self.tile + tiles, self.e, self.fb)

    def _dyn(self, n, per_expert, per_step):
        for reg, per in ((self.e, per_expert), (self.fb, per_step)):
            if reg is not None:
                n = reg * per + n
        return n

    def used(self, i):
        return self._dyn(self.unit + i + 1, EXPERT_UNITS, STEP_UNITS)

    def ring(self, i):
        return (self.unit + i) % RING

    def slot(self, j):
        return (self.tile + j) % SLOTS

    def loaded(self, j):
        return self._dyn(16 * ((self.tile + j) // SLOTS + 1), 16 * EXPERT_TILES // SLOTS, 16 * STEP_TILES // SLOTS)

    def freed(self, j):
        t = self.tile + j - SLOTS
        short = SHORT_BY if t >= SHORT_TILE else 0
        return self._dyn(TILE_UNITS * (t + 1) - short, EXPERT_UNITS, STEP_UNITS)


def encoder(nc, x_in, positions, w_in, w_out, norm_mix, norm_ffn, lq1, lk1, lq2, lk2, da_subln, mla_q_norm, mla_w_uq,
            mla_kv_norm, mla_w_ukv, ffn_gate, ffn_up, ffn_down, router, moe_gate, moe_up, moe_down, norm_final,
            freqs, out):
    F32, F32R, I32 = mybir.dt.float32, mybir.dt.float32r, mybir.dt.int32
    ALU, ACT, AX = mybir.AluOpType, mybir.ActivationFunctionType, mybir.AxisListType

    with ExitStack() as ctx:
        def sb(name, shape, dt=F32):
            return ctx.enter_context(nc.sbuf_tensor(name, shape, dt))

        def sem(name):
            return ctx.enter_context(nc.semaphore(name))

        raw = [sb(f"raw{i}", [P, TILE_UNITS * UNIT]) for i in range(SLOTS)]
        w_hi = [sb(f"w_hi{i}", [P, UNIT], F32R) for i in range(RING)]
        w_lo = [sb(f"w_lo{i}", [P, UNIT], F32R) for i in range(RING)]

        x = sb("x", [P, TOKS, D])
        h = sb("h", [P, TOKS, D])
        t_hi = sb("t_hi", [P, KC * S], F32R)
        t_lo = sb("t_lo", [P, KC * S], F32R)
        hT_hi = t_hi[:, :].rearrange("p (c t) -> p c t", c=KC)
        hT_lo = t_lo[:, :].rearrange("p (c t) -> p c t", c=KC)
        h_hi = t_hi[:, :].rearrange("p (t d) -> p t d", t=TOKS)
        h_lo = t_lo[:, :].rearrange("p (t d) -> p t d", t=TOKS)
        g_hi = sb("g_hi", [P, KC, P], F32R)
        g_lo = sb("g_lo", [P, KC, P], F32R)
        aT_hi = sb("aT_hi", [P, FB // P, S], F32R)
        aT_lo = sb("aT_lo", [P, FB // P, S], F32R)
        gain = [sb(f"gain{i}", [P, D]) for i in range(2)]

        ARENA = 12672
        arena = sb("arena", [P, ARENA])
        used_cols = [0]

        def cut(cols):
            a = used_cols[0]
            used_cols[0] = a + cols
            assert used_cols[0] <= ARENA
            return arena[:, a:a + cols]

        def view(ap, pattern, **sizes):
            return ap.rearrange(pattern, **sizes)

        q_rot = view(cut(TOKS * DA_COLS), "p (t c) -> p t c", t=TOKS)
        k_rot_raw = cut(TOKS * KV_COLS)
        k_rot = view(k_rot_raw[:, 0:TOKS * DA_COLS], "p (t c) -> p t c", t=TOKS)
        v_da = view(cut(TOKS * DA_COLS), "p (t c) -> p t c", t=TOKS)
        rest = view(cut(TOKS * REST), "p (t c) -> p t c", t=TOKS)
        qT_da = view(cut(DA_HEADS * S), "p (h t) -> p h t", h=DA_HEADS)
        kT_da = view(cut(DA_HEADS * S), "p (h t) -> p h t", h=DA_HEADS)
        qT_ml = view(cut(ML_HEADS * S), "p (h t) -> p h t", h=ML_HEADS)
        kT_ml = view(cut(ML_HEADS * S), "p (h t) -> p h t", h=ML_HEADS)
        latent_raw, cqT_raw = cut(TOKS * (Q_RANK + KV_RANK)), cut(2 * S)
        latent = view(latent_raw, "p (t c) -> p t c", t=TOKS)
        cqT = view(cqT_raw, "p (c t) -> p c t", c=2)
        ckT = cut(S)
        probs_raw = [cut(2 * S) for _ in range(2)]
        probs = [view(a, "p (c k) -> p c k", c=2) for a in probs_raw]
        mixed = [cut(S) for _ in range(2)]
        probsT = [cut(2 * S) for _ in range(2)]
        k_pe = view(cut(TOKS * ROPE), "p (t c) -> p t c", t=TOKS)
        q_ml = view(q_rot.rearrange("p t c -> p (t c)")[:, 0:TOKS * ML_Q_COLS], "p (t h c) -> p t h c", t=TOKS, c=ML_QK)
        k_ml = view(k_rot_raw[:, 0:TOKS * ML_Q_COLS], "p (t h c) -> p t h c", t=TOKS, c=ML_QK)
        v_ml_at = TOKS * (DA_COLS + KV_COLS + DA_COLS + REST) + 2 * DA_HEADS * S + 2 * ML_HEADS * S
        v_ml = view(arena[:, v_ml_at:v_ml_at + TOKS * ML_HEADS * ML_V], "p (t c) -> p t c", t=TOKS)
        silu = view(arena[:, 0:TOKS * FB], "p (t c) -> p t c", t=TOKS)
        act = view(arena[:, 1024:1024 + TOKS * FB], "p (t c) -> p t c", t=TOKS)
        y_sb = arena[:, 2048:2048 + D]
        junk = sb("junk", [P, Q_RANK])

        w_uq = sb("w_uq", [P, 2, ML_Q_COLS])
        w_ukv = sb("w_ukv", [P, KV_COLS])
        latent_gain = sb("latent_gain", [P, Q_RANK + KV_RANK])
        sub_gain = sb("sub_gain", [P, DA_V])
        sub_scaled = sb("sub_scaled", [P, DA_V])
        lam_vecs = view(arena[:, 0:4 * DEPTH * DA_DIM], "p (i l c) -> p i l c", i=4, l=DEPTH)
        lam_prod = view(arena[:, 512:512 + 2 * DEPTH * DA_DIM], "p (i l c) -> p i l c", i=2, l=DEPTH)
        angle = view(arena[:, 768:768 + TOKS * FREQS], "p (t c) -> p t c", t=TOKS)
        turns_f = view(arena[:, 896:896 + TOKS * FREQS], "p (t c) -> p t c", t=TOKS)
        lam_dots = sb("lam_dots", [P, 2, DEPTH])
        lam_exps = sb("lam_exps", [P, 2, DEPTH])
        neg_lam = sb("neg_lam", [P, DEPTH])
        pos_i = sb("pos_i", [P, TOKS], I32)
        pos_f = sb("pos_f", [P, TOKS])
        freq = sb("freq", [P, FREQS])
        turns_i = sb("turns_i", [P, TOKS, FREQS], I32)
        sines = sb("sines", [P, 2, TOKS, FREQS])
        cos_t = sb("cos_t", [P, TOKS, DA_DIM + ROPE])
        sin_t = sb("sin_t", [P, TOKS, DA_DIM + ROPE])
        eps_t = sb("eps_t", [P, 2])
        mean_sq = sb("mean_sq", [P, TOKS])
        norm_sd = sb("norm_sd", [P, TOKS])
        norm_r = sb("norm_r", [P, TOKS])
        lat_sq = sb("lat_sq", [P, TOKS, 2])
        lat_sd = sb("lat_sd", [P, TOKS, 2])
        lat_r = sb("lat_r", [P, TOKS, 2])
        o_sq = sb("o_sq", [P, TOKS, DA_HEADS])
        o_sd = sb("o_sd", [P, TOKS, DA_HEADS])
        o_r = sb("o_r", [P, TOKS, DA_HEADS])
        row_max = sb("row_max", [P, JOBS, 2])
        neg_max = sb("neg_max", [P, JOBS, 2])
        row_sum = sb("row_sum", [P, JOBS, 2])
        row_inv = sb("row_inv", [P, JOBS, 2])
        mix_coef = sb("mix_coef", [P, JOBS])
        ident = sb("ident", [P, P])
        before = sb("before", [P, P])
        ones = sb("ones", [P, P])
        slot_no = sb("slot_no", [P, P])
        expert_no = sb("expert_no", [P, TOKS, EXPERTS])
        r_w = sb("r_w", [P, KC, EXPERTS])
        r_hi = sb("r_hi", [P, KC, EXPERTS], F32R)
        r_lo = sb("r_lo", [P, KC, EXPERTS], F32R)
        rt = {n: sb(f"r_{n}", [P, TOKS, EXPERTS]) for n in
              ("logits", "eq", "cand", "first", "logits2", "eq2", "cand2", "second", "w1", "w2")}
        rs = {n: sb(f"r_{n}", [P, TOKS]) for n in ("m1", "i1", "m2", "i2", "d", "e", "e1", "g1", "g2")}
        mask = sb("mask", [P, TOKS, EXPERTS + 1])
        share = sb("share", [P, TOKS, EXPERTS + 1])
        rank = [sb(f"rank{i}", [P, TOKS, EXPERTS + 1]) for i in range(2)]
        most = sb("most", [P, 1])
        over = sb("over", [P, 1])
        over_i = sb("over_i", [P, 1], I32)
        pick = sb("pick", [P, TOKS, P], F32R)
        give = sb("give", [P, TOKS, P])
        giveT = sb("giveT", [P, TOKS, P])

        psum = ctx.enter_context(nc.psum_tensor("psum", [P, 8, 512], F32))
        bank = [psum[:, i, :] for i in range(8)]
        scores = [psum[:, 2 * i:2 * i + 2, 0:S] for i in range(2)]

        loaded = [sem(f"weights_loaded{i}") for i in range(SLOTS)]
        hi_ready, lo_ready, unit_used = sem("hi_ready"), sem("lo_ready"), sem("unit_used")
        x_loaded, rope_in, lam_in = sem("x_loaded"), sem("rope_in"), sem("lam_in")
        gain_loaded = [sem(f"gain_loaded{i}") for i in range(2)]
        small_loaded, router_loaded = sem("small_loaded"), sem("router_loaded")
        out_stored = sem("out_stored")
        consts = sem("consts")
        iotas = sem("iotas")
        sd_ready = sem("sd_ready")
        h_ready = sem("h_ready")
        turned, tT_hi, tT_lo = sem("turned"), sem("tT_hi"), sem("tT_lo")
        rotated = sem("rotated")
        v_copied = sem("v_copied")
        da_turned, da_qT, da_kT = sem("da_turned"), sem("da_qT"), sem("da_kT")
        lat_sd_ready, lat_ready = sem("lat_sd_ready"), sem("lat_ready")
        lat_turned, cqT_ready, ckT_ready = sem("lat_turned"), sem("cqT_ready"), sem("ckT_ready")
        ml_proj = sem("ml_proj")
        ml_nope, ml_qk = sem("ml_nope"), sem("ml_qk")
        ml_turned, ml_qT, ml_kT = sem("ml_turned"), sem("ml_qT"), sem("ml_kT")
        scored, max_ready, probs_ready, mix_ready = sem("scored"), sem("max_ready"), sem("probs_ready"), sem("mix_ready")
        probs_turned, probsT_ready, pv_ready, o_ready = (sem("probs_turned"), sem("probsT_ready"), sem("pv_ready"),
                                                         sem("o_ready"))
        o_sd_ready = sem("o_sd_ready")
        x_added = sem("x_added")
        angles, sines_ready = sem("angles"), sem("sines_ready")
        dots, lam_exp = sem("dots"), sem("lam_exp")
        vstep, astep = sem("vstep"), sem("astep")
        silu_ready, act_ready = sem("silu_ready"), sem("act_ready")
        act_turned, aT_hi_ready, aT_lo_ready = sem("act_turned"), sem("aT_hi_ready"), sem("aT_lo_ready")
        r_split, routed_ps, router_exp, router_d = sem("r_split"), sem("routed_ps"), sem("router_exp"), sem("router_d")
        mask_ready, ranked_ps, flag_ready, h_hi_ready, h_split = (sem("mask_ready"), sem("ranked_ps"), sem("flag_ready"),
                                                                  sem("h_hi_ready"), sem("h_split"))
        pick_ready, give_ready, gathered, g_hi_ready, g_lo_ready = (sem("pick_ready"), sem("give_ready"),
                                                                    sem("gathered"), sem("g_hi_ready"), sem("g_lo_ready"))
        give_turned, giveT_ready = sem("give_turned"), sem("giveT_ready")
        y_ready, scattered, scatter_added = sem("y_ready"), sem("scattered"), sem("scatter_added")

        w_in_v = w_in.rearrange("l (c p) n -> l p c n", p=P)
        w_out_v = w_out.rearrange("l (c p) n -> l p c n", p=P)
        gate_v = ffn_gate.rearrange("o (c p) n -> o p c n", p=P)
        up_v = ffn_up.rearrange("o (c p) n -> o p c n", p=P)
        mgate_v = moe_gate.rearrange("o e (c p) n -> (o e) p c n", p=P)
        mup_v = moe_up.rearrange("o e (c p) n -> (o e) p c n", p=P)
        down_v = ffn_down[0, 0:(DENSE_STEPS - 1) * FB, :].rearrange("(b p c) n -> b p (c n)", p=P, c=FB // P)
        down_last_v = ffn_down[0, (DENSE_STEPS - 1) * FB:, :].rearrange("(p c) n -> p (c n)", p=P)
        mdown_v = moe_down.rearrange("o e (b p c) n -> (o e) b p (c n)", p=P, c=FB // P)
        x_v = x_in.rearrange("o (t p) d -> p (o t) d", p=P)
        out_v = out.rearrange("o (t p) d -> p (o t) d", p=P)
        gains_v = [norm_mix[0:1], norm_ffn[0:1], norm_mix[1:2], norm_ffn[1:2], norm_final.rearrange("(o d) -> o d", o=1)]

        def cols_of(step, moe):
            return DENSE_LAST if not moe and step == DENSE_STEPS - 1 else FB

        block = ctx.enter_context(nc.Block())

        @block.sync
        def _(sp):
            def load(place, j, src, cols=FB):
                if place.tile + j >= SLOTS:
                    sp.wait_ge(lo_ready, place.freed(j))
                if src.ndim == 3:
                    dst = raw[place.slot(j)][:, :].rearrange("p (c n) -> p c n", c=KC)[:, :, 0:cols]
                else:
                    dst = raw[place.slot(j)][:, 0:cols]
                sp.dma_start(dst, src).then_inc(loaded[place.slot(j)], 16)

            def load_gain(k):
                if k >= 2:
                    sp.wait_ge(h_ready, {2: 1, 3: 3, 4: 4}[k])
                sp.dma_start(gain[k % 2][:, :], gains_v[k].to_broadcast([P, D])).then_inc(gain_loaded[k % 2], 16)

            def load_small(l):
                if l:
                    sp.wait_ge(ml_proj, 3)
                    sp.wait_ge(lat_ready, 1)
                sp.dma_start(w_uq[:, :, :], mla_w_uq[l].rearrange("(c p) n -> p c n", p=P)).then_inc(small_loaded, 16)
                sp.dma_start(w_ukv[:, :], mla_w_ukv[l]).then_inc(small_loaded, 16)
                sp.dma_start(latent_gain[:, 0:Q_RANK], mla_q_norm[l:l + 1].to_broadcast([P, Q_RANK])).then_inc(small_loaded, 16)
                sp.dma_start(latent_gain[:, Q_RANK:], mla_kv_norm[l:l + 1].to_broadcast([P, KV_RANK])).then_inc(small_loaded, 16)
                sp.dma_start(sub_gain[:, :], da_subln[l:l + 1].to_broadcast([P, DA_V])).then_inc(small_loaded, 16)

            def attention(l):
                place = Place(UNIT0[l], TILE0[l])
                for n in range(4):
                    cols = min(FB, IN_COLS - n * FB)
                    load(place, n, w_in_v[l, :, :, n * FB:n * FB + cols], cols)
                    if n == 1:
                        load_small(l)
                        load_gain(2 * l + 1)
                for n in range(2):
                    load(place, 4 + n, w_out_v[l, :, :, n * FB:(n + 1) * FB])

            for t in range(TOKS):
                sp.dma_start(x[:, t, :], x_v[:, t, :]).then_inc(x_loaded, 16)
            load_gain(0)
            attention(0)
            place = Place(DENSE_UNIT, DENSE_TILE)
            load(place, 0, gate_v[0, :, :, 0:FB])
            load(place, 1, up_v[0, :, :, 0:FB])
            with sp.Fori(0, DENSE_STEPS - 2) as i:
                step = Place(DENSE_UNIT + 8, DENSE_TILE + 2, fb=i)
                load(step, 0, gate_v[0, :, :, bass.ds((i + 1) * FB, FB)])
                load(step, 1, up_v[0, :, :, bass.ds((i + 1) * FB, FB)])
                load(step, 2, down_v[i], FB // P * D)
            last = Place(DENSE_UNIT + 8 + STEP_UNITS * (DENSE_STEPS - 2), DENSE_TILE + 2 + STEP_TILES * (DENSE_STEPS - 2))
            load(last, 0, gate_v[0, :, :, (DENSE_STEPS - 1) * FB:FF_DENSE], DENSE_LAST)
            load(last, 1, up_v[0, :, :, (DENSE_STEPS - 1) * FB:FF_DENSE], DENSE_LAST)
            load(last, 2, down_v[DENSE_STEPS - 2], FB // P * D)
            load(last, 3, down_last_v, DENSE_LAST // P * D)
            load_gain(2)
            attention(1)
            sp.dma_start(r_w[:, :, :], router[0].rearrange("(c p) n -> p c n", p=P)).then_inc(router_loaded, 16)

            def experts(unit0, tile0):
                with sp.Fori(0, EXPERTS) as e:
                    first = Place(unit0, tile0, e=e)
                    load(first, 0, mgate_v[e, :, :, 0:FB])
                    load(first, 1, mup_v[e, :, :, 0:FB])
                    with sp.Fori(0, STEPS - 1) as i:
                        step = Place(unit0 + 8, tile0 + 2, e=e, fb=i)
                        load(step, 0, mgate_v[e, :, :, bass.ds((i + 1) * FB, FB)])
                        load(step, 1, mup_v[e, :, :, bass.ds((i + 1) * FB, FB)])
                        load(step, 2, mdown_v[e, i], FB // P * D)
                    load(Place(unit0 + 8 + STEP_UNITS * (STEPS - 1), tile0 + 2 + STEP_TILES * (STEPS - 1), e=e), 0,
                         mdown_v[e, STEPS - 1], FB // P * D)

            experts(MOE_UNIT, MOE_TILE)
            load_gain(4)
            sp.wait_ge(flag_ready, 1)
            some_over = sp.value_load(over_i[0:1, 0:1], min_val=0, max_val=1)
            with sp.If(some_over == 1):
                experts(MOE_UNIT + EXPERTS * EXPERT_UNITS, MOE_TILE + EXPERTS * EXPERT_TILES)
            for t in range(TOKS):
                sp.wait_ge(h_ready, 7 + t)
                sp.dma_start(out_v[:, t, :], h[:, t, :]).then_inc(out_stored, 16)
            sp.wait_ge(out_stored, 16 * TOKS)

        @block.gpsimd
        def _(pool):
            pool.memset(ident[:, :], 0.0).then_inc(iotas, 1)
            pool.memset(before[:, :], 1.0).then_inc(iotas, 1)
            pool.memset(ones[:, :], 1.0).then_inc(consts, 1)
            pool.memset(eps_t[:, 0:1], NORM_EPS).then_inc(consts, 1)
            pool.memset(eps_t[:, 1:2], SUBLN_EPS).then_inc(consts, 1)
            pool.wait_ge(iotas, 2)
            pool.affine_select(out=ident[:, :], in_=ident[:, :], compare_op=ALU.not_equal, fill=1.0, base=0,
                               pattern=[[-1, P]], channel_multiplier=1).then_inc(consts, 1)
            pool.affine_select(out=before[:, :], in_=before[:, :], compare_op=ALU.is_gt, fill=0.0, base=0,
                               pattern=[[1, P]], channel_multiplier=-1).then_inc(consts, 1)
            pool.iota(slot_no[:, :], pattern=[[1, P]], base=0, channel_multiplier=0,
                      allow_small_or_imprecise_dtypes=True).then_inc(consts, 1)
            pool.iota(expert_no[:, :, :], pattern=[[0, TOKS], [1, EXPERTS]], base=-EXPERTS, channel_multiplier=0,
                      allow_small_or_imprecise_dtypes=True).then_inc(consts, 1)
            for tab in (mask, share, rank[0], rank[1]):
                pool.memset(tab[:, :, EXPERTS:EXPERTS + 1], 0.0).then_inc(consts, 1)

        CONSTS = 11

        @block.scalar
        def _(sc):
            steps = [0]

            def chain(ins):
                steps[0] += 1
                ins.then_inc(astep, 1)
                sc.wait_ge(astep, steps[0])

            def high(place, units, cols=FB):
                for i in units:
                    if i % TILE_UNITS == 0:
                        sc.wait_ge(loaded[place.slot(i // TILE_UNITS)], place.loaded(i // TILE_UNITS))
                    if place.unit + i >= RING:
                        sc.wait_ge(unit_used, place.used(i - RING))
                    src = raw[place.slot(i // TILE_UNITS)][:, i % TILE_UNITS * UNIT:(i % TILE_UNITS + 1) * UNIT]
                    dst = w_hi[place.ring(i)][:, :]
                    if cols < FB:
                        src = src.rearrange("p (c n) -> p c n", c=2)[:, :, 0:cols]
                        dst = dst.rearrange("p (c n) -> p c n", c=2)[:, :, 0:cols]
                    sc.activation(dst, src, ACT.Copy).then_inc(hi_ready, 1)

            def norm(k):
                if k:
                    sc.wait_ge(x_added, {1: 2, 2: 3, 3: 5, 4: 6}[k])
                for t in range(TOKS):
                    if k == 0:
                        sc.wait_ge(x_loaded, 16 * TOKS)
                    chain(sc.activation(h[:, t, :], x[:, t, :], ACT.Square, scale=D ** -0.5, accum_out=mean_sq[:, t:t + 1]))
                if k == 0:
                    sc.wait_ge(consts, CONSTS)
                sc.activation(norm_sd[:, :], mean_sq[:, :], ACT.Sqrt, bias=eps_t[:, 0:1]).then_inc(sd_ready, 1)

            def turn(k):
                for g in range(4):
                    sc.wait_ge(turned, 4 * k + g + 1)
                    t, c = g // 2, 4 * (g % 2)
                    sc.activation(hT_hi[:, c:c + 4, t * P:(t + 1) * P], bank[4 + g][:, :].rearrange("p (c t) -> p c t", c=4),
                                  ACT.Copy).then_inc(tT_hi, 1)

            def attention(l):
                place = Place(UNIT0[l], TILE0[l])
                norm(2 * l)
                turn(3 * l)
                high(place, range(AHEAD, 12))
                high(place, range(12, 16), IN_COLS - 3 * FB)
                high(place, [16])
                sc.wait_ge(unit_used, place.used(11))
                for t in range(TOKS):
                    ins = sc.activation(v_da[:, t, :], bank[t][:, :], ACT.Copy)
                ins.then_inc(v_copied, 1)
                high(place, range(17, 16 + AHEAD))
                sc.wait_ge(unit_used, place.used(15))
                for t in range(TOKS):
                    ins = sc.activation(rest[:, t, :], bank[2 + t][:, 0:REST], ACT.Copy)
                ins.then_inc(v_copied, 1)
                sc.wait_ge(v_copied, 2 * l + 2)
                for t in range(TOKS):
                    for i, (a, n) in enumerate(((0, Q_RANK), (Q_RANK, KV_RANK))):
                        ins = sc.activation(junk[:, 0:n], rest[:, t, a:a + n], ACT.Square, scale=n ** -0.5,
                                            accum_out=lat_sq[:, t, i:i + 1])
                        chain(ins)
                sc.activation(lat_sd[:, :, :], lat_sq[:, :, :], ACT.Sqrt, bias=eps_t[:, 0:1]).then_inc(lat_sd_ready, 1)
                for g in range(2):
                    sc.wait_ge(da_turned, 4 * l + g + 1)
                    sc.activation(qT_da[:, 2 * g:2 * g + 2, :], bank[4 + g][:, :].rearrange("p (h t) -> p h t", h=2),
                                  ACT.Copy).then_inc(da_qT, 1)
                sc.wait_ge(lat_turned, 2 * l + 1)
                sc.activation(cqT[:, :, :], bank[0][:, :].rearrange("p (c t) -> p c t", c=2), ACT.Copy).then_inc(cqT_ready, 1)
                sc.wait_ge(da_kT, 2 * l + 2)
                sc.wait_ge(ml_proj, 3 * l + 1)
                for t in range(TOKS):
                    ins = sc.activation(q_ml[:, t, :, 0:NOPE],
                                        bank[2 + t][:, 0:ML_Q_COLS].rearrange("p (h c) -> p h c", c=ML_QK)[:, :, 0:NOPE], ACT.Copy)
                ins.then_inc(ml_nope, 1)
                for t in range(TOKS):
                    sc.wait_ge(ml_proj, 3 * l + 2 + t)
                    for i in range(2):
                        kv = bank[4 + 2 * t + i][:, 0:2 * KV_HEAD].rearrange("p (h c) -> p h c", c=KV_HEAD)
                        ins = sc.activation(k_ml[:, t, 2 * i:2 * i + 2, 0:NOPE], kv[:, :, 0:NOPE], ACT.Copy)
                    ins.then_inc(ml_nope, 1)
                for g in range(2):
                    sc.wait_ge(ml_turned, 4 * l + g + 1)
                    sc.activation(qT_ml[0:ML_QK, 2 * g:2 * g + 2, :], bank[g][0:ML_QK, :].rearrange("p (h t) -> p h t", h=2),
                                  ACT.Copy).then_inc(ml_qT, 1)
                base = JOBS * l
                for i in range(JOBS + 3):
                    if i < JOBS:
                        j = i
                        scale = (DA_DIM if j < DA_JOBS else ML_QK) ** -0.5
                        sc.wait_ge(max_ready, base + j + 1)
                        if j >= 2:
                            sc.wait_ge(probs_turned, base + j - 1)
                        for c in range(2):
                            ins = sc.activation(probs[j % 2][:, c, :], scores[j % 2][:, c, :], ACT.Exp,
                                                bias=neg_max[:, j, c:c + 1], scale=scale, accum_out=row_sum[:, j, c:c + 1])
                        ins.then_inc(probs_ready, 1)
                    if i == JOBS:
                        sc.wait_ge(o_ready, base + DA_JOBS)
                        for t in range(TOKS):
                            for hd in range(DA_HEADS):
                                chain(sc.activation(junk[:, 0:P], h[:, t, hd * P:(hd + 1) * P], ACT.Square, scale=DA_V ** -0.5,
                                                    accum_out=o_sq[:, t, hd:hd + 1]))
                        sc.activation(o_sd[:, :, :], o_sq[:, :, :], ACT.Sqrt, bias=eps_t[:, 1:2]).then_inc(o_sd_ready, 1)
                    j = i - 2
                    if 0 <= j < JOBS:
                        n = S if j < DA_JOBS else 2 * S
                        sc.wait_ge(probs_turned, base + j + 1)
                        if j >= 2:
                            sc.wait_ge(pv_ready, base + j - 1)
                        sc.activation(probsT[j % 2][:, 0:n], bank[4 + j % 2][:, 0:n], ACT.Copy).then_inc(probsT_ready, 1)
                turn(3 * l + 1)
                high(place, range(16 + AHEAD, 24))
                nxt = Place(place.unit + 24, place.tile + 6)
                high(nxt, range(AHEAD))
                norm(2 * l + 1)
                turn(3 * l + 2)

            def silu_of(step, fb_count, toks, cols):
                sc.wait_ge(unit_used, step.used(3))
                if not (isinstance(fb_count, int) and fb_count == 1):
                    sc.wait_ge(act_ready, fb_count - 1)
                for t in range(toks):
                    ins = sc.activation(silu[:, t, 0:cols], bank[t][:, 0:cols], ACT.Silu)
                ins.then_inc(silu_ready, 1)

            def act_hi(count, toks, banks, chunks):
                for t in range(toks):
                    sc.wait_ge(act_turned, count + t + 1)
                    sc.activation(aT_hi[:, 0:chunks, t * P:(t + 1) * P],
                                  bank[banks[t]][:, 0:chunks * P].rearrange("p (c t) -> p c t", c=chunks),
                                  ACT.Copy).then_inc(aT_hi_ready, 1)

            sc.dma_start(pos_i[:, :], positions.rearrange("o (t p) -> p (o t)", p=P), allow_slow_non_contiguous=True).then_inc(rope_in, 16)
            sc.dma_start(freq[:, :], freqs.to_broadcast([P, FREQS])).then_inc(rope_in, 16)
            for i, vec in enumerate((lq1, lk1, lq2, lk2)):
                sc.dma_start(lam_vecs[:, i, :, :], vec.unsqueeze(0).to_broadcast([P, DEPTH, DA_DIM])).then_inc(lam_in, 16)
            sc.wait_ge(angles, 1)
            sc.activation(sines[:, 0, :, :], angle[:, :, :], ACT.Sin)
            sc.activation(sines[:, 1, :, :], angle[:, :, :], ACT.Sin, scale=0.5).then_inc(sines_ready, 1)
            sc.wait_ge(dots, 1)
            sc.activation(lam_exps[:, :, :], lam_dots[:, :, :], ACT.Exp).then_inc(lam_exp, 1)
            high(Place(0, 0), range(AHEAD))
            attention(0)

            high(Place(DENSE_UNIT, DENSE_TILE), range(AHEAD, 8))
            silu_of(Place(DENSE_UNIT, DENSE_TILE), 1, TOKS, FB)
            with sc.Fori(0, DENSE_STEPS - 2) as i:
                step = Place(DENSE_UNIT + 8, DENSE_TILE + 2, fb=i)
                high(step, range(0, AHEAD))
                act_hi(i * TOKS, TOKS, (2, 3), FB // P)
                high(step, range(AHEAD, 9))
                silu_of(step, i + 2, TOKS, FB)
                high(step, range(9, 12))
            last = Place(DENSE_UNIT + 8 + STEP_UNITS * (DENSE_STEPS - 2), DENSE_TILE + 2 + STEP_TILES * (DENSE_STEPS - 2))
            high(last, range(0, AHEAD), DENSE_LAST)
            act_hi((DENSE_STEPS - 2) * TOKS, TOKS, (2, 3), FB // P)
            high(last, range(AHEAD, 8), DENSE_LAST)
            high(last, [8])
            silu_of(last, DENSE_STEPS, TOKS, DENSE_LAST)
            high(last, range(9, 12 + DENSE_LAST // P))
            act_hi((DENSE_STEPS - 1) * TOKS, TOKS, (2, 3), DENSE_LAST // P)
            high(Place(UNIT0[1], TILE0[1]), range(AHEAD))
            attention(1)

            sc.wait_ge(router_loaded, 16)
            sc.activation(r_hi[:, :, :], r_w[:, :, :], ACT.Copy).then_inc(r_split, 1)
            sc.wait_ge(routed_ps, 1)
            for t in range(TOKS):
                sc.activation(h_hi[:, t, :], h[:, t, :], ACT.Copy).then_inc(h_hi_ready, 1)
            sc.wait_ge(router_d, 1)
            sc.activation(rs["e"][:, :], rs["d"][:, :], ACT.Exp).then_inc(router_exp, 1)

            def experts(unit0, tile0, fb0, tok0, e0):
                def gather_hi(e):
                    for g in range(2):
                        sc.wait_ge(gathered, (e + e0) * 4 + g + 1)
                        sc.activation(g_hi[:, 4 * g:4 * g + 4, :], bank[3 + g][:, :].rearrange("p (c t) -> p c t", c=4),
                                      ACT.Copy).then_inc(g_hi_ready, 1)

                def y_out(nxt):
                    sc.wait_ge(unit_used, nxt.used(-1))
                    for half in range(2):
                        sc.activation(y_sb[:, half * 512:(half + 1) * 512], bank[5 + half][:, :], ACT.Copy).then_inc(y_ready, 1)

                def step0(e, place):
                    high(place, range(AHEAD, 8))
                    silu_of(place, e * STEPS + (fb0 + 1), 1, FB)
                    sc.wait_ge(give_turned, e + (e0 + 1))
                    sc.activation(giveT[:, :, :], bank[2][:, 0:S].rearrange("p (t s) -> p t s", t=TOKS),
                                  ACT.Copy).then_inc(giveT_ready, 1)

                def steps(e, reg):
                    step = Place(unit0 + 8, tile0 + 2, e=reg)
                    if reg is None:
                        step = step.plus(e * EXPERT_UNITS, e * EXPERT_TILES)
                    high(step, range(0, 9))
                    silu_of(step, e * STEPS + (fb0 + 2), 1, FB)
                    act_hi(e * STEPS + tok0, 1, (2,), FB // P)
                    high(step, range(9, 12))
                    with sc.Fori(0, STEPS - 2) as i:
                        step = Place(step.unit + STEP_UNITS, step.tile + STEP_TILES, e=reg, fb=i)
                        high(step, range(0, AHEAD))
                        act_hi(e * STEPS + i + (tok0 + 1), 1, (2,), FB // P)
                        high(step, range(AHEAD, 9))
                        silu_of(step, e * STEPS + i + (fb0 + 3), 1, FB)
                        high(step, range(9, 12))
                    tail = Place(step.unit + STEP_UNITS * (STEPS - 2), step.tile + STEP_TILES * (STEPS - 2), e=reg)
                    high(tail, range(4))
                    act_hi(e * STEPS + (tok0 + STEPS - 1), 1, (2,), FB // P)
                    return tail.plus(4, 1)

                first = Place(unit0, tile0)
                if e0:
                    high(first, range(AHEAD))
                gather_hi(0)
                step0(0, first)
                with sc.Fori(0, EXPERTS - 1) as e:
                    nxt = steps(e, e)
                    gather_hi(e + 1)
                    high(nxt, range(AHEAD))
                    y_out(nxt)
                    step0(e + 1, nxt)
                y_out(steps(EXPERTS - 1, None))

            experts(MOE_UNIT, MOE_TILE, DENSE_STEPS, DENSE_STEPS * TOKS, 0)
            sc.wait_ge(flag_ready, 1)
            some_over = sc.value_load(over_i[0:1, 0:1], min_val=0, max_val=1)
            with sc.If(some_over == 1):
                experts(MOE_UNIT + EXPERTS * EXPERT_UNITS, MOE_TILE + EXPERTS * EXPERT_TILES,
                        DENSE_STEPS + EXPERTS * STEPS, DENSE_STEPS * TOKS + EXPERTS * STEPS, EXPERTS)
            norm(4)

        @block.vector
        def _(ve):
            steps_done = [0]

            def chain(ins):
                steps_done[0] += 1
                ins.then_inc(vstep, 1)
                ve.wait_ge(vstep, steps_done[0])

            def low(place, units, cols=FB):
                for i in units:
                    ve.wait_ge(hi_ready, place.used(i))
                    src = raw[place.slot(i // TILE_UNITS)][:, i % TILE_UNITS * UNIT:(i % TILE_UNITS + 1) * UNIT]
                    hi, lo = w_hi[place.ring(i)][:, :].bitcast(F32), w_lo[place.ring(i)][:, :]
                    if cols < FB:
                        src, hi, lo = (a.rearrange("p (c n) -> p c n", c=2)[:, :, 0:cols] for a in (src, hi, lo))
                    ve.tensor_tensor(lo, src, hi, ALU.subtract).then_inc(lo_ready, 1)

            def norm(k):
                ve.wait_ge(sd_ready, k + 1)
                chain(ve.reciprocal(norm_r[:, :], norm_sd[:, :]))
                ve.wait_ge(gain_loaded[k % 2], 16 * (k // 2 + 1))
                for t in range(TOKS):
                    ins = ve.scalar_tensor_tensor(out=h[:, t, :], in0=x[:, t, :], scalar=norm_r[:, t:t + 1],
                                                  in1=gain[k % 2][:, :], op0=ALU.mult, op1=ALU.mult)
                    if k == 4:
                        ins.then_inc(h_ready, 1)
                if k < 4:
                    ins.then_inc(h_ready, 1)

            def turn(k):
                for g in range(4):
                    ve.wait_ge(tT_hi, 4 * k + g + 1)
                    t, c = g // 2, 4 * (g % 2)
                    at = (slice(None), slice(c, c + 4), slice(t * P, (t + 1) * P))
                    ve.tensor_tensor(hT_lo[at], bank[4 + g][:, :].rearrange("p (c t) -> p c t", c=4),
                                     hT_hi[at].bitcast(F32), ALU.subtract).then_inc(tT_lo, 1)

            def rotate(dst, src, t, heads, half, at):
                cos = cos_t[:, t, at:at + 2 * half].unsqueeze(1).to_broadcast([P, heads, 2 * half])
                sn = [sin_t[:, t, at + i * half:at + (i + 1) * half].unsqueeze(1).to_broadcast([P, heads, half])
                      for i in range(2)]
                n = heads * 2 * half
                a = probs_raw[0][:, 0:n].rearrange("p (h c) -> p h c", h=heads)
                b = probs_raw[1][:, 0:n].rearrange("p (h c) -> p h c", h=heads)
                ve.tensor_tensor(a, src, cos, ALU.mult)
                ve.tensor_tensor(b[:, :, 0:half], src[:, :, half:], sn[0], ALU.mult)
                chain(ve.tensor_tensor(b[:, :, half:], src[:, :, 0:half], sn[1], ALU.mult))
                return ve.tensor_tensor(dst, a, b, ALU.add)

            def attention(l):
                place = Place(UNIT0[l], TILE0[l])
                norm(2 * l)
                turn(3 * l)
                low(place, range(AHEAD, 9))
                for n, dst in enumerate((q_rot, k_rot)):
                    ve.wait_ge(unit_used, place.used(4 * n + 3))
                    for t in range(TOKS):
                        ins = rotate(dst[:, t, :].rearrange("p (h c) -> p h c", c=DA_DIM),
                               bank[2 * n + t][:, :].rearrange("p (h c) -> p h c", c=DA_DIM), t, 2 * DA_HEADS, HALF, 0)
                        if t < TOKS - 1:
                            chain(ins)
                    ins.then_inc(rotated, 1)
                    ve.wait_ge(rotated, 2 * l + n + 1)
                    if n == 0:
                        low(place, range(9, 12))
                        low(place, [12], IN_COLS - 3 * FB)
                low(place, range(13, 16), IN_COLS - 3 * FB)
                low(place, range(16, 16 + AHEAD))
                ve.wait_ge(v_copied, 2 * l + 2)
                for t in range(TOKS):
                    chain(rotate(k_pe[:, t, :].unsqueeze(1), rest[:, t, Q_RANK + KV_RANK:].unsqueeze(1), t, 1, ROPE // 2, DA_DIM))
                ve.wait_ge(small_loaded, 80 * (l + 1))
                chain(ve.tensor_scalar(sub_scaled[:, :], sub_gain[:, :], 1.0 - lambda_init(l), None, ALU.mult))
                ve.wait_ge(lat_sd_ready, l + 1)
                chain(ve.reciprocal(lat_r[:, :, :], lat_sd[:, :, :]))
                for t in range(TOKS):
                    for i, (a, n) in enumerate(((0, Q_RANK), (Q_RANK, KV_RANK))):
                        ins = ve.scalar_tensor_tensor(out=latent[:, t, a:a + n], in0=rest[:, t, a:a + n],
                                                      scalar=lat_r[:, t, i:i + 1], in1=latent_gain[:, a:a + n],
                                                      op0=ALU.mult, op1=ALU.mult)
                ins.then_inc(lat_ready, 1)
                for g in range(2):
                    ve.wait_ge(da_turned, 4 * l + 3 + g)
                    ve.tensor_copy(kT_da[:, 2 * g:2 * g + 2, :],
                                   bank[6 + g][:, :].rearrange("p (h t) -> p h t", h=2)).then_inc(da_kT, 1)
                ve.wait_ge(lat_turned, 2 * l + 2)
                ve.tensor_copy(ckT[:, :], bank[1][:, 0:S]).then_inc(ckT_ready, 1)
                ve.wait_ge(ml_nope, 3 * l + 1)
                for t in range(TOKS):
                    ins = rotate(q_ml[:, t, :, NOPE:], bank[2 + t][:, 0:ML_Q_COLS].rearrange("p (h c) -> p h c", c=ML_QK)[:, :, NOPE:],
                                 t, ML_HEADS, ROPE // 2, DA_DIM)
                    if t < TOKS - 1:
                        chain(ins)
                ins.then_inc(ml_qk, 1)
                for t in range(TOKS):
                    ve.wait_ge(ml_nope, 3 * l + 2 + t)
                    for i in range(2):
                        kv = bank[4 + 2 * t + i][:, 0:2 * KV_HEAD].rearrange("p (h c) -> p h c", c=KV_HEAD)
                        ve.tensor_copy(v_ml[:, t, 2 * i * ML_V:2 * (i + 1) * ML_V].rearrange("p (h c) -> p h c", h=2),
                                       kv[:, :, NOPE:])
                    ins = ve.tensor_copy(k_ml[:, t, :, NOPE:], k_pe[:, t, :].unsqueeze(1).to_broadcast([P, ML_HEADS, ROPE]))
                ins.then_inc(ml_qk, 1)
                for g in range(2):
                    ve.wait_ge(ml_turned, 4 * l + 3 + g)
                    ve.tensor_copy(kT_ml[0:ML_QK, 2 * g:2 * g + 2, :],
                                   bank[2 + g][0:ML_QK, :].rearrange("p (h t) -> p h t", h=2)).then_inc(ml_kT, 1)
                base = JOBS * l
                for i in range(JOBS + 4):
                    j = i
                    if j < JOBS:
                        scale = (DA_DIM if j < DA_JOBS else ML_QK) ** -0.5
                        ve.wait_ge(scored, base + j + 1)
                        chain(ve.tensor_reduce(row_max[:, j, :], scores[j % 2], AX.X, ALU.max))
                        ve.tensor_scalar(neg_max[:, j, :], row_max[:, j, :], -scale, None, ALU.mult).then_inc(max_ready, 1)
                    j = i - 1
                    if 0 <= j < JOBS:
                        ve.wait_ge(probs_ready, base + j + 1)
                        ins = ve.reciprocal(row_inv[:, j, :], row_sum[:, j, :])
                        if j < DA_JOBS:
                            chain(ins)
                            chain(ve.scalar_tensor_tensor(out=mix_coef[:, j:j + 1], in0=row_inv[:, j, 1:2],
                                                          scalar=row_sum[:, j, 0:1], in1=neg_lam[:, l:l + 1],
                                                          op0=ALU.mult, op1=ALU.mult))
                            if j >= 2:
                                ve.wait_ge(probs_turned, base + j - 1)
                            ins = ve.scalar_tensor_tensor(out=mixed[j % 2][:, :], in0=probs[j % 2][:, 1, :],
                                                          scalar=mix_coef[:, j:j + 1], in1=probs[j % 2][:, 0, :],
                                                          op0=ALU.mult, op1=ALU.add)
                        ins.then_inc(mix_ready, 1)
                    j = i - 4
                    if 0 <= j < JOBS:
                        ve.wait_ge(pv_ready, base + j + 1)
                        if j < DA_JOBS:
                            t, hd = j % 2, j // 2
                            ins = ve.tensor_scalar(h[:, t, hd * P:(hd + 1) * P], bank[6 + j % 2][:, 0:P],
                                                   row_inv[:, j, 0:1], None, ALU.mult)
                        else:
                            t, pair = j % 2, (j - DA_JOBS) // 2
                            for c in range(2):
                                col = DA_HEADS * DA_V + (2 * pair + c) * P
                                ins = ve.tensor_scalar(h[:, t, col:col + P], bank[6 + j % 2][:, c * P:(c + 1) * P],
                                                       row_inv[:, j, c:c + 1], None, ALU.mult)
                        ins.then_inc(o_ready, 1)
                ve.wait_ge(o_sd_ready, l + 1)
                chain(ve.reciprocal(o_r[:, :, :], o_sd[:, :, :]))
                for t in range(TOKS):
                    for hd in range(DA_HEADS):
                        o = h[:, t, hd * P:(hd + 1) * P]
                        ins = ve.scalar_tensor_tensor(out=o, in0=o, scalar=o_r[:, t, hd:hd + 1], in1=sub_scaled[:, :],
                                                      op0=ALU.mult, op1=ALU.mult)
                ins.then_inc(h_ready, 1)
                turn(3 * l + 1)
                low(place, range(16 + AHEAD, 24))
                nxt = Place(place.unit + 24, place.tile + 6)
                low(nxt, [0])
                for n in range(2):
                    ve.wait_ge(unit_used, place.used(19 + 4 * n))
                    for t in range(TOKS):
                        xs = x[:, t, n * 512:(n + 1) * 512]
                        ins = ve.tensor_tensor(xs, xs, bank[2 * n + t][:, :], ALU.add)
                    ins.then_inc(x_added, 1)
                    if n == 0:
                        low(nxt, range(1, AHEAD))
                norm(2 * l + 1)
                turn(3 * l + 2)

            def multiply(up_used, fb_count, toks, up_banks, cols):
                ve.wait_ge(silu_ready, fb_count)
                ve.wait_ge(unit_used, up_used)
                for t in range(toks):
                    ins = ve.tensor_tensor(act[:, t, 0:cols], silu[:, t, 0:cols], bank[up_banks[t]][:, 0:cols], ALU.mult)
                ins.then_inc(act_ready, 1)

            def act_lo(count, toks, banks, chunks):
                for t in range(toks):
                    ve.wait_ge(aT_hi_ready, count + t + 1)
                    at = (slice(None), slice(0, chunks), slice(t * P, (t + 1) * P))
                    ve.tensor_tensor(aT_lo[at], bank[banks[t]][:, 0:chunks * P].rearrange("p (c t) -> p c t", c=chunks),
                                     aT_hi[at].bitcast(F32), ALU.subtract).then_inc(aT_lo_ready, 1)

            ve.wait_ge(rope_in, 32)
            chain(ve.tensor_copy(pos_f[:, :], pos_i[:, :]))
            for t in range(TOKS):
                ins = ve.tensor_scalar(angle[:, t, :], freq[:, :], pos_f[:, t:t + 1], None, ALU.mult)
            chain(ins)
            chain(ve.tensor_scalar(turns_i[:, :, :], angle[:, :, :], 1 / TWO_PI, None, ALU.mult))
            chain(ve.tensor_copy(turns_f[:, :, :], turns_i[:, :, :]))
            for c in (_C1, _C2, _C3):
                chain(ve.scalar_tensor_tensor(out=angle[:, :, :], in0=turns_f[:, :, :], scalar=-c, in1=angle[:, :, :],
                                              op0=ALU.mult, op1=ALU.add))
            ve.tensor_scalar(angle[:, :, :], angle[:, :, :], PI_DOWN, -PI_DOWN, ALU.min, ALU.max).then_inc(angles, 1)
            ve.wait_ge(lam_in, 64)
            for i in range(2):
                ins = ve.tensor_tensor(lam_prod[:, i, :, :], lam_vecs[:, 2 * i, :, :], lam_vecs[:, 2 * i + 1, :, :], ALU.mult)
            chain(ins)
            ve.tensor_reduce(lam_dots[:, :, :], lam_prod[:, :, :, :], AX.X, ALU.add).then_inc(dots, 1)
            ve.wait_ge(sines_ready, 1)
            for t in range(TOKS):
                for a, f, n in ((0, 0, HALF), (DA_DIM, HALF, ROPE // 2)):
                    s, s_half = sines[:, 0, t, f:f + n], sines[:, 1, t, f:f + n]
                    ve.tensor_scalar(sin_t[:, t, a:a + n], s, -1.0, None, ALU.mult)
                    ve.tensor_copy(sin_t[:, t, a + n:a + 2 * n], s)
                    for i in range(2):
                        ins = ve.tensor_tensor(cos_t[:, t, a + i * n:a + (i + 1) * n], s_half, s_half, ALU.mult)
            chain(ins)
            chain(ve.tensor_scalar(cos_t[:, :, :], cos_t[:, :, :], -2.0, 1.0, ALU.mult, ALU.add))
            ve.wait_ge(lam_exp, 1)
            chain(ve.tensor_tensor(neg_lam[:, :], lam_exps[:, 1, :], lam_exps[:, 0, :], ALU.subtract))
            for l in range(DEPTH):
                ins = ve.tensor_scalar(neg_lam[:, l:l + 1], neg_lam[:, l:l + 1], -lambda_init(l), None, ALU.add)
            chain(ins)
            low(Place(0, 0), range(AHEAD))
            attention(0)

            low(Place(DENSE_UNIT, DENSE_TILE), range(AHEAD, 8))
            multiply(Place(DENSE_UNIT, DENSE_TILE).used(7), 1, TOKS, (2, 3), FB)
            with ve.Fori(0, DENSE_STEPS - 2) as i:
                step = Place(DENSE_UNIT + 8, DENSE_TILE + 2, fb=i)
                low(step, range(0, AHEAD))
                act_lo(i * TOKS, TOKS, (2, 3), FB // P)
                low(step, range(AHEAD, 12))
                multiply(step.used(7), i + 2, TOKS, (2, 3), FB)
            last = Place(DENSE_UNIT + 8 + STEP_UNITS * (DENSE_STEPS - 2), DENSE_TILE + 2 + STEP_TILES * (DENSE_STEPS - 2))
            low(last, range(0, AHEAD), DENSE_LAST)
            act_lo((DENSE_STEPS - 2) * TOKS, TOKS, (2, 3), FB // P)
            low(last, range(AHEAD, 8), DENSE_LAST)
            low(last, range(8, 12))
            multiply(last.used(7), DENSE_STEPS, TOKS, (2, 3), DENSE_LAST)
            low(last, range(12, 12 + DENSE_LAST // P))
            act_lo((DENSE_STEPS - 1) * TOKS, TOKS, (2, 3), DENSE_LAST // P)
            low(Place(UNIT0[1], TILE0[1]), range(AHEAD))
            ve.wait_ge(unit_used, Place(UNIT0[1], TILE0[1]).used(-1))
            for t in range(TOKS):
                for half in range(2):
                    xs = x[:, t, half * 512:(half + 1) * 512]
                    ins = ve.tensor_tensor(xs, xs, bank[4 + 2 * t + half][:, :], ALU.add)
            ins.then_inc(x_added, 1)
            attention(1)

            ve.wait_ge(r_split, 1)
            ve.tensor_tensor(r_lo[:, :, :], r_w[:, :, :], r_hi[:, :, :].bitcast(F32), ALU.subtract).then_inc(r_split, 1)
            ve.wait_ge(routed_ps, 1)
            shape = [P, TOKS, EXPERTS]

            def wide(a):
                return a[:, :].unsqueeze(2).to_broadcast(shape)

            chain(ve.tensor_copy(rt["logits"][:, :, :], bank[0][:, 0:TOKS * EXPERTS].rearrange("p (t e) -> p t e", t=TOKS)))
            ve.wait_ge(consts, CONSTS)

            def best(logits, m, eq, cand, i, onehot):
                chain(ve.tensor_reduce(rs[m][:, :], rt[logits][:, :, :], AX.X, ALU.max))
                chain(ve.tensor_tensor(rt[eq][:, :, :], rt[logits][:, :, :], wide(rs[m]), ALU.is_equal))
                chain(ve.tensor_tensor(rt[cand][:, :, :], rt[eq][:, :, :], expert_no[:, :, :], ALU.mult))
                chain(ve.tensor_reduce(rs[i][:, :], rt[cand][:, :, :], AX.X, ALU.min))
                chain(ve.tensor_tensor(rt[onehot][:, :, :], expert_no[:, :, :], wide(rs[i]), ALU.is_equal))

            best("logits", "m1", "eq", "cand", "i1", "first")
            chain(ve.scalar_tensor_tensor(out=rt["logits2"][:, :, :], in0=rt["first"][:, :, :], scalar=-3e38,
                                          in1=rt["logits"][:, :, :], op0=ALU.mult, op1=ALU.add))
            best("logits2", "m2", "eq2", "cand2", "i2", "second")
            ve.tensor_tensor(rs["d"][:, :], rs["m2"][:, :], rs["m1"][:, :], ALU.subtract).then_inc(router_d, 1)
            ve.tensor_tensor(mask[:, :, 0:EXPERTS], rt["first"][:, :, :], rt["second"][:, :, :], ALU.add).then_inc(mask_ready, 1)
            ve.wait_ge(router_exp, 1)
            chain(ve.tensor_scalar(rs["e1"][:, :], rs["e"][:, :], 1.0, None, ALU.add))
            chain(ve.reciprocal(rs["g1"][:, :], rs["e1"][:, :]))
            chain(ve.tensor_tensor(rs["g2"][:, :], rs["g1"][:, :], rs["e"][:, :], ALU.mult))
            ve.tensor_tensor(rt["w1"][:, :, :], rt["first"][:, :, :], wide(rs["g1"]), ALU.mult)
            chain(ve.tensor_tensor(rt["w2"][:, :, :], rt["second"][:, :, :], wide(rs["g2"]), ALU.mult))
            chain(ve.tensor_tensor(share[:, :, 0:EXPERTS], rt["w1"][:, :, :], rt["w2"][:, :, :], ALU.add))
            for t in range(TOKS):
                ve.wait_ge(h_hi_ready, t + 1)
                ve.tensor_tensor(h_lo[:, t, :], h[:, t, :], h_hi[:, t, :].bitcast(F32), ALU.subtract).then_inc(h_split, 1)
            ve.wait_ge(ranked_ps, 1)
            ranks = bank[1][:, 0:TOKS * EXPERTS].rearrange("p (t e) -> p t e", t=TOKS)
            chain(ve.tensor_copy(rank[0][:, :, 0:EXPERTS], ranks))
            ve.tensor_scalar(rank[1][:, :, 0:EXPERTS], ranks, -float(P), None, ALU.add)
            chain(ve.tensor_reduce(most[:, :], bank[1][:, TOKS * EXPERTS:(TOKS + 1) * EXPERTS], AX.X, ALU.max))
            chain(ve.tensor_scalar(over[:, :], most[:, :], float(P), None, ALU.is_gt))
            ve.tensor_copy(over_i[:, :], over[:, :]).then_inc(flag_ready, 1)

            def experts(unit0, tile0, fb0, tok0, e0, ranks):
                def col(table, t, e):
                    return table[:, t, bass.ds(e, 1)] if not isinstance(e, int) else table[:, t, e:e + 1]

                def choose(e):
                    for t in range(TOKS):
                        ins = ve.tensor_scalar(pick[:, t, :], slot_no[:, :], col(ranks, t, e), col(mask, t, e),
                                               ALU.is_equal, ALU.mult)
                    ins.then_inc(pick_ready, 1)

                def gather_lo(e):
                    for g in range(2):
                        ve.wait_ge(gathered, (e + e0) * 4 + g + 3)
                        ve.tensor_copy(g_lo[:, 4 * g:4 * g + 4, :],
                                       bank[3 + g][:, :].rearrange("p (c t) -> p c t", c=4)).then_inc(g_lo_ready, 1)

                def add_out(e):
                    for g in range(4):
                        ve.wait_ge(scattered, (e + e0) * 4 + g + 1)
                        t, half = g % 2, g // 2
                        xs = x[:, t, half * 512:(half + 1) * 512]
                        ve.tensor_tensor(xs, xs, bank[(7, 2, 1, 7)[g]][:, :], ALU.add).then_inc(scatter_added, 1)

                def step0(e, place, add):
                    gather_lo(e)
                    for t in range(TOKS):
                        ins = ve.tensor_scalar(give[:, t, :], slot_no[:, :], col(ranks, t, e), col(share, t, e),
                                               ALU.is_equal, ALU.mult)
                    ins.then_inc(give_ready, 1)
                    choose(e + 1)
                    low(place, [AHEAD])
                    if add:
                        add_out(e - 1)
                    low(place, range(AHEAD + 1, 8))

                def steps(e, reg):
                    step = Place(unit0 + 8, tile0 + 2, e=reg)
                    if reg is None:
                        step = step.plus(e * EXPERT_UNITS, e * EXPERT_TILES)
                    low(step, range(0, AHEAD))
                    multiply(step.used(-1), e * STEPS + (fb0 + 1), 1, (1,), FB)
                    low(step, range(AHEAD, 9))
                    act_lo(e * STEPS + tok0, 1, (2,), FB // P)
                    low(step, range(9, 12))
                    multiply(step.used(7), e * STEPS + (fb0 + 2), 1, (1,), FB)
                    with ve.Fori(0, STEPS - 2) as i:
                        step = Place(step.unit + STEP_UNITS, step.tile + STEP_TILES, e=reg, fb=i)
                        low(step, range(0, AHEAD))
                        act_lo(e * STEPS + i + (tok0 + 1), 1, (2,), FB // P)
                        low(step, range(AHEAD, 12))
                        multiply(step.used(7), e * STEPS + i + (fb0 + 3), 1, (1,), FB)
                    tail = Place(step.unit + STEP_UNITS * (STEPS - 2), step.tile + STEP_TILES * (STEPS - 2), e=reg)
                    low(tail, range(4))
                    act_lo(e * STEPS + (tok0 + STEPS - 1), 1, (2,), FB // P)
                    return tail.plus(4, 1)

                first = Place(unit0, tile0)
                choose(0)
                if e0:
                    low(first, range(AHEAD))
                step0(0, first, False)
                with ve.Fori(0, EXPERTS - 1) as e:
                    nxt = steps(e, e)
                    low(nxt, range(AHEAD))
                    step0(e + 1, nxt, True)
                steps(EXPERTS - 1, None)
                add_out(EXPERTS - 1)
                ve.wait_ge(scatter_added, (e0 + EXPERTS) * 4)

            experts(MOE_UNIT, MOE_TILE, DENSE_STEPS, DENSE_STEPS * TOKS, 0, rank[0])
            ve.wait_ge(flag_ready, 1)
            some_over = ve.value_load(over_i[0:1, 0:1], min_val=0, max_val=1)
            with ve.If(some_over == 1):
                experts(MOE_UNIT + EXPERTS * EXPERT_UNITS, MOE_TILE + EXPERTS * EXPERT_TILES,
                        DENSE_STEPS + EXPERTS * STEPS, DENSE_STEPS * TOKS + EXPERTS * STEPS, EXPERTS, rank[1])
            ve.sem_inc(x_added, 1)
            norm(4)

        @block.tensor
        def _(pe):
            def product(out_ap, a_hi, a_lo, b_hi, b_lo, first, last):
                pe.matmul(out_ap, a_hi, b_hi, start=first, stop=False)
                pe.matmul(out_ap, a_hi, b_lo, start=False, stop=False)
                return pe.matmul(out_ap, a_lo, b_hi, start=False, stop=last)

            def columns(place, i0, a_hi, a_lo, toks, banks, cols):
                for u in range(TILE_UNITS):
                    pe.wait_ge(lo_ready, place.used(i0 + u))
                    r = place.ring(i0 + u)
                    for c in range(2):
                        k = 2 * u + c
                        for t in range(toks):
                            tk = slice(t * P, (t + 1) * P)
                            w = slice(c * 512, c * 512 + cols)
                            ins = product(bank[banks[t]][:, 0:cols], a_hi[:, k, tk], a_lo[:, k, tk],
                                          w_hi[r][:, w], w_lo[r][:, w], k == 0, k == KC - 1)
                    ins.then_inc(unit_used, 1)

            def down(place, i0, toks, banks, chunks, first, last):
                for c in range(chunks):
                    pe.wait_ge(lo_ready, place.used(i0 + c))
                    r = place.ring(i0 + c)
                    for t in range(toks):
                        tk = slice(t * P, (t + 1) * P)
                        for half in range(2):
                            w = slice(half * 512, (half + 1) * 512)
                            ins = product(bank[banks[2 * t + half]][:, :], aT_hi[:, c, tk], aT_lo[:, c, tk],
                                          w_hi[r][:, w], w_lo[r][:, w], first and c == 0, last and c == chunks - 1)
                    ins.then_inc(unit_used, 1)

            def turn(k):
                pe.wait_ge(h_ready, k + 1)
                for g in range(4):
                    t, c0 = g // 2, 4 * (g % 2)
                    for c in range(4):
                        ins = pe.transpose(bank[4 + g][:, c * P:(c + 1) * P], h[:, t, (c0 + c) * P:(c0 + c + 1) * P], ident[:, :])
                    ins.then_inc(turned, 1)
                pe.wait_ge(tT_lo, 4 * k + 4)

            def attention(l):
                place = Place(UNIT0[l], TILE0[l])
                turn(3 * l)
                for n in range(4):
                    if n == 2:
                        pe.wait_ge(rotated, 2 * l + 1)
                    if n == 3:
                        pe.wait_ge(rotated, 2 * l + 2)
                    cols = min(FB, IN_COLS - n * FB)
                    columns(place, 4 * n, hT_hi, hT_lo, TOKS, (2 * (n % 2), 2 * (n % 2) + 1), cols)
                for g in range(4):
                    src = (q_rot, k_rot)[g // 2]
                    for hh in range(2):
                        hd = 2 * (g % 2) + hh
                        for t in range(TOKS):
                            ins = pe.transpose(bank[4 + g][:, hh * S + t * P:hh * S + (t + 1) * P],
                                               src[:, t, hd * P:(hd + 1) * P], ident[:, :])
                    ins.then_inc(da_turned, 1)
                pe.wait_ge(lat_ready, l + 1)
                pe.wait_ge(v_copied, 2 * l + 2)
                for c in range(2):
                    for t in range(TOKS):
                        ins = pe.transpose(bank[0][:, c * S + t * P:c * S + (t + 1) * P], latent[:, t, c * P:(c + 1) * P], ident[:, :])
                ins.then_inc(lat_turned, 1)
                for t in range(TOKS):
                    ins = pe.transpose(bank[1][:, t * P:(t + 1) * P], latent[:, t, Q_RANK:], ident[:, :])
                ins.then_inc(lat_turned, 1)
                pe.wait_ge(small_loaded, 80 * (l + 1))
                pe.wait_ge(cqT_ready, l + 1)
                for t in range(TOKS):
                    for c in range(2):
                        ins = pe.matmul(bank[2 + t][:, 0:ML_Q_COLS], cqT[:, c, t * P:(t + 1) * P], w_uq[:, c, :],
                                        start=(c == 0), stop=(c == 1))
                ins.then_inc(ml_proj, 1)
                pe.wait_ge(ckT_ready, l + 1)
                pe.wait_ge(da_qT, 2 * l + 2)
                pe.wait_ge(da_kT, 2 * l + 2)
                for t in range(TOKS):
                    for i in range(2):
                        ins = pe.matmul(bank[4 + 2 * t + i][:, 0:2 * KV_HEAD], ckT[:, t * P:(t + 1) * P],
                                        w_ukv[:, 2 * i * KV_HEAD:2 * (i + 1) * KV_HEAD], start=True, stop=True)
                    ins.then_inc(ml_proj, 1)
                for kind, src in enumerate((q_ml, k_ml)):
                    pe.wait_ge(ml_qk, 2 * l + kind + 1)
                    for g in range(2):
                        for hh in range(2):
                            for t in range(TOKS):
                                ins = pe.transpose(bank[2 * kind + g][0:ML_QK, hh * S + t * P:hh * S + (t + 1) * P],
                                                   src[:, t, 2 * g + hh, :], ident[:, :])
                        ins.then_inc(ml_turned, 1)
                base = JOBS * l
                pe.wait_ge(ml_qT, 2 * l + 2)
                pe.wait_ge(ml_kT, 2 * l + 2)
                for i in range(JOBS + 3):
                    j = i
                    if j < JOBS:
                        if j >= 2:
                            pe.wait_ge(probs_ready, base + j - 1)
                        t = j % 2
                        for c in range(2):
                            if j < DA_JOBS:
                                part = slice(c * DA_DIM, (c + 1) * DA_DIM)
                                q, k = qT_da[part, j // 2, t * P:(t + 1) * P], kT_da[part, j // 2, :]
                            else:
                                hd = 2 * ((j - DA_JOBS) // 2) + c
                                q, k = qT_ml[0:ML_QK, hd, t * P:(t + 1) * P], kT_ml[0:ML_QK, hd, :]
                            ins = pe.matmul(scores[j % 2][:, c, :], q, k, start=True, stop=True)
                        ins.then_inc(scored, 1)
                    j = i - 2
                    if 0 <= j < JOBS:
                        pe.wait_ge(mix_ready, base + j + 1)
                        if j >= 2:
                            pe.wait_ge(probsT_ready, base + j - 1)
                        for c in range(1 if j < DA_JOBS else 2):
                            for kc in range(TOKS):
                                src = mixed[j % 2][:, kc * P:(kc + 1) * P] if j < DA_JOBS else probs[j % 2][:, c, kc * P:(kc + 1) * P]
                                ins = pe.transpose(bank[4 + j % 2][:, c * S + kc * P:c * S + (kc + 1) * P], src, ident[:, :])
                        ins.then_inc(probs_turned, 1)
                    j = i - 3
                    if 0 <= j < JOBS:
                        pe.wait_ge(probsT_ready, base + j + 1)
                        if j >= 2:
                            pe.wait_ge(o_ready, base + j - 1)
                        for c in range(1 if j < DA_JOBS else 2):
                            for kc in range(TOKS):
                                if j < DA_JOBS:
                                    v = v_da[:, kc, (j // 2) * DA_V:(j // 2 + 1) * DA_V]
                                else:
                                    hd = 2 * ((j - DA_JOBS) // 2) + c
                                    v = v_ml[:, kc, hd * ML_V:(hd + 1) * ML_V]
                                ins = pe.matmul(bank[6 + j % 2][:, c * P:(c + 1) * P], probsT[j % 2][:, c * S + kc * P:c * S + (kc + 1) * P],
                                                v, start=(kc == 0), stop=(kc == 1))
                        ins.then_inc(pv_ready, 1)
                turn(3 * l + 1)
                for n in range(2):
                    columns(place, 16 + 4 * n, hT_hi, hT_lo, TOKS, (2 * n, 2 * n + 1), FB)
                turn(3 * l + 2)

            def turn_act(count, toks, banks, chunks):
                pe.wait_ge(act_ready, count)
                for t in range(toks):
                    a = act[:, t, 0:chunks * P].rearrange("p (m c) -> p c m", c=chunks)
                    for c in range(chunks):
                        ins = pe.transpose(bank[banks[t]][:, c * P:(c + 1) * P], a[:, c, :], ident[:, :])
                    ins.then_inc(act_turned, 1)

            pe.wait_ge(consts, CONSTS)
            attention(0)

            Y = (4, 5, 6, 7)

            def dense_step(place, count, cols, first):
                if not (isinstance(count, int) and count == 1):
                    pe.wait_ge(silu_ready, count - 1)
                columns(place, 0, hT_hi, hT_lo, TOKS, (0, 1), cols)
                if not (isinstance(count, int) and count == 1):
                    pe.wait_ge(aT_lo_ready, (count - 1) * TOKS)
                columns(place, 4, hT_hi, hT_lo, TOKS, (2, 3), cols)
                if first is not None:
                    down(place, 8, TOKS, Y, FB // P, first, False)
                turn_act(count, TOKS, (2, 3), cols // P)

            dense_step(Place(DENSE_UNIT, DENSE_TILE), 1, FB, None)
            dense_step(Place(DENSE_UNIT + 8, DENSE_TILE + 2), 2, FB, True)
            with pe.Fori(0, DENSE_STEPS - 3) as i:
                dense_step(Place(DENSE_UNIT + 8 + STEP_UNITS, DENSE_TILE + 2 + STEP_TILES, fb=i), i + 3, FB, False)
            last = Place(DENSE_UNIT + 8 + STEP_UNITS * (DENSE_STEPS - 2), DENSE_TILE + 2 + STEP_TILES * (DENSE_STEPS - 2))
            dense_step(last, DENSE_STEPS, DENSE_LAST, False)
            pe.wait_ge(aT_lo_ready, DENSE_STEPS * TOKS)
            down(last, 12, TOKS, Y, DENSE_LAST // P, False, True)
            attention(1)

            pe.wait_ge(r_split, 2)
            for t in range(TOKS):
                for k in range(KC):
                    tk = slice(t * P, (t + 1) * P)
                    ins = product(bank[0][:, t * EXPERTS:(t + 1) * EXPERTS], hT_hi[:, k, tk], hT_lo[:, k, tk],
                                  r_hi[:, k, :], r_lo[:, k, :], k == 0, k == KC - 1)
            ins.then_inc(routed_ps, 1)
            pe.wait_ge(mask_ready, 1)
            E = EXPERTS
            m = [mask[:, t, 0:E] for t in range(TOKS)]
            pe.matmul(bank[1][:, 0:E], before[:, :], m[0], start=True, stop=True)
            pe.matmul(bank[1][:, E:2 * E], ones[:, :], m[0], start=True, stop=False)
            pe.matmul(bank[1][:, E:2 * E], before[:, :], m[1], start=False, stop=True)
            pe.matmul(bank[1][:, 2 * E:3 * E], ones[:, :], m[0], start=True, stop=False)
            pe.matmul(bank[1][:, 2 * E:3 * E], ones[:, :], m[1], start=False, stop=True).then_inc(ranked_ps, 1)
            pe.wait_ge(flag_ready, 1)
            pe.wait_ge(h_split, TOKS)

            def experts(unit0, tile0, fb0, tok0, e0):
                def gather(e, lo):
                    src = h_lo if lo else h_hi
                    for g in range(2):
                        if lo:
                            pe.wait_ge(g_hi_ready, (e + e0) * 2 + g + 1)
                        for c in range(4):
                            k = 4 * g + c
                            for t in range(TOKS):
                                ins = pe.matmul(bank[3 + g][:, c * P:(c + 1) * P], src[:, t, k * P:(k + 1) * P], pick[:, t, :],
                                                start=(t == 0), stop=(t == TOKS - 1))
                        ins.then_inc(gathered, 1)

                def step0(e, place, after):
                    pe.wait_ge(g_lo_ready, (e + e0) * 2 + 2)
                    columns(place, 0, g_hi, g_lo, 1, (0,), FB)
                    pe.wait_ge(give_ready, e + (e0 + 1))
                    if after:
                        pe.wait_ge(scatter_added, (e + e0) * 4)
                    for t in range(TOKS):
                        ins = pe.transpose(bank[2][:, t * P:(t + 1) * P], give[:, t, :], ident[:, :])
                    ins.then_inc(give_turned, 1)
                    columns(place, 4, g_hi, g_lo, 1, (1,), FB)

                def steps(e, reg):
                    step = Place(unit0 + 8, tile0 + 2, e=reg)
                    if reg is None:
                        step = step.plus(e * EXPERT_UNITS, e * EXPERT_TILES)
                    pe.wait_ge(silu_ready, e * STEPS + (fb0 + 1))
                    columns(step, 0, g_hi, g_lo, 1, (0,), FB)
                    pe.wait_ge(giveT_ready, e + (e0 + 1))
                    turn_act(e * STEPS + (fb0 + 1), 1, (2,), FB // P)
                    columns(step, 4, g_hi, g_lo, 1, (1,), FB)
                    pe.wait_ge(aT_lo_ready, e * STEPS + (tok0 + 1))
                    down(step, 8, 1, (5, 6), FB // P, True, False)
                    turn_act(e * STEPS + (fb0 + 2), 1, (2,), FB // P)
                    with pe.Fori(0, STEPS - 2) as i:
                        step = Place(step.unit + STEP_UNITS, step.tile + STEP_TILES, e=reg, fb=i)
                        pe.wait_ge(silu_ready, e * STEPS + i + (fb0 + 2))
                        columns(step, 0, g_hi, g_lo, 1, (0,), FB)
                        columns(step, 4, g_hi, g_lo, 1, (1,), FB)
                        pe.wait_ge(aT_lo_ready, e * STEPS + i + (tok0 + 2))
                        down(step, 8, 1, (5, 6), FB // P, False, False)
                        turn_act(e * STEPS + i + (fb0 + 3), 1, (2,), FB // P)
                    return Place(step.unit + STEP_UNITS * (STEPS - 2), step.tile + STEP_TILES * (STEPS - 2), e=reg)

                def finish(e, place):
                    pe.wait_ge(aT_lo_ready, e * STEPS + (tok0 + STEPS))
                    down(place, 0, 1, (5, 6), FB // P, False, True)

                def scatter(e):
                    for g in range(4):
                        t, half = g % 2, g // 2
                        pe.wait_ge(y_ready, (e + e0) * 2 + half + 1)
                        if g == 3:
                            pe.wait_ge(scatter_added, (e + e0) * 4 + 1)
                        pe.matmul(bank[(7, 2, 1, 7)[g]][:, :], giveT[:, t, :], y_sb[:, half * 512:(half + 1) * 512],
                                  start=True, stop=True).then_inc(scattered, 1)

                pe.wait_ge(pick_ready, e0 + (e0 // EXPERTS) + 1)
                gather(0, False)
                gather(0, True)
                step0(0, Place(unit0, tile0), e0 > 0)
                with pe.Fori(0, EXPERTS - 1) as e:
                    tail = steps(e, e)
                    pe.wait_ge(pick_ready, e + (e0 + e0 // EXPERTS + 2))
                    gather(e + 1, False)
                    finish(e, tail)
                    gather(e + 1, True)
                    scatter(e)
                    step0(e + 1, tail.plus(4, 1), True)
                tail = steps(EXPERTS - 1, None)
                finish(EXPERTS - 1, tail)
                scatter(EXPERTS - 1)

            experts(MOE_UNIT, MOE_TILE, DENSE_STEPS, DENSE_STEPS * TOKS, 0)
            some_over = pe.value_load(over_i[0:1, 0:1], min_val=0, max_val=1)
            with pe.If(some_over == 1):
                experts(MOE_UNIT + EXPERTS * EXPERT_UNITS, MOE_TILE + EXPERTS * EXPERT_TILES,
                        DENSE_STEPS + EXPERTS * STEPS, DENSE_STEPS * TOKS + EXPERTS * STEPS, EXPERTS)


_INS = ["x", "positions", "w_in", "w_out", "norm_mix", "norm_ffn", "da_lambda_q1", "da_lambda_k1", "da_lambda_q2",
        "da_lambda_k2", "da_subln", "mla_q_norm", "mla_w_uq", "mla_kv_norm", "mla_w_ukv", "ffn_w_gate", "ffn_w_up",
        "ffn_w_down", "moe_router", "moe_w_gate", "moe_w_up", "moe_w_down", "norm_final"]


def kernel(**inputs):
    import concourse.bacc as _bacc
    from concourse.bass_utils import run_bass_kernel_spmd as _run

    nc = _bacc.Bacc("TRN2", target_bir_lowering=False, num_devices=1, dynamic_dma_scratch_size=1024)
    arrays, args = {}, []
    for name in _INS + ["rope_freqs"]:
        a = rope_freqs() if name == "rope_freqs" else np.ascontiguousarray(inputs[name])
        arrays[f"in_{name}"] = a
        args.append(nc.dram_tensor(f"in_{name}", a.shape, mybir.dt.from_np(a.dtype), kind="ExternalInput").ap())
    out = nc.dram_tensor("out_x", (1, S, D), mybir.dt.float32, kind="ExternalOutput").ap()
    encoder(nc, *args, out)
    r = _run(nc, [arrays], core_ids=[0])
    return r.results[0]["out_x"]
```

```python
from contextlib import ExitStack

import numpy as np

import concourse.bass as bass
from concourse import mybir

P = 128
D = 1024
S = 256
TOKS = S // P
KC = D // P
DEPTH = 2
NORM_EPS, SUBLN_EPS = 1e-6, 1e-5

DA_HEADS, DA_DIM, DA_V = 4, 64, 128
DA_COLS = DA_HEADS * 2 * DA_DIM
HALF = DA_DIM // 2
ML_HEADS, NOPE, ROPE, ML_V = 4, 64, 32, 128
ML_QK = NOPE + ROPE
Q_RANK, KV_RANK = 256, 128
ML_Q_COLS = ML_HEADS * ML_QK
KV_HEAD = NOPE + ML_V
KV_COLS = ML_HEADS * KV_HEAD
REST = Q_RANK + KV_RANK + ROPE
IN_COLS = 3 * DA_COLS + REST
FREQS = HALF + ROPE // 2

FF_DENSE, FF_EXPERT = 2816, 3584
EXPERTS = 8
FB = 512
DENSE_STEPS = -(-FF_DENSE // FB)
DENSE_LAST = FF_DENSE - (DENSE_STEPS - 1) * FB
STEPS = FF_EXPERT // FB

UNIT = 1024
TILE_UNITS = 4
SLOTS = 3
RING = 6
AHEAD = 5
LAYER_UNITS = (4 + 2) * TILE_UNITS
DENSE_UNITS = 2 * TILE_UNITS * DENSE_STEPS + TILE_UNITS * (DENSE_STEPS - 1) + DENSE_LAST // P
DENSE_TILES = 3 * DENSE_STEPS
STEP_UNITS, STEP_TILES = 3 * TILE_UNITS, 3
EXPERT_UNITS, EXPERT_TILES = STEPS * STEP_UNITS, STEPS * STEP_TILES
LAYER_TILES = 6
UNIT0 = (0, LAYER_UNITS + DENSE_UNITS)
TILE0 = (0, LAYER_TILES + DENSE_TILES)
MOE_UNIT, MOE_TILE = UNIT0[1] + LAYER_UNITS, TILE0[1] + LAYER_TILES
DENSE_UNIT, DENSE_TILE = LAYER_UNITS, LAYER_TILES
SHORT_TILE = DENSE_TILE + DENSE_TILES - 1
SHORT_BY = TILE_UNITS - DENSE_LAST // P
assert STEP_UNITS % RING == 0 and STEP_TILES % SLOTS == 0

JOBS = 12
DA_JOBS = DA_HEADS * TOKS

TWO_PI = 2 * np.pi
_C1 = float(np.float32(np.round(TWO_PI * 2**7) / 2**7))
_C2 = float(np.float32(np.round((TWO_PI - _C1) * 2**19) / 2**19))
_C3 = float(np.float32(TWO_PI - _C1 - _C2))
PI_DOWN = 3.1415925


NORM_PARTS, HEAD_PARTS = 4, 2
LAYER_PARTS = 2 * NORM_PARTS + HEAD_PARTS
IN_TILES = ((3 * DA_COLS, REST), (0, DA_COLS), (DA_COLS, DA_COLS), (2 * DA_COLS, DA_COLS))


def parts_before(norm):
    return norm // 2 * LAYER_PARTS + norm % 2 * (NORM_PARTS + HEAD_PARTS)


def lambda_init(layer):
    return 0.8 - 0.6 * float(np.exp(-0.3 * layer))


def rope_freqs():
    f = [1.0 / (np.float32(10000.0) ** (np.arange(0, d, 2, dtype=np.float32) / np.float32(d))) for d in (DA_DIM, ROPE)]
    return np.concatenate(f).astype(np.float32)[None, :]


class Place:

    def __init__(self, unit, tile, e=None, fb=None):
        self.unit, self.tile, self.e, self.fb = unit, tile, e, fb

    def plus(self, units, tiles):
        return Place(self.unit + units, self.tile + tiles, self.e, self.fb)

    def _dyn(self, n, per_expert, per_step):
        for reg, per in ((self.e, per_expert), (self.fb, per_step)):
            if reg is not None:
                n = reg * per + n
        return n

    def used(self, i):
        return self._dyn(self.unit + i + 1, EXPERT_UNITS, STEP_UNITS)

    def ring(self, i):
        return (self.unit + i) % RING

    def slot(self, j):
        return (self.tile + j) % SLOTS

    def loaded(self, j):
        return self._dyn(16 * ((self.tile + j) // SLOTS + 1), 16 * EXPERT_TILES // SLOTS, 16 * STEP_TILES // SLOTS)

    def freed(self, j):
        t = self.tile + j - SLOTS
        short = SHORT_BY if t >= SHORT_TILE else 0
        return self._dyn(TILE_UNITS * (t + 1) - short, EXPERT_UNITS, STEP_UNITS)


def encoder(nc, x_in, positions, w_in, w_out, norm_mix, norm_ffn, lq1, lk1, lq2, lk2, da_subln, mla_q_norm, mla_w_uq,
            mla_kv_norm, mla_w_ukv, ffn_gate, ffn_up, ffn_down, router, moe_gate, moe_up, moe_down, norm_final,
            freqs, out):
    F32, F32R, I32 = mybir.dt.float32, mybir.dt.float32r, mybir.dt.int32
    ALU, ACT, AX = mybir.AluOpType, mybir.ActivationFunctionType, mybir.AxisListType

    with ExitStack() as ctx:
        def sb(name, shape, dt=F32):
            return ctx.enter_context(nc.sbuf_tensor(name, shape, dt))

        def sem(name):
            return ctx.enter_context(nc.semaphore(name))

        raw = [sb(f"raw{i}", [P, TILE_UNITS * UNIT]) for i in range(SLOTS)]
        w_hi = [sb(f"w_hi{i}", [P, UNIT], F32R) for i in range(RING)]
        w_lo = [sb(f"w_lo{i}", [P, UNIT], F32R) for i in range(RING)]

        x = sb("x", [P, TOKS, D])
        h = sb("h", [P, TOKS, D])
        t_hi = sb("t_hi", [P, KC * S], F32R)
        t_lo = sb("t_lo", [P, KC * S], F32R)
        hT_hi = t_hi[:, :].rearrange("p (c t) -> p c t", c=KC)
        hT_lo = t_lo[:, :].rearrange("p (c t) -> p c t", c=KC)
        h_hi = t_hi[:, :].rearrange("p (t d) -> p t d", t=TOKS)
        h_lo = t_lo[:, :].rearrange("p (t d) -> p t d", t=TOKS)
        g_hi = sb("g_hi", [P, KC, P], F32R)
        g_lo = sb("g_lo", [P, KC, P], F32R)
        aT_hi = sb("aT_hi", [P, FB // P, S], F32R)
        aT_lo = sb("aT_lo", [P, FB // P, S], F32R)
        gain = [sb(f"gain{i}", [P, D]) for i in range(2)]

        ARENA = 13184
        arena = sb("arena", [P, ARENA])
        used_cols = [0]

        def cut(cols):
            a = used_cols[0]
            used_cols[0] = a + cols
            assert used_cols[0] <= ARENA
            return arena[:, a:a + cols]

        def view(ap, pattern, **sizes):
            return ap.rearrange(pattern, **sizes)

        q_rot = view(cut(TOKS * DA_COLS), "p (t c) -> p t c", t=TOKS)
        k_rot = view(cut(TOKS * DA_COLS), "p (t c) -> p t c", t=TOKS)
        v_da = view(cut(TOKS * DA_COLS), "p (t c) -> p t c", t=TOKS)
        rest_raw = cut(TOKS * REST)
        rest = view(rest_raw, "p (t c) -> p t c", t=TOKS)
        qT_da = view(cut(DA_HEADS * S), "p (h t) -> p h t", h=DA_HEADS)
        kT_da = view(cut(DA_HEADS * S), "p (h t) -> p h t", h=DA_HEADS)
        qT_ml = view(cut(ML_HEADS * S), "p (h t) -> p h t", h=ML_HEADS)
        kT_ml = view(cut(ML_HEADS * S), "p (h t) -> p h t", h=ML_HEADS)
        latent_raw = cut(TOKS * (Q_RANK + KV_RANK))
        latent = view(latent_raw, "p (t c) -> p t c", t=TOKS)
        v_ml = view(cut(TOKS * ML_HEADS * ML_V), "p (t c) -> p t c", t=TOKS)
        cqT = view(cut(2 * S), "p (c t) -> p c t", c=2)
        ckT = cut(S)
        probs_raw = [cut(2 * S) for _ in range(2)]
        probs = [view(a, "p (c k) -> p c k", c=2) for a in probs_raw]
        mixed = [cut(S) for _ in range(2)]
        probsT = [cut(2 * S) for _ in range(2)]
        k_pe = view(cut(TOKS * ROPE), "p (t c) -> p t c", t=TOKS)
        q_ml = view(rest_raw[:, 0:TOKS * ML_Q_COLS], "p (t h c) -> p t h c", t=TOKS, c=ML_QK)
        k_ml = view(latent_raw[:, 0:TOKS * ML_Q_COLS], "p (t h c) -> p t h c", t=TOKS, c=ML_QK)
        o_squares = view(arena[:, 0:DA_JOBS * DA_V], "p (j c) -> p j c", j=DA_JOBS)
        silu = view(arena[:, 0:TOKS * FB], "p (t c) -> p t c", t=TOKS)
        act = view(arena[:, 1024:1024 + TOKS * FB], "p (t c) -> p t c", t=TOKS)
        y_sb = arena[:, 2048:2048 + D]
        give = view(arena[:, 3072:3072 + S], "p (t s) -> p t s", t=TOKS)
        giveT = view(arena[:, 3328:3328 + S], "p (t s) -> p t s", t=TOKS)
        junk = sb("junk", [P, Q_RANK])

        w_uq = sb("w_uq", [P, 2, ML_Q_COLS])
        w_ukv = sb("w_ukv", [P, KV_COLS])
        latent_gain = sb("latent_gain", [P, Q_RANK + KV_RANK])
        sub_gain = sb("sub_gain", [P, DA_V])
        sub_scaled = sb("sub_scaled", [P, DA_V])
        lam_vecs = view(arena[:, 0:4 * DEPTH * DA_DIM], "p (i l c) -> p i l c", i=4, l=DEPTH)
        lam_prod = view(arena[:, 512:512 + 2 * DEPTH * DA_DIM], "p (i l c) -> p i l c", i=2, l=DEPTH)
        angle = view(arena[:, 768:768 + TOKS * FREQS], "p (t c) -> p t c", t=TOKS)
        turns_f = view(arena[:, 896:896 + TOKS * FREQS], "p (t c) -> p t c", t=TOKS)
        lam_dots = sb("lam_dots", [P, 2, DEPTH])
        lam_exps = sb("lam_exps", [P, 2, DEPTH])
        neg_lam = sb("neg_lam", [P, DEPTH])
        pos_i = sb("pos_i", [P, TOKS], I32)
        pos_f = sb("pos_f", [P, TOKS])
        freq = sb("freq", [P, FREQS])
        turns_i = sb("turns_i", [P, TOKS, FREQS], I32)
        sines = sb("sines", [P, 2, TOKS, FREQS])
        cos_t = sb("cos_t", [P, TOKS, DA_DIM + ROPE])
        sin_t = sb("sin_t", [P, TOKS, DA_DIM + ROPE])
        eps_t = sb("eps_t", [P, 2])
        mean_sq = sb("mean_sq", [P, TOKS])
        norm_sd = sb("norm_sd", [P, TOKS])
        norm_r = sb("norm_r", [P, TOKS])
        lat_sq = sb("lat_sq", [P, TOKS, 2])
        lat_sd = sb("lat_sd", [P, TOKS, 2])
        lat_r = sb("lat_r", [P, TOKS, 2])
        o_sq = sb("o_sq", [P, TOKS, DA_HEADS])
        o_sd = sb("o_sd", [P, TOKS, DA_HEADS])
        o_r = sb("o_r", [P, TOKS, DA_HEADS])
        neg_max = sb("neg_max", [P, JOBS, 2])
        row_sum = sb("row_sum", [P, JOBS, 2])
        row_inv = sb("row_inv", [P, JOBS, 2])
        mix_coef = sb("mix_coef", [P, JOBS])
        ident = sb("ident", [P, P])
        before = sb("before", [P, P])
        ones = sb("ones", [P, P])
        slot_no = sb("slot_no", [P, P])
        expert_no = sb("expert_no", [P, TOKS, EXPERTS])
        r_w = sb("r_w", [P, KC, EXPERTS])
        r_halves = sb("r_halves", [P, KC, 2, EXPERTS], F32R)
        logit_halves = sb("logit_halves", [P, TOKS, 2, EXPERTS])
        rt = {n: sb(f"r_{n}", [P, TOKS, EXPERTS]) for n in
              ("logits", "eq", "cand", "first", "logits2", "eq2", "cand2", "second", "w1", "w2")}
        rs = {n: sb(f"r_{n}", [P, TOKS]) for n in ("m1", "i1", "m2", "i2", "d", "e", "e1", "g1", "g2")}
        mask = sb("mask", [P, TOKS, EXPERTS + 1])
        share = sb("share", [P, TOKS, EXPERTS + 1])
        rank = [sb(f"rank{i}", [P, TOKS, EXPERTS + 1]) for i in range(2)]
        most = sb("most", [P, 1])
        over = sb("over", [P, 1])
        over_i = sb("over_i", [P, 1], I32)
        pick = sb("pick", [P, TOKS, P], F32R)

        psum = ctx.enter_context(nc.psum_tensor("psum", [P, 8, 512], F32))
        bank = [psum[:, i, :] for i in range(8)]
        scores = [psum[:, 2 * i:2 * i + 2, 0:S] for i in range(2)]

        loaded = [sem(f"weights_loaded{i}") for i in range(SLOTS)]
        hi_ready, lo_ready, unit_used = sem("hi_ready"), sem("lo_ready"), sem("unit_used")
        x_loaded = [sem(f"x_loaded{t}") for t in range(TOKS)]
        rope_in, lam_in = sem("rope_in"), sem("lam_in")
        gain_loaded = [sem(f"gain_loaded{i}") for i in range(2)]
        small_loaded, router_loaded = sem("small_loaded"), sem("router_loaded")
        out_stored = sem("out_stored")
        consts = sem("consts")
        iotas = sem("iotas")
        sq_ready = sem("sq_ready")
        sd_ready = sem("sd_ready")
        h_ready = sem("h_ready")
        turned, tT_hi, tT_lo = sem("turned"), sem("tT_hi"), sem("tT_lo")
        rotated = sem("rotated")
        v_copied = sem("v_copied")
        da_turned, da_qT, da_kT = sem("da_turned"), sem("da_qT"), sem("da_kT")
        lat_sd_ready, lat_ready = sem("lat_sd_ready"), sem("lat_ready")
        lat_turned, cqT_ready, ckT_ready = sem("lat_turned"), sem("cqT_ready"), sem("ckT_ready")
        ml_proj = sem("ml_proj")
        ml_nope, ml_qk = sem("ml_nope"), sem("ml_qk")
        ml_turned, ml_qT, ml_kT = sem("ml_turned"), sem("ml_qT"), sem("ml_kT")
        scored, max_ready, probs_ready, mix_ready = sem("scored"), sem("max_ready"), sem("probs_ready"), sem("mix_ready")
        probs_turned, probsT_ready, pv_ready, o_ready = (sem("probs_turned"), sem("probsT_ready"), sem("pv_ready"),
                                                         sem("o_ready"))
        o_sd_ready = sem("o_sd_ready")
        x_added = sem("x_added")
        angles, sines_ready = sem("angles"), sem("sines_ready")
        dots, lam_exp = sem("dots"), sem("lam_exp")
        vstep, astep = sem("vstep"), sem("astep")
        silu_ready, act_ready = sem("silu_ready"), sem("act_ready")
        act_turned, aT_hi_ready, aT_lo_ready = sem("act_turned"), sem("aT_hi_ready"), sem("aT_lo_ready")
        r_split, routed_ps, router_exp, router_d = sem("r_split"), sem("routed_ps"), sem("router_exp"), sem("router_d")
        mask_ready, ranked_ps, flag_ready, h_hi_ready, h_split = (sem("mask_ready"), sem("ranked_ps"), sem("flag_ready"),
                                                                  sem("h_hi_ready"), sem("h_split"))
        pick_ready, give_ready, gathered, g_hi_ready, g_lo_ready = (sem("pick_ready"), sem("give_ready"),
                                                                    sem("gathered"), sem("g_hi_ready"), sem("g_lo_ready"))
        give_turned, giveT_ready = sem("give_turned"), sem("giveT_ready")
        y_ready, scattered, scatter_added = sem("y_ready"), sem("scattered"), sem("scatter_added")

        w_in_v = w_in.rearrange("l (c p) n -> l p c n", p=P)
        w_out_v = w_out.rearrange("l (c p) n -> l p c n", p=P)
        gate_v = ffn_gate.rearrange("o (c p) n -> o p c n", p=P)
        up_v = ffn_up.rearrange("o (c p) n -> o p c n", p=P)
        mgate_v = moe_gate.rearrange("o e (c p) n -> (o e) p c n", p=P)
        mup_v = moe_up.rearrange("o e (c p) n -> (o e) p c n", p=P)
        down_v = ffn_down[0, 0:(DENSE_STEPS - 1) * FB, :].rearrange("(b p c) n -> b p (c n)", p=P, c=FB // P)
        down_last_v = ffn_down[0, (DENSE_STEPS - 1) * FB:, :].rearrange("(p c) n -> p (c n)", p=P)
        mdown_v = moe_down.rearrange("o e (b p c) n -> (o e) b p (c n)", p=P, c=FB // P)
        x_v = x_in.rearrange("o (t p) d -> p (o t) d", p=P)
        out_v = out.rearrange("o (t p) d -> p (o t) d", p=P)
        gains_v = [norm_mix[0:1], norm_ffn[0:1], norm_mix[1:2], norm_ffn[1:2], norm_final.rearrange("(o d) -> o d", o=1)]

        def cols_of(step, moe):
            return DENSE_LAST if not moe and step == DENSE_STEPS - 1 else FB

        block = ctx.enter_context(nc.Block())

        @block.sync
        def _(sp):
            def load(place, j, src, cols=FB):
                if place.tile + j >= SLOTS:
                    sp.wait_ge(lo_ready, place.freed(j))
                if src.ndim == 3:
                    dst = raw[place.slot(j)][:, :].rearrange("p (c n) -> p c n", c=KC)[:, :, 0:cols]
                else:
                    dst = raw[place.slot(j)][:, 0:cols]
                sp.dma_start(dst, src).then_inc(loaded[place.slot(j)], 16)

            def load_gain(k):
                if k >= 2:
                    sp.wait_ge(h_ready, parts_before(k - 2) + NORM_PARTS)
                sp.dma_start(gain[k % 2][:, :], gains_v[k].to_broadcast([P, D])).then_inc(gain_loaded[k % 2], 16)

            def load_small(l):
                if l:
                    sp.wait_ge(ml_proj, 3)
                    sp.wait_ge(lat_ready, 1)
                sp.dma_start(w_uq[:, :, :], mla_w_uq[l].rearrange("(c p) n -> p c n", p=P)).then_inc(small_loaded, 16)
                sp.dma_start(w_ukv[:, :], mla_w_ukv[l]).then_inc(small_loaded, 16)
                sp.dma_start(latent_gain[:, 0:Q_RANK], mla_q_norm[l:l + 1].to_broadcast([P, Q_RANK])).then_inc(small_loaded, 16)
                sp.dma_start(latent_gain[:, Q_RANK:], mla_kv_norm[l:l + 1].to_broadcast([P, KV_RANK])).then_inc(small_loaded, 16)
                sp.dma_start(sub_gain[:, :], da_subln[l:l + 1].to_broadcast([P, DA_V])).then_inc(small_loaded, 16)

            def load_start():
                sp.dma_start(pos_i[:, :], positions.rearrange("o (t p) -> p (o t)", p=P),
                             allow_slow_non_contiguous=True).then_inc(rope_in, 16)
                sp.dma_start(freq[:, :], freqs.to_broadcast([P, FREQS])).then_inc(rope_in, 16)
                for i, vec in enumerate((lq1, lk1, lq2, lk2)):
                    sp.dma_start(lam_vecs[:, i, :, :], vec.unsqueeze(0).to_broadcast([P, DEPTH, DA_DIM])).then_inc(lam_in, 16)
                sp.dma_start(r_w[:, :, :], router[0].rearrange("(c p) n -> p c n", p=P)).then_inc(router_loaded, 16)

            def attention(l):
                place = Place(UNIT0[l], TILE0[l])
                for n, (at, cols) in enumerate(IN_TILES):
                    load(place, n, w_in_v[l, :, :, at:at + cols], cols)
                    if l == 0 and n == 0:
                        load_start()
                    if n == 1:
                        load_small(l)
                        load_gain(2 * l + 1)
                for n in range(2):
                    load(place, 4 + n, w_out_v[l, :, :, n * FB:(n + 1) * FB])

            for t in range(TOKS):
                sp.dma_start(x[:, t, :], x_v[:, t, :]).then_inc(x_loaded[t], 16)
            load_gain(0)
            attention(0)
            place = Place(DENSE_UNIT, DENSE_TILE)
            load(place, 0, gate_v[0, :, :, 0:FB])
            load(place, 1, up_v[0, :, :, 0:FB])
            with sp.Fori(0, DENSE_STEPS - 2) as i:
                step = Place(DENSE_UNIT + 8, DENSE_TILE + 2, fb=i)
                load(step, 0, gate_v[0, :, :, bass.ds((i + 1) * FB, FB)])
                load(step, 1, up_v[0, :, :, bass.ds((i + 1) * FB, FB)])
                load(step, 2, down_v[i], FB // P * D)
            last = Place(DENSE_UNIT + 8 + STEP_UNITS * (DENSE_STEPS - 2), DENSE_TILE + 2 + STEP_TILES * (DENSE_STEPS - 2))
            load(last, 0, gate_v[0, :, :, (DENSE_STEPS - 1) * FB:FF_DENSE], DENSE_LAST)
            load(last, 1, up_v[0, :, :, (DENSE_STEPS - 1) * FB:FF_DENSE], DENSE_LAST)
            load(last, 2, down_v[DENSE_STEPS - 2], FB // P * D)
            load(last, 3, down_last_v, DENSE_LAST // P * D)
            load_gain(2)
            attention(1)

            def experts(unit0, tile0):
                with sp.Fori(0, EXPERTS) as e:
                    first = Place(unit0, tile0, e=e)
                    load(first, 0, mgate_v[e, :, :, 0:FB])
                    load(first, 1, mup_v[e, :, :, 0:FB])
                    with sp.Fori(0, STEPS - 1) as i:
                        step = Place(unit0 + 8, tile0 + 2, e=e, fb=i)
                        load(step, 0, mgate_v[e, :, :, bass.ds((i + 1) * FB, FB)])
                        load(step, 1, mup_v[e, :, :, bass.ds((i + 1) * FB, FB)])
                        load(step, 2, mdown_v[e, i], FB // P * D)
                    load(Place(unit0 + 8 + STEP_UNITS * (STEPS - 1), tile0 + 2 + STEP_TILES * (STEPS - 1), e=e), 0,
                         mdown_v[e, STEPS - 1], FB // P * D)

            experts(MOE_UNIT, MOE_TILE)
            load_gain(4)
            sp.wait_ge(flag_ready, 1)
            some_over = sp.value_load(over_i[0:1, 0:1], min_val=0, max_val=1)
            with sp.If(some_over == 1):
                experts(MOE_UNIT + EXPERTS * EXPERT_UNITS, MOE_TILE + EXPERTS * EXPERT_TILES)
            for t in range(TOKS):
                sp.wait_ge(h_ready, parts_before(4) + 2 * (t + 1))
                sp.dma_start(out_v[:, t, :], h[:, t, :]).then_inc(out_stored, 16)
            sp.wait_ge(out_stored, 16 * TOKS)

        @block.gpsimd
        def _(pool):
            pool.memset(ident[:, :], 0.0).then_inc(iotas, 1)
            pool.memset(before[:, :], 1.0).then_inc(iotas, 1)
            pool.memset(ones[:, :], 1.0).then_inc(consts, 1)
            pool.memset(eps_t[:, 0:1], NORM_EPS).then_inc(consts, 1)
            pool.memset(eps_t[:, 1:2], SUBLN_EPS).then_inc(consts, 1)
            pool.wait_ge(iotas, 2)
            pool.affine_select(out=ident[:, :], in_=ident[:, :], compare_op=ALU.not_equal, fill=1.0, base=0,
                               pattern=[[-1, P]], channel_multiplier=1).then_inc(consts, 1)
            pool.affine_select(out=before[:, :], in_=before[:, :], compare_op=ALU.is_gt, fill=0.0, base=0,
                               pattern=[[1, P]], channel_multiplier=-1).then_inc(consts, 1)
            pool.iota(slot_no[:, :], pattern=[[1, P]], base=0, channel_multiplier=0,
                      allow_small_or_imprecise_dtypes=True).then_inc(consts, 1)
            pool.iota(expert_no[:, :, :], pattern=[[0, TOKS], [1, EXPERTS]], base=-EXPERTS, channel_multiplier=0,
                      allow_small_or_imprecise_dtypes=True).then_inc(consts, 1)
            for tab in (mask, share, rank[0], rank[1]):
                pool.memset(tab[:, :, EXPERTS:EXPERTS + 1], 0.0).then_inc(consts, 1)

        CONSTS = 11

        @block.scalar
        def _(sc):
            steps = [0]

            def chain(ins):
                steps[0] += 1
                ins.then_inc(astep, 1)
                sc.wait_ge(astep, steps[0])

            def high(place, units, cols=FB):
                for i in units:
                    if i % TILE_UNITS == 0:
                        sc.wait_ge(loaded[place.slot(i // TILE_UNITS)], place.loaded(i // TILE_UNITS))
                    if place.unit + i >= RING:
                        sc.wait_ge(unit_used, place.used(i - RING))
                    src = raw[place.slot(i // TILE_UNITS)][:, i % TILE_UNITS * UNIT:(i % TILE_UNITS + 1) * UNIT]
                    dst = w_hi[place.ring(i)][:, :]
                    if cols < FB:
                        src = src.rearrange("p (c n) -> p c n", c=2)[:, :, 0:cols]
                        dst = dst.rearrange("p (c n) -> p c n", c=2)[:, :, 0:cols]
                    sc.activation(dst, src, ACT.Copy).then_inc(hi_ready, 1)

            def norm(k):
                if k:
                    sc.wait_ge(x_added, {1: 2, 2: 3, 3: 5, 4: 6}[k])
                else:
                    sc.wait_ge(x_loaded[0], 16)
                chain(sc.activation(h[:, 0, :], x[:, 0, :], ACT.Square, scale=D ** -0.5, accum_out=mean_sq[:, 0:1]))
                if k == 0:
                    sc.wait_ge(consts, CONSTS)
                sc.wait_ge(sq_ready, k + 1)
                sc.activation(norm_sd[:, :], mean_sq[:, :], ACT.Sqrt, bias=eps_t[:, 0:1]).then_inc(sd_ready, 1)

            def turn(k, first_bank):
                for g in range(4):
                    sc.wait_ge(turned, 4 * k + g + 1)
                    t, c = g % 2, 4 * (g // 2)
                    sc.activation(hT_hi[:, c:c + 4, t * P:(t + 1) * P],
                                  bank[first_bank + g].rearrange("p (c t) -> p c t", c=4), ACT.Copy).then_inc(tT_hi, 1)

            def heads_of(b, heads=ML_HEADS):
                return b[:, 0:ML_Q_COLS].rearrange("p (h c) -> p h c", c=ML_QK)

            def attention(l):
                place = Place(UNIT0[l], TILE0[l])
                high(place, range(AHEAD, 7))
                sc.wait_ge(unit_used, place.used(3))
                for t in range(TOKS):
                    ins = sc.activation(rest[:, t, :], bank[t][:, 0:REST], ACT.Copy)
                ins.then_inc(v_copied, 1)
                sc.wait_ge(v_copied, 2 * l + 1)
                for t in range(TOKS):
                    for i, (a, n) in enumerate(((0, Q_RANK), (Q_RANK, KV_RANK))):
                        ins = sc.activation(junk[:, 0:n], rest[:, t, a:a + n], ACT.Square, scale=n ** -0.5,
                                            accum_out=lat_sq[:, t, i:i + 1])
                        chain(ins)
                sc.activation(lat_sd[:, :, :], lat_sq[:, :, :], ACT.Sqrt, bias=eps_t[:, 0:1]).then_inc(lat_sd_ready, 1)
                high(place, range(7, 10))
                sc.wait_ge(lat_turned, 2 * l + 1)
                sc.activation(cqT[:, :, :], bank[0].rearrange("p (c t) -> p c t", c=2), ACT.Copy).then_inc(cqT_ready, 1)
                high(place, range(10, 14))
                sc.wait_ge(ml_proj, 3 * l + 1)
                for t in range(TOKS):
                    ins = sc.activation(q_ml[:, t, :, 0:NOPE], heads_of(bank[t])[:, :, 0:NOPE], ACT.Copy)
                ins.then_inc(ml_nope, 1)
                high(place, range(14, 18))
                sc.wait_ge(unit_used, place.used(15))
                for t in range(TOKS):
                    ins = sc.activation(v_da[:, t, :], bank[6 + t], ACT.Copy)
                ins.then_inc(v_copied, 1)
                for t in range(TOKS):
                    sc.wait_ge(ml_proj, 3 * l + 2 + t)
                    for i in range(2):
                        kv = bank[2 + 2 * t + i][:, 0:2 * KV_HEAD].rearrange("p (h c) -> p h c", c=KV_HEAD)
                        ins = sc.activation(k_ml[:, t, 2 * i:2 * i + 2, 0:NOPE], kv[:, :, 0:NOPE], ACT.Copy)
                    ins.then_inc(ml_nope, 1)
                for g in range(2):
                    sc.wait_ge(da_turned, 4 * l + g + 1)
                    sc.activation(qT_da[:, 2 * g:2 * g + 2, :], bank[g].rearrange("p (h t) -> p h t", h=2),
                                  ACT.Copy, scale=DA_DIM ** -0.5).then_inc(da_qT, 1)
                for g in range(2):
                    sc.wait_ge(ml_turned, 4 * l + g + 1)
                    sc.activation(qT_ml[0:ML_QK, 2 * g:2 * g + 2, :], bank[2 + g][0:ML_QK, :].rearrange("p (h t) -> p h t", h=2),
                                  ACT.Copy, scale=ML_QK ** -0.5).then_inc(ml_qT, 1)
                base = JOBS * l
                for i in range(JOBS + 3):
                    if i == 3:
                        high(place, range(18, 16 + AHEAD))
                    j = i
                    if j < JOBS:
                        sc.wait_ge(max_ready, base + j + 1)
                        if j >= 2:
                            sc.wait_ge(probs_turned, base + j - 1)
                        for c in range(2):
                            ins = sc.activation(probs[j % 2][:, c, :], scores[j % 2][:, c, :], ACT.Exp,
                                                bias=neg_max[:, j, c:c + 1], accum_out=row_sum[:, j, c:c + 1])
                        ins.then_inc(probs_ready, 1)
                    j = i - 2
                    if 0 <= j < JOBS:
                        n = S if j < DA_JOBS else 2 * S
                        sc.wait_ge(probs_turned, base + j + 1)
                        if j >= 2:
                            sc.wait_ge(pv_ready, base + j - 1)
                        sc.activation(probsT[j % 2][:, 0:n], bank[4 + j % 2][:, 0:n], ACT.Copy).then_inc(probsT_ready, 1)
                    j = i - 5
                    if 0 <= j < DA_JOBS:
                        sc.wait_ge(o_ready, base + j + 1)
                        t, hd = j % 2, j // 2
                        ins = sc.activation(o_squares[:, j, :], h[:, t, hd * P:(hd + 1) * P], ACT.Square, scale=DA_V ** -0.5,
                                            accum_out=o_sq[:, t, hd:hd + 1])
                        if j == DA_JOBS - 1:
                            chain(ins)
                            sc.activation(o_sd[:, :, :], o_sq[:, :, :], ACT.Sqrt, bias=eps_t[:, 1:2]).then_inc(o_sd_ready, 1)
                turn(3 * l + 1, 0)
                high(place, range(16 + AHEAD, 24))
                nxt = Place(place.unit + 24, place.tile + 6)
                high(nxt, range(AHEAD))
                norm(2 * l + 1)
                turn(3 * l + 2, 0)

            def silu_of(step, fb_count, toks, cols):
                sc.wait_ge(unit_used, step.used(3))
                if not (isinstance(fb_count, int) and fb_count == 1):
                    sc.wait_ge(act_ready, fb_count - 1)
                for t in range(toks):
                    ins = sc.activation(silu[:, t, 0:cols], bank[t][:, 0:cols], ACT.Silu)
                ins.then_inc(silu_ready, 1)

            def act_hi(count, toks, banks, chunks):
                for t in range(toks):
                    sc.wait_ge(act_turned, count + t + 1)
                    sc.activation(aT_hi[:, 0:chunks, t * P:(t + 1) * P],
                                  bank[banks[t]][:, 0:chunks * P].rearrange("p (c t) -> p c t", c=chunks),
                                  ACT.Copy).then_inc(aT_hi_ready, 1)

            norm(0)
            turn(0, 4)
            high(Place(0, 0), range(4), REST)
            high(Place(0, 0), [4])
            sc.wait_ge(angles, 1)
            sc.activation(sines[:, 0, :, :], angle[:, :, :], ACT.Sin)
            sc.activation(sines[:, 1, :, :], angle[:, :, :], ACT.Sin, scale=0.5).then_inc(sines_ready, 1)
            sc.wait_ge(dots, 1)
            sc.activation(lam_exps[:, :, :], lam_dots[:, :, :], ACT.Exp).then_inc(lam_exp, 1)
            sc.wait_ge(router_loaded, 16)
            sc.activation(r_halves[:, :, 0, :], r_w[:, :, :], ACT.Copy).then_inc(r_split, 1)
            attention(0)

            high(Place(DENSE_UNIT, DENSE_TILE), range(AHEAD, 8))
            silu_of(Place(DENSE_UNIT, DENSE_TILE), 1, TOKS, FB)
            with sc.Fori(0, DENSE_STEPS - 2) as i:
                step = Place(DENSE_UNIT + 8, DENSE_TILE + 2, fb=i)
                high(step, range(0, AHEAD))
                act_hi(i * TOKS, TOKS, (2, 3), FB // P)
                high(step, range(AHEAD, 9))
                silu_of(step, i + 2, TOKS, FB)
                high(step, range(9, 12))
            last = Place(DENSE_UNIT + 8 + STEP_UNITS * (DENSE_STEPS - 2), DENSE_TILE + 2 + STEP_TILES * (DENSE_STEPS - 2))
            high(last, range(0, AHEAD), DENSE_LAST)
            act_hi((DENSE_STEPS - 2) * TOKS, TOKS, (2, 3), FB // P)
            high(last, range(AHEAD, 8), DENSE_LAST)
            high(last, [8])
            silu_of(last, DENSE_STEPS, TOKS, DENSE_LAST)
            high(last, range(9, 12 + DENSE_LAST // P))
            act_hi((DENSE_STEPS - 1) * TOKS, TOKS, (2, 3), DENSE_LAST // P)
            high(Place(UNIT0[1], TILE0[1]), range(4), REST)
            high(Place(UNIT0[1], TILE0[1]), [4])
            norm(2)
            turn(3, 4)
            attention(1)

            sc.wait_ge(routed_ps, 1)
            for t in range(TOKS):
                sc.activation(h_hi[:, t, :], h[:, t, :], ACT.Copy).then_inc(h_hi_ready, 1)
            sc.wait_ge(router_d, 1)
            sc.activation(rs["e"][:, :], rs["d"][:, :], ACT.Exp).then_inc(router_exp, 1)

            def experts(unit0, tile0, fb0, tok0, e0):
                def gather_hi(e):
                    for g in range(2):
                        sc.wait_ge(gathered, (e + e0) * 4 + g + 1)
                        sc.activation(g_hi[:, 4 * g:4 * g + 4, :], bank[3 + g][:, :].rearrange("p (c t) -> p c t", c=4),
                                      ACT.Copy).then_inc(g_hi_ready, 1)

                def y_out(nxt):
                    sc.wait_ge(unit_used, nxt.used(-1))
                    for half in range(2):
                        sc.activation(y_sb[:, half * 512:(half + 1) * 512], bank[5 + half][:, :], ACT.Copy).then_inc(y_ready, 1)

                def step0(e, place, units):
                    high(place, units)
                    silu_of(place, e * STEPS + (fb0 + 1), 1, FB)
                    sc.wait_ge(give_turned, e + (e0 + 1))
                    sc.activation(giveT[:, :, :], bank[2][:, 0:S].rearrange("p (t s) -> p t s", t=TOKS),
                                  ACT.Copy).then_inc(giveT_ready, 1)

                def steps(e, reg):
                    step = Place(unit0 + 8, tile0 + 2, e=reg)
                    if reg is None:
                        step = step.plus(e * EXPERT_UNITS, e * EXPERT_TILES)
                    high(step, range(0, 9))
                    silu_of(step, e * STEPS + (fb0 + 2), 1, FB)
                    act_hi(e * STEPS + tok0, 1, (2,), FB // P)
                    high(step, range(9, 12))
                    with sc.Fori(0, STEPS - 2) as i:
                        step = Place(step.unit + STEP_UNITS, step.tile + STEP_TILES, e=reg, fb=i)
                        high(step, range(0, AHEAD))
                        act_hi(e * STEPS + i + (tok0 + 1), 1, (2,), FB // P)
                        high(step, range(AHEAD, 9))
                        silu_of(step, e * STEPS + i + (fb0 + 3), 1, FB)
                        high(step, range(9, 12))
                    tail = Place(step.unit + STEP_UNITS * (STEPS - 2), step.tile + STEP_TILES * (STEPS - 2), e=reg)
                    high(tail, range(2))
                    act_hi(e * STEPS + (tok0 + STEPS - 1), 1, (2,), FB // P)
                    high(tail, [2])
                    return tail

                first = Place(unit0, tile0)
                if e0:
                    high(first, range(AHEAD))
                gather_hi(0)
                step0(0, first, range(AHEAD, 8))
                with sc.Fori(0, EXPERTS - 1) as e:
                    tail = steps(e, e)
                    gather_hi(e + 1)
                    high(tail, [3])
                    nxt = tail.plus(4, 1)
                    high(nxt, [0])
                    y_out(nxt)
                    step0(e + 1, nxt, range(1, 8))
                tail = steps(EXPERTS - 1, None)
                high(tail, [3])
                y_out(tail.plus(4, 1))

            experts(MOE_UNIT, MOE_TILE, DENSE_STEPS, DENSE_STEPS * TOKS, 0)
            sc.wait_ge(flag_ready, 1)
            some_over = sc.value_load(over_i[0:1, 0:1], min_val=0, max_val=1)
            with sc.If(some_over == 1):
                experts(MOE_UNIT + EXPERTS * EXPERT_UNITS, MOE_TILE + EXPERTS * EXPERT_TILES,
                        DENSE_STEPS + EXPERTS * STEPS, DENSE_STEPS * TOKS + EXPERTS * STEPS, EXPERTS)
            norm(4)

        @block.vector
        def _(ve):
            steps_done = [0]

            def chain(ins):
                steps_done[0] += 1
                ins.then_inc(vstep, 1)
                ve.wait_ge(vstep, steps_done[0])

            def low(place, units, cols=FB):
                for i in units:
                    ve.wait_ge(hi_ready, place.used(i))
                    src = raw[place.slot(i // TILE_UNITS)][:, i % TILE_UNITS * UNIT:(i % TILE_UNITS + 1) * UNIT]
                    hi, lo = w_hi[place.ring(i)][:, :].bitcast(F32), w_lo[place.ring(i)][:, :]
                    if cols < FB:
                        src, hi, lo = (a.rearrange("p (c n) -> p c n", c=2)[:, :, 0:cols] for a in (src, hi, lo))
                    ve.tensor_tensor(lo, src, hi, ALU.subtract).then_inc(lo_ready, 1)

            def norm(k):
                if k == 0:
                    ve.wait_ge(x_loaded[1], 16)
                elif k < 4:
                    ve.wait_ge(x_added, {1: 2, 2: 3, 3: 5}[k])
                ve.tensor_tensor_reduce(h[:, 1, :], x[:, 1, :], x[:, 1, :], 1.0 / D, 0.0, ALU.mult, ALU.add,
                                        mean_sq[:, 1:2]).then_inc(sq_ready, 1)
                ve.wait_ge(sd_ready, k + 1)
                chain(ve.reciprocal(norm_r[:, :], norm_sd[:, :]))
                ve.wait_ge(gain_loaded[k % 2], 16 * (k // 2 + 1))
                if k == 0:
                    ve.wait_ge(x_loaded[0], 16)
                for g in range(4):
                    t, half = (g % 2, g // 2) if k < 4 else (g // 2, g % 2)
                    part = slice(half * 512, (half + 1) * 512)
                    ve.scalar_tensor_tensor(out=h[:, t, part], in0=x[:, t, part], scalar=norm_r[:, t:t + 1],
                                            in1=gain[k % 2][:, part], op0=ALU.mult, op1=ALU.mult).then_inc(h_ready, 1)

            def turn(k, first_bank):
                for g in range(4):
                    ve.wait_ge(tT_hi, 4 * k + g + 1)
                    t, c = g % 2, 4 * (g // 2)
                    at = (slice(None), slice(c, c + 4), slice(t * P, (t + 1) * P))
                    ve.tensor_tensor(hT_lo[at], bank[first_bank + g].rearrange("p (c t) -> p c t", c=4),
                                     hT_hi[at].bitcast(F32), ALU.subtract).then_inc(tT_lo, 1)

            def rotate(dst, src, t, heads, half, at):
                cos = cos_t[:, t, at:at + 2 * half].unsqueeze(1).to_broadcast([P, heads, 2 * half])
                sn = [sin_t[:, t, at + i * half:at + (i + 1) * half].unsqueeze(1).to_broadcast([P, heads, half])
                      for i in range(2)]
                n = heads * 2 * half
                a = probs_raw[0][:, 0:n].rearrange("p (h c) -> p h c", h=heads)
                b = probs_raw[1][:, 0:n].rearrange("p (h c) -> p h c", h=heads)
                ve.tensor_tensor(a, src, cos, ALU.mult)
                ve.tensor_tensor(b[:, :, 0:half], src[:, :, half:], sn[0], ALU.mult)
                chain(ve.tensor_tensor(b[:, :, half:], src[:, :, 0:half], sn[1], ALU.mult))
                return ve.tensor_tensor(dst, a, b, ALU.add)

            def rotate_da(l, n, dst, banks):
                ve.wait_ge(unit_used, Place(UNIT0[l], TILE0[l]).used(4 * n + 7))
                for t in range(TOKS):
                    ins = rotate(dst[:, t, :].rearrange("p (h c) -> p h c", c=DA_DIM),
                                 bank[banks[t]].rearrange("p (h c) -> p h c", c=DA_DIM), t, 2 * DA_HEADS, HALF, 0)
                    if t < TOKS - 1:
                        chain(ins)
                ins.then_inc(rotated, 1)
                ve.wait_ge(rotated, 2 * l + n + 1)

            def attention(l):
                place = Place(UNIT0[l], TILE0[l])
                low(place, range(AHEAD, 7))
                if l == 0:
                    tables()
                ve.wait_ge(v_copied, 2 * l + 1)
                for t in range(TOKS):
                    chain(rotate(k_pe[:, t, :].unsqueeze(1), rest[:, t, Q_RANK + KV_RANK:].unsqueeze(1), t, 1, ROPE // 2, DA_DIM))
                ve.wait_ge(small_loaded, 80 * (l + 1))
                ve.tensor_scalar(sub_scaled[:, :], sub_gain[:, :], 1.0 - lambda_init(l), None, ALU.mult)
                ve.wait_ge(lat_sd_ready, l + 1)
                chain(ve.reciprocal(lat_r[:, :, :], lat_sd[:, :, :]))
                for t in range(TOKS):
                    for i, (a, n) in enumerate(((0, Q_RANK), (Q_RANK, KV_RANK))):
                        ins = ve.scalar_tensor_tensor(out=latent[:, t, a:a + n], in0=rest[:, t, a:a + n],
                                                      scalar=lat_r[:, t, i:i + 1], in1=latent_gain[:, a:a + n],
                                                      op0=ALU.mult, op1=ALU.mult)
                ins.then_inc(lat_ready, 1)
                low(place, range(7, 10))
                rotate_da(l, 0, q_rot, (2, 3))
                ve.wait_ge(lat_turned, 2 * l + 2)
                ve.tensor_copy(ckT[:, :], bank[1][:, 0:S]).then_inc(ckT_ready, 1)
                low(place, range(10, 14))
                rotate_da(l, 1, k_rot, (4, 5))
                low(place, [14])
                ve.wait_ge(ml_nope, 3 * l + 1)
                for t in range(TOKS):
                    ins = rotate(q_ml[:, t, :, NOPE:], bank[t][:, 0:ML_Q_COLS].rearrange("p (h c) -> p h c", c=ML_QK)[:, :, NOPE:],
                                 t, ML_HEADS, ROPE // 2, DA_DIM)
                    if t < TOKS - 1:
                        chain(ins)
                ins.then_inc(ml_qk, 1)
                low(place, range(15, 18))
                for t in range(TOKS):
                    ve.wait_ge(ml_nope, 3 * l + 2 + t)
                    for i in range(2):
                        kv = bank[2 + 2 * t + i][:, 0:2 * KV_HEAD].rearrange("p (h c) -> p h c", c=KV_HEAD)
                        ve.tensor_copy(v_ml[:, t, 2 * i * ML_V:2 * (i + 1) * ML_V].rearrange("p (h c) -> p h c", h=2),
                                       kv[:, :, NOPE:])
                    ins = ve.tensor_copy(k_ml[:, t, :, NOPE:], k_pe[:, t, :].unsqueeze(1).to_broadcast([P, ML_HEADS, ROPE]))
                ins.then_inc(ml_qk, 1)
                for g in range(2):
                    ve.wait_ge(da_turned, 4 * l + 3 + g)
                    ve.tensor_copy(kT_da[:, 2 * g:2 * g + 2, :],
                                   bank[6 + g].rearrange("p (h t) -> p h t", h=2)).then_inc(da_kT, 1)
                for g in range(2):
                    ve.wait_ge(ml_turned, 4 * l + 3 + g)
                    ve.tensor_copy(kT_ml[0:ML_QK, 2 * g:2 * g + 2, :],
                                   bank[4 + g][0:ML_QK, :].rearrange("p (h t) -> p h t", h=2)).then_inc(ml_kT, 1)
                base = JOBS * l
                for i in range(JOBS + 4):
                    if i == 3:
                        low(place, range(18, 16 + AHEAD))
                    j = i
                    if j < JOBS:
                        ve.wait_ge(scored, base + j + 1)
                        ve.tensor_reduce(neg_max[:, j, :], scores[j % 2], AX.X, ALU.max, negate=True).then_inc(max_ready, 1)
                    j = i - 1
                    if 0 <= j < JOBS:
                        ve.wait_ge(probs_ready, base + j + 1)
                        ins = ve.reciprocal(row_inv[:, j, :], row_sum[:, j, :])
                        if j < DA_JOBS:
                            chain(ins)
                            chain(ve.scalar_tensor_tensor(out=mix_coef[:, j:j + 1], in0=row_inv[:, j, 1:2],
                                                          scalar=row_sum[:, j, 0:1], in1=neg_lam[:, l:l + 1],
                                                          op0=ALU.mult, op1=ALU.mult))
                            if j >= 2:
                                ve.wait_ge(probs_turned, base + j - 1)
                            ins = ve.scalar_tensor_tensor(out=mixed[j % 2][:, :], in0=probs[j % 2][:, 1, :],
                                                          scalar=mix_coef[:, j:j + 1], in1=probs[j % 2][:, 0, :],
                                                          op0=ALU.mult, op1=ALU.add)
                        ins.then_inc(mix_ready, 1)
                    if i == JOBS + 2:
                        ve.wait_ge(o_sd_ready, l + 1)
                        chain(ve.reciprocal(o_r[:, :, :], o_sd[:, :, :]))
                        for t in range(TOKS):
                            for hd in range(DA_HEADS):
                                o = h[:, t, hd * P:(hd + 1) * P]
                                ins = ve.scalar_tensor_tensor(out=o, in0=o, scalar=o_r[:, t, hd:hd + 1], in1=sub_scaled[:, :],
                                                              op0=ALU.mult, op1=ALU.mult)
                            ins.then_inc(h_ready, 1)
                    j = i - 4
                    if 0 <= j < JOBS:
                        ve.wait_ge(pv_ready, base + j + 1)
                        if j < DA_JOBS:
                            t, hd = j % 2, j // 2
                            ins = ve.tensor_scalar(h[:, t, hd * P:(hd + 1) * P], bank[6 + j % 2][:, 0:P],
                                                   row_inv[:, j, 0:1], None, ALU.mult)
                        else:
                            t, pair = j % 2, (j - DA_JOBS) // 2
                            for c in range(2):
                                col = DA_HEADS * DA_V + (2 * pair + c) * P
                                ins = ve.tensor_scalar(h[:, t, col:col + P], bank[6 + j % 2][:, c * P:(c + 1) * P],
                                                       row_inv[:, j, c:c + 1], None, ALU.mult)
                        ins.then_inc(o_ready, 1)
                turn(3 * l + 1, 0)
                low(place, range(16 + AHEAD, 24))
                nxt = Place(place.unit + 24, place.tile + 6)
                low(nxt, [0])
                for n in range(2):
                    ve.wait_ge(unit_used, place.used(19 + 4 * n))
                    for t in range(TOKS):
                        xs = x[:, t, n * 512:(n + 1) * 512]
                        ins = ve.tensor_tensor(xs, xs, bank[4 + 2 * n + t], ALU.add)
                    ins.then_inc(x_added, 1)
                    if n == 0:
                        low(nxt, range(1, AHEAD))
                norm(2 * l + 1)
                turn(3 * l + 2, 0)

            def multiply(up_used, fb_count, toks, up_banks, cols):
                ve.wait_ge(silu_ready, fb_count)
                ve.wait_ge(unit_used, up_used)
                for t in range(toks):
                    ins = ve.tensor_tensor(act[:, t, 0:cols], silu[:, t, 0:cols], bank[up_banks[t]][:, 0:cols], ALU.mult)
                ins.then_inc(act_ready, 1)

            def act_lo(count, toks, banks, chunks):
                for t in range(toks):
                    ve.wait_ge(aT_hi_ready, count + t + 1)
                    at = (slice(None), slice(0, chunks), slice(t * P, (t + 1) * P))
                    ve.tensor_tensor(aT_lo[at], bank[banks[t]][:, 0:chunks * P].rearrange("p (c t) -> p c t", c=chunks),
                                     aT_hi[at].bitcast(F32), ALU.subtract).then_inc(aT_lo_ready, 1)

            def tables():
                ve.wait_ge(sines_ready, 1)
                for t in range(TOKS):
                    for a, f, n in ((0, 0, HALF), (DA_DIM, HALF, ROPE // 2)):
                        s, s_half = sines[:, 0, t, f:f + n], sines[:, 1, t, f:f + n]
                        ve.tensor_scalar(sin_t[:, t, a:a + n], s, -1.0, None, ALU.mult)
                        ve.tensor_copy(sin_t[:, t, a + n:a + 2 * n], s)
                        for i in range(2):
                            ins = ve.tensor_tensor(cos_t[:, t, a + i * n:a + (i + 1) * n], s_half, s_half, ALU.mult)
                chain(ins)
                chain(ve.tensor_scalar(cos_t[:, :, :], cos_t[:, :, :], -2.0, 1.0, ALU.mult, ALU.add))
                ve.wait_ge(lam_exp, 1)
                chain(ve.tensor_tensor(neg_lam[:, :], lam_exps[:, 1, :], lam_exps[:, 0, :], ALU.subtract))
                for l in range(DEPTH):
                    ins = ve.tensor_scalar(neg_lam[:, l:l + 1], neg_lam[:, l:l + 1], -lambda_init(l), None, ALU.add)
                chain(ins)

            norm(0)
            turn(0, 4)
            low(Place(0, 0), range(4), REST)
            low(Place(0, 0), [4])
            ve.wait_ge(rope_in, 32)
            chain(ve.tensor_copy(pos_f[:, :], pos_i[:, :]))
            for t in range(TOKS):
                ins = ve.tensor_scalar(angle[:, t, :], freq[:, :], pos_f[:, t:t + 1], None, ALU.mult)
            chain(ins)
            chain(ve.tensor_scalar(turns_i[:, :, :], angle[:, :, :], 1 / TWO_PI, None, ALU.mult))
            chain(ve.tensor_copy(turns_f[:, :, :], turns_i[:, :, :]))
            for c in (_C1, _C2, _C3):
                chain(ve.scalar_tensor_tensor(out=angle[:, :, :], in0=turns_f[:, :, :], scalar=-c, in1=angle[:, :, :],
                                              op0=ALU.mult, op1=ALU.add))
            ve.tensor_scalar(angle[:, :, :], angle[:, :, :], PI_DOWN, -PI_DOWN, ALU.min, ALU.max).then_inc(angles, 1)
            ve.wait_ge(lam_in, 64)
            for i in range(2):
                ins = ve.tensor_tensor(lam_prod[:, i, :, :], lam_vecs[:, 2 * i, :, :], lam_vecs[:, 2 * i + 1, :, :], ALU.mult)
            chain(ins)
            ve.tensor_reduce(lam_dots[:, :, :], lam_prod[:, :, :, :], AX.X, ALU.add).then_inc(dots, 1)
            ve.wait_ge(r_split, 1)
            ve.tensor_tensor(r_halves[:, :, 1, :], r_w[:, :, :], r_halves[:, :, 0, :].bitcast(F32), ALU.subtract).then_inc(r_split, 1)
            attention(0)

            low(Place(DENSE_UNIT, DENSE_TILE), range(AHEAD, 8))
            multiply(Place(DENSE_UNIT, DENSE_TILE).used(7), 1, TOKS, (2, 3), FB)
            with ve.Fori(0, DENSE_STEPS - 2) as i:
                step = Place(DENSE_UNIT + 8, DENSE_TILE + 2, fb=i)
                low(step, range(0, AHEAD))
                act_lo(i * TOKS, TOKS, (2, 3), FB // P)
                low(step, range(AHEAD, 12))
                multiply(step.used(7), i + 2, TOKS, (2, 3), FB)
            last = Place(DENSE_UNIT + 8 + STEP_UNITS * (DENSE_STEPS - 2), DENSE_TILE + 2 + STEP_TILES * (DENSE_STEPS - 2))
            low(last, range(0, AHEAD), DENSE_LAST)
            act_lo((DENSE_STEPS - 2) * TOKS, TOKS, (2, 3), FB // P)
            low(last, range(AHEAD, 8), DENSE_LAST)
            low(last, range(8, 12))
            multiply(last.used(7), DENSE_STEPS, TOKS, (2, 3), DENSE_LAST)
            low(last, range(12, 12 + DENSE_LAST // P))
            act_lo((DENSE_STEPS - 1) * TOKS, TOKS, (2, 3), DENSE_LAST // P)
            low(Place(UNIT0[1], TILE0[1]), range(4), REST)
            low(Place(UNIT0[1], TILE0[1]), [4])
            ve.wait_ge(unit_used, Place(UNIT0[1], TILE0[1]).used(-1))
            for t in range(TOKS):
                for half in range(2):
                    xs = x[:, t, half * 512:(half + 1) * 512]
                    ins = ve.tensor_tensor(xs, xs, bank[4 + 2 * t + half][:, :], ALU.add)
            ins.then_inc(x_added, 1)
            norm(2)
            turn(3, 4)
            attention(1)

            ve.wait_ge(routed_ps, 1)
            shape = [P, TOKS, EXPERTS]

            def wide(a):
                return a[:, :].unsqueeze(2).to_broadcast(shape)

            chain(ve.tensor_copy(logit_halves[:, :, :, :],
                                 bank[5][:, 0:TOKS * 2 * EXPERTS].rearrange("p (t i e) -> p t i e", t=TOKS, i=2)))
            chain(ve.tensor_tensor(rt["logits"][:, :, :], logit_halves[:, :, 0, :], logit_halves[:, :, 1, :], ALU.add))
            ve.wait_ge(consts, CONSTS)

            def best(logits, m, eq, cand, i, onehot):
                chain(ve.tensor_reduce(rs[m][:, :], rt[logits][:, :, :], AX.X, ALU.max))
                chain(ve.tensor_tensor(rt[eq][:, :, :], rt[logits][:, :, :], wide(rs[m]), ALU.is_equal))
                chain(ve.tensor_tensor(rt[cand][:, :, :], rt[eq][:, :, :], expert_no[:, :, :], ALU.mult))
                chain(ve.tensor_reduce(rs[i][:, :], rt[cand][:, :, :], AX.X, ALU.min))
                chain(ve.tensor_tensor(rt[onehot][:, :, :], expert_no[:, :, :], wide(rs[i]), ALU.is_equal))

            best("logits", "m1", "eq", "cand", "i1", "first")
            chain(ve.scalar_tensor_tensor(out=rt["logits2"][:, :, :], in0=rt["first"][:, :, :], scalar=-3e38,
                                          in1=rt["logits"][:, :, :], op0=ALU.mult, op1=ALU.add))
            best("logits2", "m2", "eq2", "cand2", "i2", "second")
            ve.tensor_tensor(rs["d"][:, :], rs["m2"][:, :], rs["m1"][:, :], ALU.subtract).then_inc(router_d, 1)
            ve.tensor_tensor(mask[:, :, 0:EXPERTS], rt["first"][:, :, :], rt["second"][:, :, :], ALU.add).then_inc(mask_ready, 1)
            for t in range(TOKS):
                ve.wait_ge(h_hi_ready, t + 1)
                ve.tensor_tensor(h_lo[:, t, :], h[:, t, :], h_hi[:, t, :].bitcast(F32), ALU.subtract).then_inc(h_split, 1)
            ve.wait_ge(ranked_ps, 1)
            ranks = bank[6][:, 0:TOKS * EXPERTS].rearrange("p (t e) -> p t e", t=TOKS)
            chain(ve.tensor_copy(rank[0][:, :, 0:EXPERTS], ranks))

            def gates():
                ve.wait_ge(router_exp, 1)
                chain(ve.tensor_scalar(rs["e1"][:, :], rs["e"][:, :], 1.0, None, ALU.add))
                chain(ve.reciprocal(rs["g1"][:, :], rs["e1"][:, :]))
                chain(ve.tensor_tensor(rs["g2"][:, :], rs["g1"][:, :], rs["e"][:, :], ALU.mult))
                ve.tensor_tensor(rt["w1"][:, :, :], rt["first"][:, :, :], wide(rs["g1"]), ALU.mult)
                chain(ve.tensor_tensor(rt["w2"][:, :, :], rt["second"][:, :, :], wide(rs["g2"]), ALU.mult))
                chain(ve.tensor_tensor(share[:, :, 0:EXPERTS], rt["w1"][:, :, :], rt["w2"][:, :, :], ALU.add))
                ve.tensor_scalar(rank[1][:, :, 0:EXPERTS], ranks, -float(P), None, ALU.add)
                chain(ve.tensor_reduce(most[:, :], bank[6][:, TOKS * EXPERTS:(TOKS + 1) * EXPERTS], AX.X, ALU.max))
                chain(ve.tensor_scalar(over[:, :], most[:, :], float(P), None, ALU.is_gt))
                ve.tensor_copy(over_i[:, :], over[:, :]).then_inc(flag_ready, 1)

            def experts(unit0, tile0, fb0, tok0, e0, ranks):
                def col(table, t, e):
                    return table[:, t, bass.ds(e, 1)] if not isinstance(e, int) else table[:, t, e:e + 1]

                def choose(e):
                    for t in range(TOKS):
                        ins = ve.tensor_scalar(pick[:, t, :], slot_no[:, :], col(ranks, t, e), col(mask, t, e),
                                               ALU.is_equal, ALU.mult)
                    ins.then_inc(pick_ready, 1)

                def gather_lo(e):
                    for g in range(2):
                        ve.wait_ge(gathered, (e + e0) * 4 + g + 3)
                        ve.tensor_copy(g_lo[:, 4 * g:4 * g + 4, :],
                                       bank[3 + g][:, :].rearrange("p (c t) -> p c t", c=4)).then_inc(g_lo_ready, 1)

                def add_out(e):
                    for g in range(4):
                        ve.wait_ge(scattered, (e + e0) * 4 + g + 1)
                        t, half = g % 2, g // 2
                        xs = x[:, t, half * 512:(half + 1) * 512]
                        ve.tensor_tensor(xs, xs, bank[(7, 2, 1, 7)[g]][:, :], ALU.add).then_inc(scatter_added, 1)

                def step0(e, place, add):
                    gather_lo(e)
                    for t in range(TOKS):
                        ins = ve.tensor_scalar(give[:, t, :], slot_no[:, :], col(ranks, t, e), col(share, t, e),
                                               ALU.is_equal, ALU.mult)
                    ins.then_inc(give_ready, 1)
                    choose(e + 1)
                    if add:
                        low(place, range(1, 4))
                        add_out(e - 1)
                        low(place, range(4, 8))
                    else:
                        low(place, range(AHEAD, 8))

                def steps(e, reg):
                    step = Place(unit0 + 8, tile0 + 2, e=reg)
                    if reg is None:
                        step = step.plus(e * EXPERT_UNITS, e * EXPERT_TILES)
                    low(step, range(0, AHEAD))
                    multiply(step.used(-1), e * STEPS + (fb0 + 1), 1, (1,), FB)
                    low(step, range(AHEAD, 9))
                    act_lo(e * STEPS + tok0, 1, (2,), FB // P)
                    low(step, range(9, 12))
                    multiply(step.used(7), e * STEPS + (fb0 + 2), 1, (1,), FB)
                    with ve.Fori(0, STEPS - 2) as i:
                        step = Place(step.unit + STEP_UNITS, step.tile + STEP_TILES, e=reg, fb=i)
                        low(step, range(0, AHEAD))
                        act_lo(e * STEPS + i + (tok0 + 1), 1, (2,), FB // P)
                        low(step, range(AHEAD, 12))
                        multiply(step.used(7), e * STEPS + i + (fb0 + 3), 1, (1,), FB)
                    tail = Place(step.unit + STEP_UNITS * (STEPS - 2), step.tile + STEP_TILES * (STEPS - 2), e=reg)
                    low(tail, range(2))
                    act_lo(e * STEPS + (tok0 + STEPS - 1), 1, (2,), FB // P)
                    low(tail, range(2, 4))
                    return tail.plus(4, 1)

                first = Place(unit0, tile0)
                choose(0)
                if e0:
                    low(first, range(AHEAD))
                else:
                    gates()
                step0(0, first, False)
                with ve.Fori(0, EXPERTS - 1) as e:
                    nxt = steps(e, e)
                    low(nxt, [0])
                    step0(e + 1, nxt, True)
                steps(EXPERTS - 1, None)
                add_out(EXPERTS - 1)
                ve.wait_ge(scatter_added, (e0 + EXPERTS) * 4)

            experts(MOE_UNIT, MOE_TILE, DENSE_STEPS, DENSE_STEPS * TOKS, 0, rank[0])
            ve.wait_ge(flag_ready, 1)
            some_over = ve.value_load(over_i[0:1, 0:1], min_val=0, max_val=1)
            with ve.If(some_over == 1):
                experts(MOE_UNIT + EXPERTS * EXPERT_UNITS, MOE_TILE + EXPERTS * EXPERT_TILES,
                        DENSE_STEPS + EXPERTS * STEPS, DENSE_STEPS * TOKS + EXPERTS * STEPS, EXPERTS, rank[1])
            ve.sem_inc(x_added, 1)
            norm(4)

        @block.tensor
        def _(pe):
            def product(out_ap, a_hi, a_lo, b_hi, b_lo, first, last):
                pe.matmul(out_ap, a_hi, b_hi, start=first, stop=False)
                pe.matmul(out_ap, a_hi, b_lo, start=False, stop=False)
                return pe.matmul(out_ap, a_lo, b_hi, start=False, stop=last)

            def columns(place, i0, a_hi, a_lo, toks, banks, cols, turned_now=None):
                for u in range(TILE_UNITS):
                    if turned_now is not None and u % 2 == 0:
                        pe.wait_ge(tT_lo, 4 * turned_now + u + 2)
                    pe.wait_ge(lo_ready, place.used(i0 + u))
                    r = place.ring(i0 + u)
                    for c in range(2):
                        k = 2 * u + c
                        for t in range(toks):
                            tk = slice(t * P, (t + 1) * P)
                            w = slice(c * 512, c * 512 + cols)
                            ins = product(bank[banks[t]][:, 0:cols], a_hi[:, k, tk], a_lo[:, k, tk],
                                          w_hi[r][:, w], w_lo[r][:, w], k == 0, k == KC - 1)
                    ins.then_inc(unit_used, 1)

            def down(place, i0, toks, banks, chunks, first, last):
                for c in range(chunks):
                    pe.wait_ge(lo_ready, place.used(i0 + c))
                    r = place.ring(i0 + c)
                    for t in range(toks):
                        tk = slice(t * P, (t + 1) * P)
                        for half in range(2):
                            w = slice(half * 512, (half + 1) * 512)
                            ins = product(bank[banks[2 * t + half]][:, :], aT_hi[:, c, tk], aT_lo[:, c, tk],
                                          w_hi[r][:, w], w_lo[r][:, w], first and c == 0, last and c == chunks - 1)
                    ins.then_inc(unit_used, 1)

            def turn(k, first_bank, waits):
                for g in range(4):
                    pe.wait_ge(*waits[g])
                    t, c0 = g % 2, 4 * (g // 2)
                    for c in range(4):
                        ins = pe.transpose(bank[first_bank + g][:, c * P:(c + 1) * P], h[:, t, (c0 + c) * P:(c0 + c + 1) * P],
                                           ident[:, :])
                    ins.then_inc(turned, 1)

            def turn_norm(k, norm, first_bank):
                turn(k, first_bank, [(h_ready, parts_before(norm) + g + 1) for g in range(4)])

            def attention(l):
                place = Place(UNIT0[l], TILE0[l])
                turn_norm(3 * l, 2 * l, 4)
                columns(place, 0, hT_hi, hT_lo, TOKS, (0, 1), REST, 3 * l)
                columns(place, 4, hT_hi, hT_lo, TOKS, (2, 3), FB)
                pe.wait_ge(lat_ready, l + 1)
                pe.wait_ge(v_copied, 2 * l + 1)
                for c in range(2):
                    for t in range(TOKS):
                        ins = pe.transpose(bank[0][:, c * S + t * P:c * S + (t + 1) * P], latent[:, t, c * P:(c + 1) * P], ident[:, :])
                ins.then_inc(lat_turned, 1)
                for t in range(TOKS):
                    ins = pe.transpose(bank[1][:, t * P:(t + 1) * P], latent[:, t, Q_RANK:], ident[:, :])
                ins.then_inc(lat_turned, 1)
                columns(place, 8, hT_hi, hT_lo, TOKS, (4, 5), FB)
                pe.wait_ge(small_loaded, 80 * (l + 1))
                pe.wait_ge(cqT_ready, l + 1)
                pe.wait_ge(ckT_ready, l + 1)
                for t in range(TOKS):
                    for c in range(2):
                        ins = pe.matmul(bank[t][:, 0:ML_Q_COLS], cqT[:, c, t * P:(t + 1) * P], w_uq[:, c, :],
                                        start=(c == 0), stop=(c == 1))
                ins.then_inc(ml_proj, 1)
                columns(place, 12, hT_hi, hT_lo, TOKS, (6, 7), FB)
                for t in range(TOKS):
                    pe.wait_ge(rotated, 2 * l + t + 1)
                    for i in range(2):
                        ins = pe.matmul(bank[2 + 2 * t + i][:, 0:2 * KV_HEAD], ckT[:, t * P:(t + 1) * P],
                                        w_ukv[:, 2 * i * KV_HEAD:2 * (i + 1) * KV_HEAD], start=True, stop=True)
                    ins.then_inc(ml_proj, 1)
                pe.wait_ge(ml_qk, 2 * l + 1)
                for g in range(4):
                    src = (q_rot, k_rot)[g // 2]
                    if g == 2:
                        pe.wait_ge(v_copied, 2 * l + 2)
                    for hh in range(2):
                        hd = 2 * (g % 2) + hh
                        for t in range(TOKS):
                            ins = pe.transpose(bank[(0, 1, 6, 7)[g]][:, hh * S + t * P:hh * S + (t + 1) * P],
                                               src[:, t, hd * P:(hd + 1) * P], ident[:, :])
                    ins.then_inc(da_turned, 1)
                pe.wait_ge(ml_qk, 2 * l + 2)
                for kind, src in enumerate((q_ml, k_ml)):
                    for g in range(2):
                        for hh in range(2):
                            for t in range(TOKS):
                                ins = pe.transpose(bank[2 + 2 * kind + g][0:ML_QK, hh * S + t * P:hh * S + (t + 1) * P],
                                                   src[:, t, 2 * g + hh, :], ident[:, :])
                        ins.then_inc(ml_turned, 1)
                base = JOBS * l
                pe.wait_ge(da_qT, 2 * l + 2)
                pe.wait_ge(da_kT, 2 * l + 2)
                for i in range(JOBS + 3):
                    j = i
                    if j < JOBS:
                        if j >= 2:
                            pe.wait_ge(probs_ready, base + j - 1)
                        if j == 1:
                            pe.wait_ge(ml_qT, 2 * l + 2)
                            pe.wait_ge(ml_kT, 2 * l + 2)
                        t = j % 2
                        for c in range(2):
                            if j < DA_JOBS:
                                part = slice(c * DA_DIM, (c + 1) * DA_DIM)
                                q, k = qT_da[part, j // 2, t * P:(t + 1) * P], kT_da[part, j // 2, :]
                            else:
                                hd = 2 * ((j - DA_JOBS) // 2) + c
                                q, k = qT_ml[0:ML_QK, hd, t * P:(t + 1) * P], kT_ml[0:ML_QK, hd, :]
                            ins = pe.matmul(scores[j % 2][:, c, :], q, k, start=True, stop=True)
                        ins.then_inc(scored, 1)
                    j = i - 2
                    if 0 <= j < JOBS:
                        pe.wait_ge(mix_ready, base + j + 1)
                        if j >= 2:
                            pe.wait_ge(probsT_ready, base + j - 1)
                        for c in range(1 if j < DA_JOBS else 2):
                            for kc in range(TOKS):
                                src = mixed[j % 2][:, kc * P:(kc + 1) * P] if j < DA_JOBS else probs[j % 2][:, c, kc * P:(kc + 1) * P]
                                ins = pe.transpose(bank[4 + j % 2][:, c * S + kc * P:c * S + (kc + 1) * P], src, ident[:, :])
                        ins.then_inc(probs_turned, 1)
                    j = i - 3
                    if 0 <= j < JOBS:
                        pe.wait_ge(probsT_ready, base + j + 1)
                        if j >= 2:
                            pe.wait_ge(o_ready, base + j - 1)
                        for c in range(1 if j < DA_JOBS else 2):
                            for kc in range(TOKS):
                                if j < DA_JOBS:
                                    v = v_da[:, kc, (j // 2) * DA_V:(j // 2 + 1) * DA_V]
                                else:
                                    hd = 2 * ((j - DA_JOBS) // 2) + c
                                    v = v_ml[:, kc, hd * ML_V:(hd + 1) * ML_V]
                                ins = pe.matmul(bank[6 + j % 2][:, c * P:(c + 1) * P], probsT[j % 2][:, c * S + kc * P:c * S + (kc + 1) * P],
                                                v, start=(kc == 0), stop=(kc == 1))
                        ins.then_inc(pv_ready, 1)
                parts = parts_before(2 * l) + NORM_PARTS
                turn(3 * l + 1, 0, [(h_ready, parts + 1), (h_ready, parts + 2), (o_ready, base + JOBS - 1), (o_ready, base + JOBS)])
                for n in range(2):
                    columns(place, 16 + 4 * n, hT_hi, hT_lo, TOKS, (4 + 2 * n, 5 + 2 * n), FB, None if n else 3 * l + 1)
                turn_norm(3 * l + 2, 2 * l + 1, 0)

            def turn_act(count, toks, banks, chunks):
                pe.wait_ge(act_ready, count)
                for t in range(toks):
                    a = act[:, t, 0:chunks * P].rearrange("p (m c) -> p c m", c=chunks)
                    for c in range(chunks):
                        ins = pe.transpose(bank[banks[t]][:, c * P:(c + 1) * P], a[:, c, :], ident[:, :])
                    ins.then_inc(act_turned, 1)

            pe.wait_ge(consts, CONSTS)
            attention(0)

            Y = (4, 5, 6, 7)

            def dense_step(place, count, cols, first, turned_now=None):
                if not (isinstance(count, int) and count == 1):
                    pe.wait_ge(silu_ready, count - 1)
                columns(place, 0, hT_hi, hT_lo, TOKS, (0, 1), cols, turned_now)
                if not (isinstance(count, int) and count == 1):
                    pe.wait_ge(aT_lo_ready, (count - 1) * TOKS)
                columns(place, 4, hT_hi, hT_lo, TOKS, (2, 3), cols)
                if first is not None:
                    down(place, 8, TOKS, Y, FB // P, first, False)
                turn_act(count, TOKS, (2, 3), cols // P)

            dense_step(Place(DENSE_UNIT, DENSE_TILE), 1, FB, None, 2)
            dense_step(Place(DENSE_UNIT + 8, DENSE_TILE + 2), 2, FB, True)
            with pe.Fori(0, DENSE_STEPS - 3) as i:
                dense_step(Place(DENSE_UNIT + 8 + STEP_UNITS, DENSE_TILE + 2 + STEP_TILES, fb=i), i + 3, FB, False)
            last = Place(DENSE_UNIT + 8 + STEP_UNITS * (DENSE_STEPS - 2), DENSE_TILE + 2 + STEP_TILES * (DENSE_STEPS - 2))
            dense_step(last, DENSE_STEPS, DENSE_LAST, False)
            pe.wait_ge(aT_lo_ready, DENSE_STEPS * TOKS)
            down(last, 12, TOKS, Y, DENSE_LAST // P, False, True)
            attention(1)

            pe.wait_ge(r_split, 2)
            logits = bank[5][:, 0:TOKS * 2 * EXPERTS].rearrange("p (t n) -> p t n", t=TOKS)
            for k in range(KC):
                for t in range(TOKS):
                    if k % 4 == 0:
                        pe.wait_ge(tT_lo, 4 * 5 + k // 2 + t + 1)
                    tk = slice(t * P, (t + 1) * P)
                    pe.matmul(logits[:, t, :], hT_hi[:, k, tk], r_halves[:, k, :, :].rearrange("p i e -> p (i e)"),
                              start=(k == 0 and t == 0), stop=False, skip_group_check=True)
                    ins = pe.matmul(logits[:, t, 0:EXPERTS], hT_lo[:, k, tk], r_halves[:, k, 0, :],
                                    start=False, stop=(k == KC - 1), skip_group_check=True)
            ins.then_inc(routed_ps, 1)
            pe.wait_ge(mask_ready, 1)
            E = EXPERTS
            m = [mask[:, t, 0:E] for t in range(TOKS)]
            pe.matmul(bank[6][:, 0:E], before[:, :], m[0], start=True, stop=True)
            pe.matmul(bank[6][:, E:2 * E], ones[:, :], m[0], start=True, stop=False)
            pe.matmul(bank[6][:, E:2 * E], before[:, :], m[1], start=False, stop=True)
            pe.matmul(bank[6][:, 2 * E:3 * E], ones[:, :], m[0], start=True, stop=False)
            pe.matmul(bank[6][:, 2 * E:3 * E], ones[:, :], m[1], start=False, stop=True).then_inc(ranked_ps, 1)

            def experts(unit0, tile0, fb0, tok0, e0):
                def gather(e, lo):
                    src = h_lo if lo else h_hi
                    if isinstance(e, int) and e0 == 0:
                        pe.wait_ge(*((h_split, TOKS) if lo else (h_hi_ready, TOKS)))
                    for g in range(2):
                        if lo:
                            pe.wait_ge(g_hi_ready, (e + e0) * 2 + g + 1)
                        for c in range(4):
                            k = 4 * g + c
                            for t in range(TOKS):
                                ins = pe.matmul(bank[3 + g][:, c * P:(c + 1) * P], src[:, t, k * P:(k + 1) * P], pick[:, t, :],
                                                start=(t == 0), stop=(t == TOKS - 1))
                        ins.then_inc(gathered, 1)

                def step0(e, place, after):
                    pe.wait_ge(g_lo_ready, (e + e0) * 2 + 2)
                    columns(place, 0, g_hi, g_lo, 1, (0,), FB)
                    pe.wait_ge(give_ready, e + (e0 + 1))
                    if after:
                        pe.wait_ge(scatter_added, (e + e0) * 4)
                    for t in range(TOKS):
                        ins = pe.transpose(bank[2][:, t * P:(t + 1) * P], give[:, t, :], ident[:, :])
                    ins.then_inc(give_turned, 1)
                    columns(place, 4, g_hi, g_lo, 1, (1,), FB)

                def steps(e, reg):
                    step = Place(unit0 + 8, tile0 + 2, e=reg)
                    if reg is None:
                        step = step.plus(e * EXPERT_UNITS, e * EXPERT_TILES)
                    pe.wait_ge(silu_ready, e * STEPS + (fb0 + 1))
                    columns(step, 0, g_hi, g_lo, 1, (0,), FB)
                    pe.wait_ge(giveT_ready, e + (e0 + 1))
                    turn_act(e * STEPS + (fb0 + 1), 1, (2,), FB // P)
                    columns(step, 4, g_hi, g_lo, 1, (1,), FB)
                    pe.wait_ge(aT_lo_ready, e * STEPS + (tok0 + 1))
                    down(step, 8, 1, (5, 6), FB // P, True, False)
                    turn_act(e * STEPS + (fb0 + 2), 1, (2,), FB // P)
                    with pe.Fori(0, STEPS - 2) as i:
                        step = Place(step.unit + STEP_UNITS, step.tile + STEP_TILES, e=reg, fb=i)
                        pe.wait_ge(silu_ready, e * STEPS + i + (fb0 + 2))
                        columns(step, 0, g_hi, g_lo, 1, (0,), FB)
                        columns(step, 4, g_hi, g_lo, 1, (1,), FB)
                        pe.wait_ge(aT_lo_ready, e * STEPS + i + (tok0 + 2))
                        down(step, 8, 1, (5, 6), FB // P, False, False)
                        turn_act(e * STEPS + i + (fb0 + 3), 1, (2,), FB // P)
                    return Place(step.unit + STEP_UNITS * (STEPS - 2), step.tile + STEP_TILES * (STEPS - 2), e=reg)

                def finish(e, place):
                    pe.wait_ge(aT_lo_ready, e * STEPS + (tok0 + STEPS))
                    down(place, 0, 1, (5, 6), FB // P, False, True)

                def scatter(e):
                    for g in range(4):
                        t, half = g % 2, g // 2
                        pe.wait_ge(y_ready, (e + e0) * 2 + half + 1)
                        if g == 3:
                            pe.wait_ge(scatter_added, (e + e0) * 4 + 1)
                        pe.matmul(bank[(7, 2, 1, 7)[g]][:, :], giveT[:, t, :], y_sb[:, half * 512:(half + 1) * 512],
                                  start=True, stop=True).then_inc(scattered, 1)

                pe.wait_ge(pick_ready, e0 + (e0 // EXPERTS) + 1)
                gather(0, False)
                gather(0, True)
                step0(0, Place(unit0, tile0), e0 > 0)
                with pe.Fori(0, EXPERTS - 1) as e:
                    tail = steps(e, e)
                    pe.wait_ge(pick_ready, e + (e0 + e0 // EXPERTS + 2))
                    gather(e + 1, False)
                    finish(e, tail)
                    gather(e + 1, True)
                    scatter(e)
                    step0(e + 1, tail.plus(4, 1), True)
                tail = steps(EXPERTS - 1, None)
                finish(EXPERTS - 1, tail)
                scatter(EXPERTS - 1)

            experts(MOE_UNIT, MOE_TILE, DENSE_STEPS, DENSE_STEPS * TOKS, 0)
            pe.wait_ge(flag_ready, 1)
            some_over = pe.value_load(over_i[0:1, 0:1], min_val=0, max_val=1)
            with pe.If(some_over == 1):
                experts(MOE_UNIT + EXPERTS * EXPERT_UNITS, MOE_TILE + EXPERTS * EXPERT_TILES,
                        DENSE_STEPS + EXPERTS * STEPS, DENSE_STEPS * TOKS + EXPERTS * STEPS, EXPERTS)


_INS = ["x", "positions", "w_in", "w_out", "norm_mix", "norm_ffn", "da_lambda_q1", "da_lambda_k1", "da_lambda_q2",
        "da_lambda_k2", "da_subln", "mla_q_norm", "mla_w_uq", "mla_kv_norm", "mla_w_ukv", "ffn_w_gate", "ffn_w_up",
        "ffn_w_down", "moe_router", "moe_w_gate", "moe_w_up", "moe_w_down", "norm_final"]


def kernel(**inputs):
    import concourse.bacc as _bacc
    from concourse.bass_utils import run_bass_kernel_spmd as _run

    nc = _bacc.Bacc("TRN2", target_bir_lowering=False, num_devices=1, dynamic_dma_scratch_size=1024)
    arrays, args = {}, []
    for name in _INS + ["rope_freqs"]:
        a = rope_freqs() if name == "rope_freqs" else np.ascontiguousarray(inputs[name])
        arrays[f"in_{name}"] = a
        args.append(nc.dram_tensor(f"in_{name}", a.shape, mybir.dt.from_np(a.dtype), kind="ExternalInput").ap())
    out = nc.dram_tensor("out_x", (1, S, D), mybir.dt.float32, kind="ExternalOutput").ap()
    encoder(nc, *args, out)
    r = _run(nc, [arrays], core_ids=[0])
    return r.results[0]["out_x"]
```

```python
from contextlib import ExitStack

import numpy as np

import concourse.bass as bass
from concourse import mybir

P = 128
D = 1024
S = 256
TOKS = S // P
KC = D // P
DEPTH = 2
NORM_EPS, SUBLN_EPS = 1e-6, 1e-5

DA_HEADS, DA_DIM, DA_V = 4, 64, 128
DA_COLS = DA_HEADS * 2 * DA_DIM
HALF = DA_DIM // 2
ML_HEADS, NOPE, ROPE, ML_V = 4, 64, 32, 128
ML_QK = NOPE + ROPE
Q_RANK, KV_RANK = 256, 128
ML_Q_COLS = ML_HEADS * ML_QK
KV_HEAD = NOPE + ML_V
KV_COLS = ML_HEADS * KV_HEAD
REST = Q_RANK + KV_RANK + ROPE
FREQS = HALF + ROPE // 2

FF_DENSE, FF_EXPERT = 2816, 3584
EXPERTS = 8
FB = 512
DENSE_STEPS = -(-FF_DENSE // FB)
DENSE_LAST = FF_DENSE - (DENSE_STEPS - 1) * FB
STEPS = FF_EXPERT // FB

UNIT = 1024
TILE_UNITS = 4
SLOTS = 3
MOE_SLOTS = 6
RING = 6
AHEAD = 5
LAYER_UNITS = (4 + 2) * TILE_UNITS
DENSE_UNITS = 2 * TILE_UNITS * DENSE_STEPS + TILE_UNITS * (DENSE_STEPS - 1) + DENSE_LAST // P
DENSE_TILES = 3 * DENSE_STEPS
STEP_UNITS, STEP_TILES = 3 * TILE_UNITS, 3
EXPERT_UNITS, EXPERT_TILES = STEPS * STEP_UNITS, STEPS * STEP_TILES
LAYER_TILES = 6
UNIT0 = (0, LAYER_UNITS + DENSE_UNITS)
TILE0 = (0, LAYER_TILES + DENSE_TILES)
MOE_UNIT, MOE_TILE = UNIT0[1] + LAYER_UNITS, TILE0[1] + LAYER_TILES
DENSE_UNIT, DENSE_TILE = LAYER_UNITS, LAYER_TILES
SHORT_TILE = DENSE_TILE + DENSE_TILES - 1
SHORT_BY = TILE_UNITS - DENSE_LAST // P
PAIR = 2
PAIR_STEPS = (STEPS - 3) // PAIR
assert STEP_UNITS % RING == 0 and STEP_TILES % SLOTS == 0 and PAIR * STEP_TILES % MOE_SLOTS == 0
assert EXPERTS % PAIR == 0 and PAIR * EXPERT_TILES % MOE_SLOTS == 0 and (STEPS - 3) % PAIR == 0

JOBS = 12
DA_JOBS = DA_HEADS * TOKS

TWO_PI = 2 * np.pi
_C1 = float(np.float32(np.round(TWO_PI * 2**7) / 2**7))
_C2 = float(np.float32(np.round((TWO_PI - _C1) * 2**19) / 2**19))
_C3 = float(np.float32(TWO_PI - _C1 - _C2))
PI_DOWN = 3.1415925


NORM_PARTS, HEAD_PARTS = 4, 2
LAYER_PARTS = 2 * NORM_PARTS + HEAD_PARTS
IN_TILES = ((3 * DA_COLS, REST), (0, DA_COLS), (DA_COLS, DA_COLS), (2 * DA_COLS, DA_COLS))


def parts_before(norm):
    return norm // 2 * LAYER_PARTS + norm % 2 * (NORM_PARTS + HEAD_PARTS)


def lambda_init(layer):
    return 0.8 - 0.6 * float(np.exp(-0.3 * layer))


def rope_freqs():
    f = [1.0 / (np.float32(10000.0) ** (np.arange(0, d, 2, dtype=np.float32) / np.float32(d))) for d in (DA_DIM, ROPE)]
    return np.concatenate(f).astype(np.float32)[None, :]


class Place:
    group, slots, tile0, earlier = 1, SLOTS, 0, 0

    def __init__(self, unit, tile, e=None, fb=None):
        self.unit, self.tile, self.e, self.fb = unit, tile, e, fb

    def at(self, unit, tile, e=None, fb=None):
        return Place(unit, tile, e, fb)

    def plus(self, units, tiles):
        return self.at(self.unit + units, self.tile + tiles, self.e, self.fb)

    def turn(self, fb):
        return self.at(self.unit, self.tile, self.e, fb)

    def _dyn(self, n, per_expert, per_step):
        for reg, per in ((self.e, per_expert), (self.fb, per_step)):
            if reg is not None:
                n = reg * (per * self.group) + n
        return n

    def used(self, i):
        return self._dyn(self.unit + i + 1, EXPERT_UNITS, STEP_UNITS)

    def ring(self, i):
        return (self.unit + i) % RING

    def slot(self, j):
        return (self.tile + j - self.tile0) % self.slots

    def loaded(self, j):
        loads = (self.tile + j - self.tile0) // self.slots + 1 + (self.earlier if self.slot(j) < SLOTS else 0)
        n = 16 * loads
        for reg, tiles in ((self.e, EXPERT_TILES), (self.fb, STEP_TILES)):
            if reg is not None:
                n = reg * (16 * self.group * tiles // self.slots) + n
        return n

    def freed(self, j):
        t = self.tile + j
        if t >= self.tile0 + self.slots:
            t -= self.slots
        elif t >= SLOTS and t < self.tile0 + SLOTS:
            t -= SLOTS
        else:
            return None
        short = SHORT_BY if t >= SHORT_TILE else 0
        return self._dyn(TILE_UNITS * (t + 1) - short, EXPERT_UNITS, STEP_UNITS)


class ExpertPlace(Place):
    group, slots, tile0, earlier = PAIR, MOE_SLOTS, MOE_TILE, MOE_TILE // SLOTS

    def at(self, unit, tile, e=None, fb=None):
        return ExpertPlace(unit, tile, e, fb)


def encoder(nc, x_in, positions, w_in, w_out, norm_mix, norm_ffn, lq1, lk1, lq2, lk2, da_subln, mla_q_norm, mla_w_uq,
            mla_kv_norm, mla_w_ukv, ffn_gate, ffn_up, ffn_down, router, moe_gate, moe_up, moe_down, norm_final,
            freqs, out):
    F32, F32R, I32 = mybir.dt.float32, mybir.dt.float32r, mybir.dt.int32
    ALU, ACT, AX = mybir.AluOpType, mybir.ActivationFunctionType, mybir.AxisListType

    with ExitStack() as ctx:
        def sb(name, shape, dt=F32):
            return ctx.enter_context(nc.sbuf_tensor(name, shape, dt))

        def sem(name):
            return ctx.enter_context(nc.semaphore(name))

        TILE = TILE_UNITS * UNIT
        raw = [sb(f"raw{i}", [P, TILE]) for i in range(SLOTS)]
        w_hi = [sb(f"w_hi{i}", [P, UNIT], F32R) for i in range(RING)]
        w_lo = [sb(f"w_lo{i}", [P, UNIT], F32R) for i in range(RING)]

        x = sb("x", [P, TOKS, D])
        t_hi = sb("t_hi", [P, KC * S], F32R)
        t_lo = sb("t_lo", [P, KC * S], F32R)
        hT_hi = t_hi[:, :].rearrange("p (c t) -> p c t", c=KC)
        hT_lo = t_lo[:, :].rearrange("p (c t) -> p c t", c=KC)
        h_hi = t_hi[:, :].rearrange("p (t d) -> p t d", t=TOKS)
        h_lo = t_lo[:, :].rearrange("p (t d) -> p t d", t=TOKS)
        g_hi = sb("g_hi", [P, KC, P], F32R)
        g_lo = sb("g_lo", [P, KC, P], F32R)
        y_hi = sb("y_hi", [P, D], F32R)
        y_lo = sb("y_lo", [P, D], F32R)
        aT_hi, aT_lo = (a[:, :].rearrange("p (c t) -> p c t", c=FB // P) for a in (y_hi, y_lo))
        gain = [sb(f"gain{i}", [P, D]) for i in range(2)]

        ARENA = 15232
        arena = sb("arena", [P, ARENA])
        used_cols = [0]

        def cut(cols):
            a = used_cols[0]
            used_cols[0] = a + cols
            assert used_cols[0] <= ARENA
            return arena[:, a:a + cols]

        def view(ap, pattern, **sizes):
            return ap.rearrange(pattern, **sizes)

        q_rot = view(cut(TOKS * DA_COLS), "p (t c) -> p t c", t=TOKS)
        k_rot = view(cut(TOKS * DA_COLS), "p (t c) -> p t c", t=TOKS)
        v_da = view(cut(TOKS * DA_COLS), "p (t c) -> p t c", t=TOKS)
        rest_raw = cut(TOKS * REST)
        rest = view(rest_raw, "p (t c) -> p t c", t=TOKS)
        qT_da = view(cut(DA_HEADS * S), "p (h t) -> p h t", h=DA_HEADS)
        kT_da = view(cut(DA_HEADS * S), "p (h t) -> p h t", h=DA_HEADS)
        qT_ml = view(cut(ML_HEADS * S), "p (h t) -> p h t", h=ML_HEADS)
        kT_ml = view(cut(ML_HEADS * S), "p (h t) -> p h t", h=ML_HEADS)
        latent_raw = cut(TOKS * (Q_RANK + KV_RANK))
        latent = view(latent_raw, "p (t c) -> p t c", t=TOKS)
        v_ml = view(cut(TOKS * ML_HEADS * ML_V), "p (t c) -> p t c", t=TOKS)
        cqT = view(cut(2 * S), "p (c t) -> p c t", c=2)
        ckT = cut(S)
        probs_raw = [cut(2 * S) for _ in range(2)]
        probs = [view(a, "p (c k) -> p c k", c=2) for a in probs_raw]
        mixed = [cut(S) for _ in range(2)]
        probsT = [cut(2 * S) for _ in range(2)]
        k_pe = view(cut(TOKS * ROPE), "p (t c) -> p t c", t=TOKS)
        h = view(cut(TOKS * D), "p (t d) -> p t d", t=TOKS)
        q_ml = view(rest_raw[:, 0:TOKS * ML_Q_COLS], "p (t h c) -> p t h c", t=TOKS, c=ML_QK)
        k_ml = view(latent_raw[:, 0:TOKS * ML_Q_COLS], "p (t h c) -> p t h c", t=TOKS, c=ML_QK)
        o_squares = view(arena[:, 0:DA_JOBS * DA_V], "p (j c) -> p j c", j=DA_JOBS)
        MOE_AT = 2 * TILE
        silu = {TOKS: view(arena[:, 0:TOKS * FB], "p (t c) -> p t c", t=TOKS), 1: arena[:, MOE_AT:MOE_AT + FB].unsqueeze(1)}
        act = {TOKS: view(arena[:, 1024:1024 + TOKS * FB], "p (t c) -> p t c", t=TOKS),
               1: arena[:, MOE_AT + FB:MOE_AT + 2 * FB].unsqueeze(1)}
        MOE_END = MOE_AT + 2 * FB
        assert MOE_END + TILE <= ARENA
        raw += [arena[:, a:a + TILE] for a in (0, TILE, MOE_END)]
        junk = sb("junk", [P, Q_RANK])

        w_uq = sb("w_uq", [P, 2, ML_Q_COLS])
        w_ukv = sb("w_ukv", [P, KV_COLS])
        latent_gain = sb("latent_gain", [P, Q_RANK + KV_RANK])
        sub_gain = sb("sub_gain", [P, DA_V])
        sub_scaled = sb("sub_scaled", [P, DA_V])
        lam_vecs = view(arena[:, 0:4 * DEPTH * DA_DIM], "p (i l c) -> p i l c", i=4, l=DEPTH)
        lam_prod = view(arena[:, 512:512 + 2 * DEPTH * DA_DIM], "p (i l c) -> p i l c", i=2, l=DEPTH)
        angle = view(arena[:, 768:768 + TOKS * FREQS], "p (t c) -> p t c", t=TOKS)
        turns_f = view(arena[:, 896:896 + TOKS * FREQS], "p (t c) -> p t c", t=TOKS)
        lam_dots = sb("lam_dots", [P, 2, DEPTH])
        lam_exps = sb("lam_exps", [P, 2, DEPTH])
        neg_lam = sb("neg_lam", [P, DEPTH])
        pos_i = sb("pos_i", [P, TOKS], I32)
        pos_f = sb("pos_f", [P, TOKS])
        freq = sb("freq", [P, FREQS])
        turns_i = sb("turns_i", [P, TOKS, FREQS], I32)
        sines = sb("sines", [P, 2, TOKS, FREQS])
        cos_t = sb("cos_t", [P, TOKS, DA_DIM + ROPE])
        sin_t = sb("sin_t", [P, TOKS, DA_DIM + ROPE])
        eps_t = sb("eps_t", [P, 2])
        mean_sq = sb("mean_sq", [P, TOKS])
        norm_sd = sb("norm_sd", [P, TOKS])
        norm_r = sb("norm_r", [P, TOKS])
        lat_sq = sb("lat_sq", [P, TOKS, 2])
        lat_sd = sb("lat_sd", [P, TOKS, 2])
        lat_r = sb("lat_r", [P, TOKS, 2])
        o_sq = sb("o_sq", [P, TOKS, DA_HEADS])
        o_sd = sb("o_sd", [P, TOKS, DA_HEADS])
        o_r = sb("o_r", [P, TOKS, DA_HEADS])
        neg_max = sb("neg_max", [P, JOBS, 2])
        row_sum = sb("row_sum", [P, JOBS, 2])
        row_inv = sb("row_inv", [P, JOBS, 2])
        mix_coef = sb("mix_coef", [P, JOBS])
        ident = sb("ident", [P, P])
        before = sb("before", [P, P])
        ones = sb("ones", [P, P])
        slot_no = sb("slot_no", [P, P])
        expert_no = sb("expert_no", [P, TOKS, EXPERTS])
        r_w = sb("r_w", [P, KC, EXPERTS])
        r_halves = sb("r_halves", [P, KC, 2, EXPERTS], F32R)
        rt = {n: sb(f"r_{n}", [P, TOKS, EXPERTS]) for n in
              ("logits", "eq", "cand", "first", "logits2", "eq2", "cand2", "second", "w1", "w2")}
        rs = {n: sb(f"r_{n}", [P, TOKS]) for n in ("m1", "i1", "m2", "i2", "d", "e", "e1", "g1", "g2")}
        mask = sb("mask", [P, TOKS, EXPERTS])
        share = sb("share", [P, TOKS, EXPERTS])
        rank = [sb(f"rank{i}", [P, TOKS, EXPERTS]) for i in range(2)]
        most = sb("most", [P, 1])
        over = sb("over", [P, 1])
        over_i = sb("over_i", [P, 1], I32)
        pick = sb("pick", [P, TOKS, P], F32R)
        pickT = sb("pickT", [P, TOKS, P], F32R)
        slot_gate = sb("slot_gate", [P, 1])

        psum = ctx.enter_context(nc.psum_tensor("psum", [P, 8, 512], F32))
        bank = [psum[:, i, :] for i in range(8)]
        scores = [psum[:, 2 * i:2 * i + 2, 0:S] for i in range(2)]

        loaded = [sem(f"weights_loaded{i}") for i in range(MOE_SLOTS)]
        hi_ready, lo_ready, unit_used = sem("hi_ready"), sem("lo_ready"), sem("unit_used")
        x_loaded = [sem(f"x_loaded{t}") for t in range(TOKS)]
        rope_in, lam_in = sem("rope_in"), sem("lam_in")
        gain_loaded = [sem(f"gain_loaded{i}") for i in range(2)]
        small_loaded, router_loaded = sem("small_loaded"), sem("router_loaded")
        out_stored = sem("out_stored")
        consts = sem("consts")
        iotas = sem("iotas")
        sq_ready = sem("sq_ready")
        sd_ready = sem("sd_ready")
        h_ready = sem("h_ready")
        turned, tT_hi, tT_lo = sem("turned"), sem("tT_hi"), sem("tT_lo")
        rotated = sem("rotated")
        v_copied = sem("v_copied")
        da_turned, da_qT, da_kT = sem("da_turned"), sem("da_qT"), sem("da_kT")
        lat_sd_ready, lat_ready = sem("lat_sd_ready"), sem("lat_ready")
        lat_turned, cqT_ready, ckT_ready = sem("lat_turned"), sem("cqT_ready"), sem("ckT_ready")
        ml_proj = sem("ml_proj")
        ml_nope, ml_qk = sem("ml_nope"), sem("ml_qk")
        ml_turned, ml_qT, ml_kT = sem("ml_turned"), sem("ml_qT"), sem("ml_kT")
        scored, max_ready, probs_ready, mix_ready = sem("scored"), sem("max_ready"), sem("probs_ready"), sem("mix_ready")
        probs_turned, probsT_ready, pv_ready = sem("probs_turned"), sem("probsT_ready"), sem("pv_ready")
        o_ready = sem("o_ready")
        o_sd_ready = sem("o_sd_ready")
        dense_summed = sem("dense_summed")
        x_added = sem("x_added")
        angles, sines_ready = sem("angles"), sem("sines_ready")
        dots, lam_exp = sem("dots"), sem("lam_exp")
        vstep, astep = sem("vstep"), sem("astep")
        silu_ready, act_ready = sem("silu_ready"), sem("act_ready")
        act_turned, aT_hi_ready, aT_lo_ready = sem("act_turned"), sem("aT_hi_ready"), sem("aT_lo_ready")
        r_split, routed_ps, router_exp, router_d = sem("r_split"), sem("routed_ps"), sem("router_exp"), sem("router_d")
        mask_ready, ranked_ps, flag_ready, h_hi_ready, h_split = (sem("mask_ready"), sem("ranked_ps"), sem("flag_ready"),
                                                                  sem("h_hi_ready"), sem("h_split"))
        pick_ready, gathered, g_ready = sem("pick_ready"), sem("gathered"), sem("g_ready")
        pick_turned, pickT_ready = sem("pick_turned"), sem("pickT_ready")
        y_hi_ready, y_lo_ready, scattered, scatter_added = (sem("y_hi_ready"), sem("y_lo_ready"), sem("scattered"),
                                                            sem("scatter_added"))

        GATHER_BANKS = (3, 4, 7, 1)
        SCATTER_BANKS = (3, 4, 7, 6)

        w_in_v = w_in.rearrange("l (c p) n -> l p c n", p=P)
        w_out_v = w_out.rearrange("l (c p) n -> l p c n", p=P)
        gate_v = ffn_gate.rearrange("o (c p) n -> o p c n", p=P)
        up_v = ffn_up.rearrange("o (c p) n -> o p c n", p=P)
        mgate_v = moe_gate.rearrange("o e (c p) n -> (o e) p c n", p=P)
        mup_v = moe_up.rearrange("o e (c p) n -> (o e) p c n", p=P)
        down_v = ffn_down[0, 0:(DENSE_STEPS - 1) * FB, :].rearrange("(b p c) n -> b p (c n)", p=P, c=FB // P)
        down_last_v = ffn_down[0, (DENSE_STEPS - 1) * FB:, :].rearrange("(p c) n -> p (c n)", p=P)
        mdown_v = moe_down.rearrange("o e (b p c) n -> (o e) b p (c n)", p=P, c=FB // P)
        x_v = x_in.rearrange("o (t p) d -> p (o t) d", p=P)
        out_v = out.rearrange("o (t p) d -> p (o t) d", p=P)
        gains_v = [norm_mix[0:1], norm_ffn[0:1], norm_mix[1:2], norm_ffn[1:2], norm_final.rearrange("(o d) -> o d", o=1)]

        def cols_of(step, moe):
            return DENSE_LAST if not moe and step == DENSE_STEPS - 1 else FB

        block = ctx.enter_context(nc.Block())

        @block.sync
        def _(sp):
            def load(place, j, src, cols=FB):
                freed = place.freed(j)
                if freed is not None:
                    sp.wait_ge(lo_ready, freed)
                if src.ndim == 3:
                    dst = raw[place.slot(j)][:, :].rearrange("p (c n) -> p c n", c=KC)[:, :, 0:cols]
                else:
                    dst = raw[place.slot(j)][:, 0:src.shape[-1]]
                sp.dma_start(dst, src).then_inc(loaded[place.slot(j)], 16)

            def load_gain(k):
                if k >= 2:
                    sp.wait_ge(h_ready, parts_before(k - 2) + NORM_PARTS)
                sp.dma_start(gain[k % 2][:, :], gains_v[k].to_broadcast([P, D])).then_inc(gain_loaded[k % 2], 16)

            def load_small(l):
                if l:
                    sp.wait_ge(ml_proj, 3)
                    sp.wait_ge(lat_ready, 1)
                sp.dma_start(w_uq[:, :, :], mla_w_uq[l].rearrange("(c p) n -> p c n", p=P)).then_inc(small_loaded, 16)
                sp.dma_start(w_ukv[:, :], mla_w_ukv[l]).then_inc(small_loaded, 16)
                sp.dma_start(latent_gain[:, 0:Q_RANK], mla_q_norm[l:l + 1].to_broadcast([P, Q_RANK])).then_inc(small_loaded, 16)
                sp.dma_start(latent_gain[:, Q_RANK:], mla_kv_norm[l:l + 1].to_broadcast([P, KV_RANK])).then_inc(small_loaded, 16)
                sp.dma_start(sub_gain[:, :], da_subln[l:l + 1].to_broadcast([P, DA_V])).then_inc(small_loaded, 16)

            def load_start():
                sp.dma_start(pos_i[:, :], positions.rearrange("o (t p) -> p (o t)", p=P),
                             allow_slow_non_contiguous=True).then_inc(rope_in, 16)
                sp.dma_start(freq[:, :], freqs.to_broadcast([P, FREQS])).then_inc(rope_in, 16)
                for i, vec in enumerate((lq1, lk1, lq2, lk2)):
                    sp.dma_start(lam_vecs[:, i, :, :], vec.unsqueeze(0).to_broadcast([P, DEPTH, DA_DIM])).then_inc(lam_in, 16)
                sp.dma_start(r_w[:, :, :], router[0].rearrange("(c p) n -> p c n", p=P)).then_inc(router_loaded, 16)

            def attention(l):
                place = Place(UNIT0[l], TILE0[l])
                for n, (at, cols) in enumerate(IN_TILES):
                    load(place, n, w_in_v[l, :, :, at:at + cols], cols)
                    if l == 0 and n == 0:
                        load_start()
                    if n == 1:
                        load_small(l)
                        load_gain(2 * l + 1)
                for n in range(2):
                    load(place, 4 + n, w_out_v[l, :, :, n * FB:(n + 1) * FB])

            for t in range(TOKS):
                sp.dma_start(x[:, t, :], x_v[:, t, :]).then_inc(x_loaded[t], 16)
            load_gain(0)
            attention(0)
            place = Place(DENSE_UNIT, DENSE_TILE)
            load(place, 0, gate_v[0, :, :, 0:FB])
            load(place, 1, up_v[0, :, :, 0:FB])
            with sp.Fori(0, DENSE_STEPS - 2) as i:
                step = Place(DENSE_UNIT + 8, DENSE_TILE + 2, fb=i)
                load(step, 0, gate_v[0, :, :, bass.ds((i + 1) * FB, FB)])
                load(step, 1, up_v[0, :, :, bass.ds((i + 1) * FB, FB)])
                load(step, 2, down_v[i])
            last = Place(DENSE_UNIT + 8 + STEP_UNITS * (DENSE_STEPS - 2), DENSE_TILE + 2 + STEP_TILES * (DENSE_STEPS - 2))
            load(last, 0, gate_v[0, :, :, (DENSE_STEPS - 1) * FB:FF_DENSE], DENSE_LAST)
            load(last, 1, up_v[0, :, :, (DENSE_STEPS - 1) * FB:FF_DENSE], DENSE_LAST)
            load(last, 2, down_v[DENSE_STEPS - 2])
            load(last, 3, down_last_v)
            load_gain(2)
            attention(1)

            def experts(unit0, tile0):
                def head(e, place):
                    tiles = [mgate_v[e, :, :, 0:FB], mup_v[e, :, :, 0:FB]]
                    for i in range(2):
                        tiles += [mgate_v[e, :, :, (i + 1) * FB:(i + 2) * FB], mup_v[e, :, :, (i + 1) * FB:(i + 2) * FB],
                                  mdown_v[e, i]]
                    for j, src in enumerate(tiles):
                        if place.tile + j == MOE_TILE + 3 and place.e is None:
                            sp.wait_ge(o_ready, DEPTH * JOBS)
                        if place.tile + j == MOE_TILE + 5 and place.e is None:
                            sp.wait_ge(h_split, TOKS)
                        load(place, j, src)

                def rest_of(e, place):
                    with sp.Fori(0, PAIR_STEPS) as i:
                        step = place.plus(8 + 2 * STEP_UNITS, 2 + 2 * STEP_TILES).turn(i)
                        for n in range(PAIR):
                            at = bass.ds((i * PAIR + (3 + n)) * FB, FB)
                            load(step, n * STEP_TILES, mgate_v[e, :, :, at])
                            load(step, n * STEP_TILES + 1, mup_v[e, :, :, at])
                            load(step, n * STEP_TILES + 2, mdown_v[e, i * PAIR + (2 + n)])
                    load(place.plus(EXPERT_UNITS - 4, EXPERT_TILES - 1), 0, mdown_v[e, STEPS - 1])

                head(0, ExpertPlace(unit0, tile0))
                if unit0 == MOE_UNIT:
                    load_gain(4)

                def pair(p, reg, more):
                    place = ExpertPlace(unit0, tile0, e=reg)
                    if reg is None:
                        place = place.plus(p * PAIR * EXPERT_UNITS, p * PAIR * EXPERT_TILES)
                    rest_of(p * PAIR, place)
                    head(p * PAIR + 1, place.plus(EXPERT_UNITS, EXPERT_TILES))
                    rest_of(p * PAIR + 1, place.plus(EXPERT_UNITS, EXPERT_TILES))
                    if more:
                        head(p * PAIR + 2, place.plus(PAIR * EXPERT_UNITS, PAIR * EXPERT_TILES))

                with sp.Fori(0, EXPERTS // PAIR - 1) as p:
                    pair(p, p, True)
                pair(EXPERTS // PAIR - 1, None, False)

            experts(MOE_UNIT, MOE_TILE)
            sp.wait_ge(flag_ready, 1)
            some_over = sp.value_load(over_i[0:1, 0:1], min_val=0, max_val=1)
            with sp.If(some_over == 1):
                experts(MOE_UNIT + EXPERTS * EXPERT_UNITS, MOE_TILE + EXPERTS * EXPERT_TILES)
            for t in range(TOKS):
                sp.wait_ge(h_ready, parts_before(4) + 2 * (t + 1))
                sp.dma_start(out_v[:, t, :], h[:, t, :]).then_inc(out_stored, 16)
            sp.wait_ge(out_stored, 16 * TOKS)

        @block.gpsimd
        def _(pool):
            pool.memset(ident[:, :], 0.0).then_inc(iotas, 1)
            pool.memset(before[:, :], 1.0).then_inc(iotas, 1)
            pool.memset(ones[:, :], 1.0).then_inc(consts, 1)
            pool.memset(eps_t[:, 0:1], NORM_EPS).then_inc(consts, 1)
            pool.memset(eps_t[:, 1:2], SUBLN_EPS).then_inc(consts, 1)
            pool.wait_ge(iotas, 2)
            pool.affine_select(out=ident[:, :], in_=ident[:, :], compare_op=ALU.not_equal, fill=1.0, base=0,
                               pattern=[[-1, P]], channel_multiplier=1).then_inc(consts, 1)
            pool.affine_select(out=before[:, :], in_=before[:, :], compare_op=ALU.is_gt, fill=0.0, base=0,
                               pattern=[[1, P]], channel_multiplier=-1).then_inc(consts, 1)
            pool.iota(slot_no[:, :], pattern=[[1, P]], base=0, channel_multiplier=0,
                      allow_small_or_imprecise_dtypes=True).then_inc(consts, 1)
            pool.iota(expert_no[:, :, :], pattern=[[0, TOKS], [1, EXPERTS]], base=-EXPERTS, channel_multiplier=0,
                      allow_small_or_imprecise_dtypes=True).then_inc(consts, 1)

        CONSTS = 7

        @block.scalar
        def _(sc):
            steps = [0]

            def chain(ins):
                steps[0] += 1
                ins.then_inc(astep, 1)
                sc.wait_ge(astep, steps[0])

            def high(place, units, cols=FB):
                for i in units:
                    if i % TILE_UNITS == 0:
                        sc.wait_ge(loaded[place.slot(i // TILE_UNITS)], place.loaded(i // TILE_UNITS))
                    if place.unit + i >= RING:
                        sc.wait_ge(unit_used, place.used(i - RING))
                    src = raw[place.slot(i // TILE_UNITS)][:, i % TILE_UNITS * UNIT:(i % TILE_UNITS + 1) * UNIT]
                    dst = w_hi[place.ring(i)][:, :]
                    if cols < FB:
                        src = src.rearrange("p (c n) -> p c n", c=2)[:, :, 0:cols]
                        dst = dst.rearrange("p (c n) -> p c n", c=2)[:, :, 0:cols]
                    sc.activation(dst, src, ACT.Copy).then_inc(hi_ready, 1)

            def norm(k):
                if k:
                    sc.wait_ge(x_added, {1: 2, 2: 3, 3: 6, 4: 7}[k])
                else:
                    sc.wait_ge(x_loaded[0], 16)
                chain(sc.activation(h[:, 0, :], x[:, 0, :], ACT.Square, scale=D ** -0.5, accum_out=mean_sq[:, 0:1]))
                sc.wait_ge(sq_ready, k + 1)
                sc.activation(norm_sd[:, :], mean_sq[:, :], ACT.Sqrt, bias=eps_t[:, 0:1]).then_inc(sd_ready, 1)

            def root_table():
                chain(sc.activation(junk[:, 0:1], eps_t[:, 0:1], ACT.Sqrt))

            def turn(k, first_bank, parts=range(4)):
                for g in parts:
                    sc.wait_ge(turned, 4 * k + g + 1)
                    t, c = g % 2, 4 * (g // 2)
                    sc.activation(hT_hi[:, c:c + 4, t * P:(t + 1) * P],
                                  bank[first_bank + g].rearrange("p (c t) -> p c t", c=4), ACT.Copy).then_inc(tT_hi, 1)

            def heads_of(b):
                return b[:, 0:ML_Q_COLS].rearrange("p (h c) -> p h c", c=ML_QK)

            def attention(l):
                place = Place(UNIT0[l], TILE0[l])
                high(place, range(AHEAD if l else RING, 8))
                sc.wait_ge(unit_used, place.used(3))
                for t in range(TOKS):
                    ins = sc.activation(rest[:, t, :], bank[t][:, 0:REST], ACT.Copy)
                ins.then_inc(v_copied, 1)
                sc.wait_ge(v_copied, 2 * l + 1)
                for t in range(TOKS):
                    for i, (a, n) in enumerate(((0, Q_RANK), (Q_RANK, KV_RANK))):
                        ins = sc.activation(junk[:, 0:n], rest[:, t, a:a + n], ACT.Square, scale=n ** -0.5,
                                            accum_out=lat_sq[:, t, i:i + 1])
                        chain(ins)
                sc.activation(lat_sd[:, :, :], lat_sq[:, :, :], ACT.Sqrt, bias=eps_t[:, 0:1]).then_inc(lat_sd_ready, 1)
                high(place, range(8, 12))
                sc.wait_ge(lat_turned, 2 * l + 1)
                sc.activation(cqT[:, :, :], bank[0].rearrange("p (c t) -> p c t", c=2), ACT.Copy).then_inc(cqT_ready, 1)
                high(place, range(12, 14))
                sc.wait_ge(ml_proj, 3 * l + 1)
                for t in range(TOKS):
                    ins = sc.activation(q_ml[:, t, :, 0:NOPE], heads_of(bank[t])[:, :, 0:NOPE], ACT.Copy)
                ins.then_inc(ml_nope, 1)
                high(place, range(14, 18))
                sc.wait_ge(unit_used, place.used(15))
                for t in range(TOKS):
                    ins = sc.activation(v_da[:, t, :], bank[6 + t], ACT.Copy)
                ins.then_inc(v_copied, 1)
                for t in range(TOKS):
                    sc.wait_ge(ml_proj, 3 * l + 2 + t)
                    for i in range(2):
                        kv = bank[2 + 2 * t + i][:, 0:2 * KV_HEAD].rearrange("p (h c) -> p h c", c=KV_HEAD)
                        ins = sc.activation(k_ml[:, t, 2 * i:2 * i + 2, 0:NOPE], kv[:, :, 0:NOPE], ACT.Copy)
                    ins.then_inc(ml_nope, 1)
                for g in range(2):
                    sc.wait_ge(da_turned, 4 * l + g + 1)
                    sc.activation(qT_da[:, 2 * g:2 * g + 2, :], bank[g].rearrange("p (h t) -> p h t", h=2),
                                  ACT.Copy, scale=DA_DIM ** -0.5).then_inc(da_qT, 1)
                for g in range(2):
                    sc.wait_ge(ml_turned, 4 * l + g + 1)
                    sc.activation(qT_ml[0:ML_QK, 2 * g:2 * g + 2, :], bank[2 + g][0:ML_QK, :].rearrange("p (h t) -> p h t", h=2),
                                  ACT.Copy, scale=ML_QK ** -0.5).then_inc(ml_qT, 1)
                base = JOBS * l
                for i in range(JOBS + 3):
                    j = i
                    if j < JOBS:
                        sc.wait_ge(max_ready, base + j + 1)
                        if j >= 2:
                            sc.wait_ge(probs_turned, base + j - 1)
                        for c in range(2):
                            ins = sc.activation(probs[j % 2][:, c, :], scores[j % 2][:, c, :], ACT.Exp,
                                                bias=neg_max[:, j, c:c + 1], accum_out=row_sum[:, j, c:c + 1])
                        ins.then_inc(probs_ready, 1)
                    j = i - 2
                    if 0 <= j < JOBS:
                        n = S if j < DA_JOBS else 2 * S
                        sc.wait_ge(probs_turned, base + j + 1)
                        if j >= 2:
                            sc.wait_ge(pv_ready, base + j - 1)
                        sc.activation(probsT[j % 2][:, 0:n], bank[4 + j % 2][:, 0:n], ACT.Copy).then_inc(probsT_ready, 1)
                    j = i - 5
                    if 0 <= j < DA_JOBS:
                        sc.wait_ge(o_ready, base + j + 1)
                        t, hd = j % 2, j // 2
                        ins = sc.activation(o_squares[:, j, :], h[:, t, hd * P:(hd + 1) * P], ACT.Square, scale=DA_V ** -0.5,
                                            accum_out=o_sq[:, t, hd:hd + 1])
                        if j == DA_JOBS - 1:
                            chain(ins)
                            sc.activation(o_sd[:, :, :], o_sq[:, :, :], ACT.Sqrt, bias=eps_t[:, 1:2]).then_inc(o_sd_ready, 1)
                turn(3 * l + 1, 0)
                high(place, range(18, 24))
                nxt = (Place, ExpertPlace)[l](UNIT0[l] + LAYER_UNITS, TILE0[l] + LAYER_TILES)
                high(nxt, range(AHEAD))
                norm(2 * l + 1)
                turn(3 * l + 2, 0)

            def silu_of(step, fb_count, toks, cols):
                sc.wait_ge(unit_used, step.used(3))
                if not (isinstance(fb_count, int) and fb_count == 1):
                    sc.wait_ge(act_ready, fb_count - 1)
                for t in range(toks):
                    ins = sc.activation(silu[toks][:, t, 0:cols], bank[t][:, 0:cols], ACT.Silu)
                ins.then_inc(silu_ready, 1)

            def act_hi(count, toks, banks, chunks):
                for t in range(toks):
                    sc.wait_ge(act_turned, count + t + 1)
                    sc.activation(aT_hi[:, 0:chunks, t * P:(t + 1) * P],
                                  bank[banks[t]][:, 0:chunks * P].rearrange("p (c t) -> p c t", c=chunks),
                                  ACT.Copy).then_inc(aT_hi_ready, 1)

            sc.wait_ge(consts, CONSTS)
            root_table()
            norm(0)
            turn(0, 4, range(2))
            high(Place(0, 0), [0], REST)
            turn(0, 4, range(2, 4))
            high(Place(0, 0), range(1, 4), REST)
            high(Place(0, 0), [4, 5])
            sc.wait_ge(angles, 1)
            sc.activation(sines[:, 0, :, :], angle[:, :, :], ACT.Sin)
            sc.activation(sines[:, 1, :, :], angle[:, :, :], ACT.Sin, scale=0.5).then_inc(sines_ready, 1)
            sc.wait_ge(dots, 1)
            sc.activation(lam_exps[:, :, :], lam_dots[:, :, :], ACT.Exp).then_inc(lam_exp, 1)
            sc.wait_ge(router_loaded, 16)
            sc.activation(r_halves[:, :, 0, :], r_w[:, :, :], ACT.Copy).then_inc(r_split, 1)
            attention(0)

            high(Place(DENSE_UNIT, DENSE_TILE), range(AHEAD, 8))
            silu_of(Place(DENSE_UNIT, DENSE_TILE), 1, TOKS, FB)
            with sc.Fori(0, DENSE_STEPS - 2) as i:
                step = Place(DENSE_UNIT + 8, DENSE_TILE + 2, fb=i)
                high(step, range(0, AHEAD))
                act_hi(i * TOKS, TOKS, (2, 3), FB // P)
                high(step, range(AHEAD, 9))
                silu_of(step, i + 2, TOKS, FB)
                high(step, range(9, 12))
            last = Place(DENSE_UNIT + 8 + STEP_UNITS * (DENSE_STEPS - 2), DENSE_TILE + 2 + STEP_TILES * (DENSE_STEPS - 2))
            high(last, range(0, AHEAD), DENSE_LAST)
            act_hi((DENSE_STEPS - 2) * TOKS, TOKS, (2, 3), FB // P)
            high(last, range(AHEAD, 8), DENSE_LAST)
            high(last, [8])
            silu_of(last, DENSE_STEPS, TOKS, DENSE_LAST)
            high(last, range(9, 12 + DENSE_LAST // P))
            root_table()
            act_hi((DENSE_STEPS - 1) * TOKS, TOKS, (2, 3), DENSE_LAST // P)
            high(Place(UNIT0[1], TILE0[1]), range(4), REST)
            high(Place(UNIT0[1], TILE0[1]), [4])
            norm(2)
            turn(3, 4)
            attention(1)

            sc.wait_ge(routed_ps, 1)
            for t in range(TOKS):
                sc.activation(h_hi[:, t, :], h[:, t, :], ACT.Copy).then_inc(h_hi_ready, 1)
            sc.wait_ge(router_d, 1)
            sc.activation(rs["e"][:, :], rs["d"][:, :], ACT.Exp).then_inc(router_exp, 1)

            def experts(unit0, tile0, fb0, tok0, e0):
                def gather_out(e):
                    for g in range(4):
                        sc.wait_ge(gathered, (e + e0) * 4 + g + 1)
                        dst = (g_hi, g_lo)[g % 2]
                        sc.activation(dst[:, g // 2 * 4:g // 2 * 4 + 4, :], bank[GATHER_BANKS[g]].rearrange("p (c t) -> p c t", c=4),
                                      ACT.Copy).then_inc(g_ready, 1)

                def y_out(nxt):
                    sc.wait_ge(unit_used, nxt.used(-1))
                    for half in range(2):
                        sc.activation(y_hi[:, half * 512:(half + 1) * 512], bank[5 + half], ACT.Copy,
                                      scale=slot_gate[:, 0:1]).then_inc(y_hi_ready, 1)

                def step0(e, place, units):
                    high(place, units)
                    silu_of(place, e * STEPS + (fb0 + 1), 1, FB)

                def steps(e, place):
                    def step_of(step, n):
                        high(step, range(0, AHEAD))
                        act_hi(e * STEPS + n + (tok0 - 1), 1, (2,), FB // P)
                        high(step, range(AHEAD, 9))
                        silu_of(step, e * STEPS + n + (fb0 + 1), 1, FB)
                        high(step, range(9, 12))

                    step = place.plus(8, 2)
                    high(step, range(3))
                    sc.wait_ge(pick_turned, e + (e0 + 1))
                    sc.activation(slot_gate[:, :], bank[5][:, S:S + 1], ACT.Copy)
                    sc.activation(pickT[:, :, :], bank[5][:, 0:S].rearrange("p (t s) -> p t s", t=TOKS),
                                  ACT.Copy).then_inc(pickT_ready, 1)
                    high(step, range(3, 9))
                    silu_of(step, e * STEPS + (fb0 + 2), 1, FB)
                    act_hi(e * STEPS + tok0, 1, (2,), FB // P)
                    high(step, range(9, 12))
                    step_of(step.plus(STEP_UNITS, STEP_TILES), 2)
                    with sc.Fori(0, PAIR_STEPS) as i:
                        turn_at = step.plus(2 * STEP_UNITS, 2 * STEP_TILES).turn(i)
                        for n in range(PAIR):
                            step_of(turn_at.plus(n * STEP_UNITS, n * STEP_TILES), i * PAIR + (3 + n))
                    tail = place.plus(EXPERT_UNITS - 4, EXPERT_TILES - 1)
                    high(tail, range(2))
                    act_hi(e * STEPS + (tok0 + STEPS - 1), 1, (2,), FB // P)
                    high(tail, [2])

                def change(e, nxt):
                    gather_out(e + 1)
                    high(nxt, range(-1, 3))
                    y_out(nxt)
                    step0(e + 1, nxt, range(3, 8))

                def pair(p, place, more):
                    for n in range(PAIR):
                        here, nxt = place.plus(n * EXPERT_UNITS, n * EXPERT_TILES), place.plus((n + 1) * EXPERT_UNITS, (n + 1) * EXPERT_TILES)
                        steps(p * PAIR + n, here)
                        if more or n < PAIR - 1:
                            change(p * PAIR + n, nxt)
                        else:
                            high(nxt, [-1])
                            y_out(nxt)

                first = ExpertPlace(unit0, tile0)
                if e0:
                    high(first, range(AHEAD))
                gather_out(0)
                step0(0, first, range(AHEAD, 8))
                with sc.Fori(0, EXPERTS // PAIR - 1) as p:
                    pair(p, ExpertPlace(unit0, tile0, e=p), True)
                p = EXPERTS // PAIR - 1
                pair(p, first.plus(p * PAIR * EXPERT_UNITS, p * PAIR * EXPERT_TILES), False)

            experts(MOE_UNIT, MOE_TILE, DENSE_STEPS, DENSE_STEPS * TOKS, 0)
            sc.wait_ge(flag_ready, 1)
            some_over = sc.value_load(over_i[0:1, 0:1], min_val=0, max_val=1)
            with sc.If(some_over == 1):
                experts(MOE_UNIT + EXPERTS * EXPERT_UNITS, MOE_TILE + EXPERTS * EXPERT_TILES,
                        DENSE_STEPS + EXPERTS * STEPS, DENSE_STEPS * TOKS + EXPERTS * STEPS, EXPERTS)
                sc.wait_ge(x_added, 8)
            root_table()
            norm(4)

        @block.vector
        def _(ve):
            steps_done = [0]

            def chain(ins):
                steps_done[0] += 1
                ins.then_inc(vstep, 1)
                ve.wait_ge(vstep, steps_done[0])

            def low(place, units, cols=FB):
                for i in units:
                    ve.wait_ge(hi_ready, place.used(i))
                    src = raw[place.slot(i // TILE_UNITS)][:, i % TILE_UNITS * UNIT:(i % TILE_UNITS + 1) * UNIT]
                    hi, lo = w_hi[place.ring(i)][:, :].bitcast(F32), w_lo[place.ring(i)][:, :]
                    if cols < FB:
                        src, hi, lo = (a.rearrange("p (c n) -> p c n", c=2)[:, :, 0:cols] for a in (src, hi, lo))
                    ve.tensor_tensor(lo, src, hi, ALU.subtract).then_inc(lo_ready, 1)

            def norm(k):
                if k == 0:
                    ve.wait_ge(x_loaded[1], 16)
                elif k < 4:
                    ve.wait_ge(x_added, {1: 2, 2: 4, 3: 6}[k])
                ve.tensor_tensor_reduce(h[:, 1, :], x[:, 1, :], x[:, 1, :], 1.0 / D, 0.0, ALU.mult, ALU.add,
                                        mean_sq[:, 1:2]).then_inc(sq_ready, 1)
                ve.wait_ge(sd_ready, k + 1)
                chain(ve.reciprocal(norm_r[:, :], norm_sd[:, :]))
                ve.wait_ge(gain_loaded[k % 2], 16 * (k // 2 + 1))
                if k == 0:
                    ve.wait_ge(x_loaded[0], 16)
                for g in range(4):
                    t, half = (g % 2, g // 2) if k < 4 else (g // 2, g % 2)
                    part = slice(half * 512, (half + 1) * 512)
                    ve.scalar_tensor_tensor(out=h[:, t, part], in0=x[:, t, part], scalar=norm_r[:, t:t + 1],
                                            in1=gain[k % 2][:, part], op0=ALU.mult, op1=ALU.mult).then_inc(h_ready, 1)

            def turn(k, first_bank, parts=range(4)):
                for g in parts:
                    ve.wait_ge(tT_hi, 4 * k + g + 1)
                    t, c = g % 2, 4 * (g // 2)
                    at = (slice(None), slice(c, c + 4), slice(t * P, (t + 1) * P))
                    ve.tensor_tensor(hT_lo[at], bank[first_bank + g].rearrange("p (c t) -> p c t", c=4),
                                     hT_hi[at].bitcast(F32), ALU.subtract).then_inc(tT_lo, 1)

            def rotate(dst, src, t, heads, half, at):
                cos = cos_t[:, t, at:at + 2 * half].unsqueeze(1).to_broadcast([P, heads, 2 * half])
                sn = [sin_t[:, t, at + i * half:at + (i + 1) * half].unsqueeze(1).to_broadcast([P, heads, half])
                      for i in range(2)]
                n = heads * 2 * half
                a = probs_raw[0][:, 0:n].rearrange("p (h c) -> p h c", h=heads)
                b = probs_raw[1][:, 0:n].rearrange("p (h c) -> p h c", h=heads)
                ve.tensor_tensor(a, src, cos, ALU.mult)
                ve.tensor_tensor(b[:, :, 0:half], src[:, :, half:], sn[0], ALU.mult)
                chain(ve.tensor_tensor(b[:, :, half:], src[:, :, 0:half], sn[1], ALU.mult))
                return ve.tensor_tensor(dst, a, b, ALU.add)

            def rotate_da(l, n, dst, banks):
                ve.wait_ge(unit_used, Place(UNIT0[l], TILE0[l]).used(4 * n + 7))
                for t in range(TOKS):
                    ins = rotate(dst[:, t, :].rearrange("p (h c) -> p h c", c=DA_DIM),
                                 bank[banks[t]].rearrange("p (h c) -> p h c", c=DA_DIM), t, 2 * DA_HEADS, HALF, 0)
                    if t < TOKS - 1:
                        chain(ins)
                ins.then_inc(rotated, 1)
                ve.wait_ge(rotated, 2 * l + n + 1)

            def attention(l):
                place = Place(UNIT0[l], TILE0[l])
                low(place, range(AHEAD if l else RING, 8))
                if l == 0:
                    tables()
                ve.wait_ge(v_copied, 2 * l + 1)
                for t in range(TOKS):
                    chain(rotate(k_pe[:, t, :].unsqueeze(1), rest[:, t, Q_RANK + KV_RANK:].unsqueeze(1), t, 1, ROPE // 2, DA_DIM))
                ve.wait_ge(small_loaded, 80 * (l + 1))
                ve.tensor_scalar(sub_scaled[:, :], sub_gain[:, :], 1.0 - lambda_init(l), None, ALU.mult)
                ve.wait_ge(lat_sd_ready, l + 1)
                chain(ve.reciprocal(lat_r[:, :, :], lat_sd[:, :, :]))
                for t in range(TOKS):
                    for i, (a, n) in enumerate(((0, Q_RANK), (Q_RANK, KV_RANK))):
                        ins = ve.scalar_tensor_tensor(out=latent[:, t, a:a + n], in0=rest[:, t, a:a + n],
                                                      scalar=lat_r[:, t, i:i + 1], in1=latent_gain[:, a:a + n],
                                                      op0=ALU.mult, op1=ALU.mult)
                ins.then_inc(lat_ready, 1)
                low(place, range(8, 12))
                rotate_da(l, 0, q_rot, (2, 3))
                ve.wait_ge(lat_turned, 2 * l + 2)
                ve.tensor_copy(ckT[:, :], bank[1][:, 0:S]).then_inc(ckT_ready, 1)
                low(place, range(12, 14))
                rotate_da(l, 1, k_rot, (4, 5))
                low(place, [14])
                ve.wait_ge(ml_nope, 3 * l + 1)
                for t in range(TOKS):
                    ins = rotate(q_ml[:, t, :, NOPE:], bank[t][:, 0:ML_Q_COLS].rearrange("p (h c) -> p h c", c=ML_QK)[:, :, NOPE:],
                                 t, ML_HEADS, ROPE // 2, DA_DIM)
                    if t < TOKS - 1:
                        chain(ins)
                ins.then_inc(ml_qk, 1)
                low(place, range(15, 18))
                for t in range(TOKS):
                    ve.wait_ge(ml_nope, 3 * l + 2 + t)
                    for i in range(2):
                        kv = bank[2 + 2 * t + i][:, 0:2 * KV_HEAD].rearrange("p (h c) -> p h c", c=KV_HEAD)
                        ve.tensor_copy(v_ml[:, t, 2 * i * ML_V:2 * (i + 1) * ML_V].rearrange("p (h c) -> p h c", h=2),
                                       kv[:, :, NOPE:])
                    ins = ve.tensor_copy(k_ml[:, t, :, NOPE:], k_pe[:, t, :].unsqueeze(1).to_broadcast([P, ML_HEADS, ROPE]))
                ins.then_inc(ml_qk, 1)
                for g in range(2):
                    ve.wait_ge(da_turned, 4 * l + 3 + g)
                    ve.tensor_copy(kT_da[:, 2 * g:2 * g + 2, :],
                                   bank[6 + g].rearrange("p (h t) -> p h t", h=2)).then_inc(da_kT, 1)
                for g in range(2):
                    ve.wait_ge(ml_turned, 4 * l + 3 + g)
                    ve.tensor_copy(kT_ml[0:ML_QK, 2 * g:2 * g + 2, :],
                                   bank[4 + g][0:ML_QK, :].rearrange("p (h t) -> p h t", h=2)).then_inc(ml_kT, 1)
                base = JOBS * l
                for i in range(JOBS + 4):
                    j = i
                    if j < JOBS:
                        ve.wait_ge(scored, base + j + 1)
                        ve.tensor_reduce(neg_max[:, j, :], scores[j % 2], AX.X, ALU.max, negate=True).then_inc(max_ready, 1)
                    j = i - 1
                    if 0 <= j < JOBS:
                        ve.wait_ge(probs_ready, base + j + 1)
                        ins = ve.reciprocal(row_inv[:, j, :], row_sum[:, j, :])
                        if j < DA_JOBS:
                            chain(ins)
                            chain(ve.scalar_tensor_tensor(out=mix_coef[:, j:j + 1], in0=row_inv[:, j, 1:2],
                                                          scalar=row_sum[:, j, 0:1], in1=neg_lam[:, l:l + 1],
                                                          op0=ALU.mult, op1=ALU.mult))
                            if j >= 2:
                                ve.wait_ge(probs_turned, base + j - 1)
                            ins = ve.scalar_tensor_tensor(out=mixed[j % 2][:, :], in0=probs[j % 2][:, 1, :],
                                                          scalar=mix_coef[:, j:j + 1], in1=probs[j % 2][:, 0, :],
                                                          op0=ALU.mult, op1=ALU.add)
                        ins.then_inc(mix_ready, 1)
                    if i == JOBS + 2:
                        ve.wait_ge(o_sd_ready, l + 1)
                        chain(ve.reciprocal(o_r[:, :, :], o_sd[:, :, :]))
                        for t in range(TOKS):
                            for hd in range(DA_HEADS):
                                o = h[:, t, hd * P:(hd + 1) * P]
                                ins = ve.scalar_tensor_tensor(out=o, in0=o, scalar=o_r[:, t, hd:hd + 1], in1=sub_scaled[:, :],
                                                              op0=ALU.mult, op1=ALU.mult)
                            ins.then_inc(h_ready, 1)
                    j = i - 4
                    if 0 <= j < JOBS:
                        ve.wait_ge(pv_ready, base + j + 1)
                        if j < DA_JOBS:
                            t, hd = j % 2, j // 2
                            ins = ve.tensor_scalar(h[:, t, hd * P:(hd + 1) * P], bank[6 + j % 2][:, 0:P],
                                                   row_inv[:, j, 0:1], None, ALU.mult)
                        else:
                            t, pair = j % 2, (j - DA_JOBS) // 2
                            for c in range(2):
                                col = DA_HEADS * DA_V + (2 * pair + c) * P
                                ins = ve.tensor_scalar(h[:, t, col:col + P], bank[6 + j % 2][:, c * P:(c + 1) * P],
                                                       row_inv[:, j, c:c + 1], None, ALU.mult)
                        ins.then_inc(o_ready, 1)
                turn(3 * l + 1, 0)
                low(place, range(18, 24))
                nxt = (Place, ExpertPlace)[l](UNIT0[l] + LAYER_UNITS, TILE0[l] + LAYER_TILES)
                low(nxt, [0])
                for n in range(2):
                    ve.wait_ge(unit_used, place.used(19 + 4 * n))
                    for t in range(TOKS):
                        xs = x[:, t, n * 512:(n + 1) * 512]
                        ins = ve.tensor_tensor(xs, xs, bank[4 + 2 * n + t], ALU.add)
                    ins.then_inc(x_added, 1)
                    if n == 0:
                        low(nxt, range(1, AHEAD))
                norm(2 * l + 1)
                turn(3 * l + 2, 0)

            def multiply(up_used, fb_count, toks, up_banks, cols):
                ve.wait_ge(silu_ready, fb_count)
                ve.wait_ge(unit_used, up_used)
                for t in range(toks):
                    ins = ve.tensor_tensor(act[toks][:, t, 0:cols], silu[toks][:, t, 0:cols], bank[up_banks[t]][:, 0:cols], ALU.mult)
                ins.then_inc(act_ready, 1)

            def act_lo(count, toks, banks, chunks):
                for t in range(toks):
                    ve.wait_ge(aT_hi_ready, count + t + 1)
                    at = (slice(None), slice(0, chunks), slice(t * P, (t + 1) * P))
                    ve.tensor_tensor(aT_lo[at], bank[banks[t]][:, 0:chunks * P].rearrange("p (c t) -> p c t", c=chunks),
                                     aT_hi[at].bitcast(F32), ALU.subtract).then_inc(aT_lo_ready, 1)

            def tables():
                ve.wait_ge(sines_ready, 1)
                for t in range(TOKS):
                    for a, f, n in ((0, 0, HALF), (DA_DIM, HALF, ROPE // 2)):
                        s, s_half = sines[:, 0, t, f:f + n], sines[:, 1, t, f:f + n]
                        ve.tensor_scalar(sin_t[:, t, a:a + n], s, -1.0, None, ALU.mult)
                        ve.tensor_copy(sin_t[:, t, a + n:a + 2 * n], s)
                        for i in range(2):
                            ins = ve.tensor_tensor(cos_t[:, t, a + i * n:a + (i + 1) * n], s_half, s_half, ALU.mult)
                chain(ins)
                chain(ve.tensor_scalar(cos_t[:, :, :], cos_t[:, :, :], -2.0, 1.0, ALU.mult, ALU.add))
                ve.wait_ge(lam_exp, 1)
                chain(ve.tensor_tensor(neg_lam[:, :], lam_exps[:, 1, :], lam_exps[:, 0, :], ALU.subtract))
                for l in range(DEPTH):
                    ins = ve.tensor_scalar(neg_lam[:, l:l + 1], neg_lam[:, l:l + 1], -lambda_init(l), None, ALU.add)
                chain(ins)

            norm(0)
            turn(0, 4, range(2))
            low(Place(0, 0), [0], REST)
            turn(0, 4, range(2, 4))
            low(Place(0, 0), range(1, 4), REST)
            low(Place(0, 0), [4, 5])
            ve.wait_ge(rope_in, 32)
            chain(ve.tensor_copy(pos_f[:, :], pos_i[:, :]))
            for t in range(TOKS):
                ins = ve.tensor_scalar(angle[:, t, :], freq[:, :], pos_f[:, t:t + 1], None, ALU.mult)
            chain(ins)
            chain(ve.tensor_scalar(turns_i[:, :, :], angle[:, :, :], 1 / TWO_PI, None, ALU.mult))
            chain(ve.tensor_copy(turns_f[:, :, :], turns_i[:, :, :]))
            for c in (_C1, _C2, _C3):
                chain(ve.scalar_tensor_tensor(out=angle[:, :, :], in0=turns_f[:, :, :], scalar=-c, in1=angle[:, :, :],
                                              op0=ALU.mult, op1=ALU.add))
            ve.tensor_scalar(angle[:, :, :], angle[:, :, :], PI_DOWN, -PI_DOWN, ALU.min, ALU.max).then_inc(angles, 1)
            ve.wait_ge(lam_in, 64)
            for i in range(2):
                ins = ve.tensor_tensor(lam_prod[:, i, :, :], lam_vecs[:, 2 * i, :, :], lam_vecs[:, 2 * i + 1, :, :], ALU.mult)
            chain(ins)
            ve.tensor_reduce(lam_dots[:, :, :], lam_prod[:, :, :, :], AX.X, ALU.add).then_inc(dots, 1)
            ve.wait_ge(r_split, 1)
            ve.tensor_tensor(r_halves[:, :, 1, :], r_w[:, :, :], r_halves[:, :, 0, :].bitcast(F32), ALU.subtract).then_inc(r_split, 1)
            attention(0)

            low(Place(DENSE_UNIT, DENSE_TILE), range(AHEAD, 8))
            multiply(Place(DENSE_UNIT, DENSE_TILE).used(7), 1, TOKS, (2, 3), FB)
            with ve.Fori(0, DENSE_STEPS - 2) as i:
                step = Place(DENSE_UNIT + 8, DENSE_TILE + 2, fb=i)
                low(step, range(0, AHEAD))
                act_lo(i * TOKS, TOKS, (2, 3), FB // P)
                low(step, range(AHEAD, 12))
                multiply(step.used(7), i + 2, TOKS, (2, 3), FB)
            last = Place(DENSE_UNIT + 8 + STEP_UNITS * (DENSE_STEPS - 2), DENSE_TILE + 2 + STEP_TILES * (DENSE_STEPS - 2))
            low(last, range(0, AHEAD), DENSE_LAST)
            act_lo((DENSE_STEPS - 2) * TOKS, TOKS, (2, 3), FB // P)
            low(last, range(AHEAD, 8), DENSE_LAST)
            low(last, range(8, 12))
            multiply(last.used(7), DENSE_STEPS, TOKS, (2, 3), DENSE_LAST)
            low(last, range(12, 12 + DENSE_LAST // P))
            act_lo((DENSE_STEPS - 1) * TOKS, TOKS, (2, 3), DENSE_LAST // P)
            low(Place(UNIT0[1], TILE0[1]), range(4), REST)
            low(Place(UNIT0[1], TILE0[1]), [4])
            for t in range(TOKS):
                if t < TOKS - 1:
                    ve.wait_ge(dense_summed, t + 1)
                else:
                    ve.wait_ge(unit_used, Place(UNIT0[1], TILE0[1]).used(-1))
                for half in range(2):
                    xs = x[:, t, half * 512:(half + 1) * 512]
                    ins = ve.tensor_tensor(xs, xs, bank[4 + 2 * t + half][:, :], ALU.add)
                ins.then_inc(x_added, 1)
            norm(2)
            turn(3, 4)
            attention(1)

            ve.wait_ge(routed_ps, 1)
            shape = [P, TOKS, EXPERTS]

            def wide(a):
                return a[:, :].unsqueeze(2).to_broadcast(shape)

            chain(ve.tensor_reduce(rt["logits"][:, :, :],
                                   bank[5][:, 0:TOKS * 2 * EXPERTS].rearrange("p (t i e) -> p t e i", t=TOKS, i=2),
                                   AX.X, ALU.add))
            ve.wait_ge(consts, CONSTS)

            def best(logits, m, eq, cand, i, onehot):
                chain(ve.tensor_reduce(rs[m][:, :], rt[logits][:, :, :], AX.X, ALU.max))
                chain(ve.tensor_tensor(rt[eq][:, :, :], rt[logits][:, :, :], wide(rs[m]), ALU.is_equal))
                chain(ve.tensor_tensor(rt[cand][:, :, :], rt[eq][:, :, :], expert_no[:, :, :], ALU.mult))
                chain(ve.tensor_reduce(rs[i][:, :], rt[cand][:, :, :], AX.X, ALU.min))
                chain(ve.tensor_tensor(rt[onehot][:, :, :], expert_no[:, :, :], wide(rs[i]), ALU.is_equal))

            best("logits", "m1", "eq", "cand", "i1", "first")
            chain(ve.scalar_tensor_tensor(out=rt["logits2"][:, :, :], in0=rt["first"][:, :, :], scalar=-3e38,
                                          in1=rt["logits"][:, :, :], op0=ALU.mult, op1=ALU.add))
            best("logits2", "m2", "eq2", "cand2", "i2", "second")
            ve.tensor_tensor(mask[:, :, 0:EXPERTS], rt["first"][:, :, :], rt["second"][:, :, :], ALU.add).then_inc(mask_ready, 1)
            ve.tensor_tensor(rs["d"][:, :], rs["m2"][:, :], rs["m1"][:, :], ALU.subtract).then_inc(router_d, 1)
            for t in range(TOKS):
                ve.wait_ge(h_hi_ready, t + 1)
                ve.tensor_tensor(h_lo[:, t, :], h[:, t, :], h_hi[:, t, :].bitcast(F32), ALU.subtract).then_inc(h_split, 1)
            ve.wait_ge(ranked_ps, 1)
            ranks = bank[6][:, 0:TOKS * EXPERTS].rearrange("p (t e) -> p t e", t=TOKS)
            chain(ve.tensor_copy(rank[0][:, :, 0:EXPERTS], ranks))

            def gates():
                ve.wait_ge(router_exp, 1)
                chain(ve.tensor_scalar(rs["e1"][:, :], rs["e"][:, :], 1.0, None, ALU.add))
                chain(ve.reciprocal(rs["g1"][:, :], rs["e1"][:, :]))
                chain(ve.tensor_tensor(rs["g2"][:, :], rs["g1"][:, :], rs["e"][:, :], ALU.mult))
                ve.tensor_tensor(rt["w1"][:, :, :], rt["first"][:, :, :], wide(rs["g1"]), ALU.mult)
                chain(ve.tensor_tensor(rt["w2"][:, :, :], rt["second"][:, :, :], wide(rs["g2"]), ALU.mult))
                chain(ve.tensor_tensor(share[:, :, 0:EXPERTS], rt["w1"][:, :, :], rt["w2"][:, :, :], ALU.add))
                ve.tensor_scalar(rank[1][:, :, 0:EXPERTS], ranks, -float(P), None, ALU.add)
                chain(ve.tensor_reduce(most[:, :], bank[6][:, TOKS * EXPERTS:(TOKS + 1) * EXPERTS], AX.X, ALU.max))
                chain(ve.tensor_scalar(over[:, :], most[:, :], float(P), None, ALU.is_gt))
                ve.tensor_copy(over_i[:, :], over[:, :]).then_inc(flag_ready, 1)

            def experts(unit0, tile0, fb0, tok0, e0, ranks):
                def col(table, t, e):
                    return table[:, t, bass.ds(e, 1)] if not isinstance(e, int) else table[:, t, e:e + 1]

                def choose(e):
                    for t in range(TOKS):
                        ins = ve.tensor_scalar(pick[:, t, :], slot_no[:, :], col(ranks, t, e), col(mask, t, e),
                                               ALU.is_equal, ALU.mult)
                    ins.then_inc(pick_ready, 1)

                def y_out(e):
                    for half in range(2):
                        part = slice(half * 512, (half + 1) * 512)
                        ve.wait_ge(y_hi_ready, (e + e0) * 2 + half + 1)
                        ve.scalar_tensor_tensor(out=y_lo[:, part], in0=bank[5 + half], scalar=slot_gate[:, 0:1],
                                                in1=y_hi[:, part].bitcast(F32), op0=ALU.mult, op1=ALU.subtract).then_inc(y_lo_ready, 1)

                def add_out(e):
                    for g in range(4):
                        ve.wait_ge(scattered, (e + e0) * 4 + g + 1)
                        t, half = g % 2, g // 2
                        xs = x[:, t, half * 512:(half + 1) * 512]
                        ve.tensor_tensor(xs, xs, bank[SCATTER_BANKS[g]], ALU.add).then_inc(scatter_added, 1)

                def block0(e, place):
                    low(place.plus(8, 2), range(3))
                    multiply(place.used(7), e * STEPS + (fb0 + 1), 1, (1,), FB)

                def steps(e, place, more):
                    def step_of(step, n):
                        low(step, range(0, AHEAD))
                        act_lo(e * STEPS + n + (tok0 - 1), 1, (2,), FB // P)
                        low(step, range(AHEAD, 12))
                        multiply(step.used(7), e * STEPS + n + (fb0 + 1), 1, (1,), FB)

                    step = place.plus(8, 2)
                    low(step, range(3, 9))
                    act_lo(e * STEPS + tok0, 1, (2,), FB // P)
                    low(step, range(9, 12))
                    multiply(step.used(7), e * STEPS + (fb0 + 2), 1, (1,), FB)
                    if more:
                        ve.wait_ge(pick_turned, e + (e0 + 1))
                        choose(e + 1)
                    step_of(step.plus(STEP_UNITS, STEP_TILES), 2)
                    with ve.Fori(0, PAIR_STEPS) as i:
                        turn_at = step.plus(2 * STEP_UNITS, 2 * STEP_TILES).turn(i)
                        for n in range(PAIR):
                            step_of(turn_at.plus(n * STEP_UNITS, n * STEP_TILES), i * PAIR + (3 + n))
                    tail = place.plus(EXPERT_UNITS - 4, EXPERT_TILES - 1)
                    low(tail, range(2))
                    act_lo(e * STEPS + (tok0 + STEPS - 1), 1, (2,), FB // P)
                    low(tail, range(2, 4))

                def pair(p, place, more):
                    for n in range(PAIR):
                        here, nxt = place.plus(n * EXPERT_UNITS, n * EXPERT_TILES), place.plus((n + 1) * EXPERT_UNITS, (n + 1) * EXPERT_TILES)
                        more_here = more or n < PAIR - 1
                        steps(p * PAIR + n, here, more_here)
                        if more_here:
                            low(nxt, range(3))
                        y_out(p * PAIR + n)
                        if more_here:
                            low(nxt, range(3, 8))
                            block0(p * PAIR + (n + 1), nxt)
                            add_out(p * PAIR + n)

                first = ExpertPlace(unit0, tile0)
                choose(0)
                if e0:
                    low(first, range(AHEAD))
                else:
                    gates()
                low(first, range(AHEAD, 8))
                block0(0, first)
                with ve.Fori(0, EXPERTS // PAIR - 1) as p:
                    pair(p, ExpertPlace(unit0, tile0, e=p), True)
                p = EXPERTS // PAIR - 1
                pair(p, first.plus(p * PAIR * EXPERT_UNITS, p * PAIR * EXPERT_TILES), False)
                add_out(EXPERTS - 1)
                ve.wait_ge(scatter_added, (e0 + EXPERTS) * 4 + 3)
                ve.sem_inc(x_added, 1)
                ve.wait_ge(scatter_added, (e0 + EXPERTS) * 4 + 4)

            ve.sem_inc(scatter_added, 4)
            experts(MOE_UNIT, MOE_TILE, DENSE_STEPS, DENSE_STEPS * TOKS, 0, rank[0])
            ve.wait_ge(flag_ready, 1)
            some_over = ve.value_load(over_i[0:1, 0:1], min_val=0, max_val=1)
            with ve.If(some_over == 1):
                experts(MOE_UNIT + EXPERTS * EXPERT_UNITS, MOE_TILE + EXPERTS * EXPERT_TILES,
                        DENSE_STEPS + EXPERTS * STEPS, DENSE_STEPS * TOKS + EXPERTS * STEPS, EXPERTS, rank[1])
            norm(4)

        @block.tensor
        def _(pe):
            def product(out_ap, a_hi, a_lo, b_hi, b_lo, first, last):
                pe.matmul(out_ap, a_hi, b_hi, start=first, stop=False)
                pe.matmul(out_ap, a_hi, b_lo, start=False, stop=False)
                return pe.matmul(out_ap, a_lo, b_hi, start=False, stop=last)

            def columns(place, i0, a_hi, a_lo, toks, banks, cols, since=None):
                for u in range(TILE_UNITS):
                    if since is not None and u % 2 == 0:
                        pe.wait_ge(since[0], since[1] + u + 2)
                    pe.wait_ge(lo_ready, place.used(i0 + u))
                    r = place.ring(i0 + u)
                    for c in range(2):
                        k = 2 * u + c
                        for t in range(toks):
                            tk = slice(t * P, (t + 1) * P)
                            w = slice(c * 512, c * 512 + cols)
                            ins = product(bank[banks[t]][:, 0:cols], a_hi[:, k, tk], a_lo[:, k, tk],
                                          w_hi[r][:, w], w_lo[r][:, w], k == 0, k == KC - 1)
                    ins.then_inc(unit_used, 1)

            def down(place, i0, toks, banks, chunks, first, last, summed=None):
                for c in range(chunks):
                    pe.wait_ge(lo_ready, place.used(i0 + c))
                    r = place.ring(i0 + c)
                    for t in range(toks):
                        tk = slice(t * P, (t + 1) * P)
                        for half in range(2):
                            w = slice(half * 512, (half + 1) * 512)
                            ins = product(bank[banks[2 * t + half]][:, :], aT_hi[:, c, tk], aT_lo[:, c, tk],
                                          w_hi[r][:, w], w_lo[r][:, w], first and c == 0, last and c == chunks - 1)
                        if summed is not None and c == chunks - 1 and t < toks - 1:
                            ins.then_inc(summed, 1)
                    ins.then_inc(unit_used, 1)

            def turn(k, first_bank, waits):
                for g in range(4):
                    pe.wait_ge(*waits[g])
                    t, c0 = g % 2, 4 * (g // 2)
                    for c in range(4):
                        ins = pe.transpose(bank[first_bank + g][:, c * P:(c + 1) * P], h[:, t, (c0 + c) * P:(c0 + c + 1) * P],
                                           ident[:, :])
                    ins.then_inc(turned, 1)

            def turn_norm(k, norm, first_bank):
                turn(k, first_bank, [(h_ready, parts_before(norm) + g + 1) for g in range(4)])

            def attention(l):
                place = Place(UNIT0[l], TILE0[l])
                turn_norm(3 * l, 2 * l, 4)
                columns(place, 0, hT_hi, hT_lo, TOKS, (0, 1), REST, (tT_lo, 4 * 3 * l))
                columns(place, 4, hT_hi, hT_lo, TOKS, (2, 3), FB)
                pe.wait_ge(lat_ready, l + 1)
                pe.wait_ge(v_copied, 2 * l + 1)
                for c in range(2):
                    for t in range(TOKS):
                        ins = pe.transpose(bank[0][:, c * S + t * P:c * S + (t + 1) * P], latent[:, t, c * P:(c + 1) * P], ident[:, :])
                ins.then_inc(lat_turned, 1)
                for t in range(TOKS):
                    ins = pe.transpose(bank[1][:, t * P:(t + 1) * P], latent[:, t, Q_RANK:], ident[:, :])
                ins.then_inc(lat_turned, 1)
                columns(place, 8, hT_hi, hT_lo, TOKS, (4, 5), FB)
                pe.wait_ge(small_loaded, 80 * (l + 1))
                pe.wait_ge(cqT_ready, l + 1)
                pe.wait_ge(ckT_ready, l + 1)
                for t in range(TOKS):
                    for c in range(2):
                        ins = pe.matmul(bank[t][:, 0:ML_Q_COLS], cqT[:, c, t * P:(t + 1) * P], w_uq[:, c, :],
                                        start=(c == 0), stop=(c == 1))
                ins.then_inc(ml_proj, 1)
                columns(place, 12, hT_hi, hT_lo, TOKS, (6, 7), FB)
                for t in range(TOKS):
                    pe.wait_ge(rotated, 2 * l + t + 1)
                    for i in range(2):
                        ins = pe.matmul(bank[2 + 2 * t + i][:, 0:2 * KV_HEAD], ckT[:, t * P:(t + 1) * P],
                                        w_ukv[:, 2 * i * KV_HEAD:2 * (i + 1) * KV_HEAD], start=True, stop=True)
                    ins.then_inc(ml_proj, 1)
                pe.wait_ge(ml_qk, 2 * l + 1)
                for g in range(4):
                    src = (q_rot, k_rot)[g // 2]
                    if g == 2:
                        pe.wait_ge(v_copied, 2 * l + 2)
                    for hh in range(2):
                        hd = 2 * (g % 2) + hh
                        for t in range(TOKS):
                            ins = pe.transpose(bank[(0, 1, 6, 7)[g]][:, hh * S + t * P:hh * S + (t + 1) * P],
                                               src[:, t, hd * P:(hd + 1) * P], ident[:, :])
                    ins.then_inc(da_turned, 1)
                pe.wait_ge(ml_qk, 2 * l + 2)
                for kind, src in enumerate((q_ml, k_ml)):
                    for g in range(2):
                        for hh in range(2):
                            for t in range(TOKS):
                                ins = pe.transpose(bank[2 + 2 * kind + g][0:ML_QK, hh * S + t * P:hh * S + (t + 1) * P],
                                                   src[:, t, 2 * g + hh, :], ident[:, :])
                        ins.then_inc(ml_turned, 1)
                base = JOBS * l
                pe.wait_ge(da_qT, 2 * l + 2)
                pe.wait_ge(da_kT, 2 * l + 2)
                for i in range(JOBS + 3):
                    j = i
                    if j < JOBS:
                        if j >= 2:
                            pe.wait_ge(probs_ready, base + j - 1)
                        if j == 1:
                            pe.wait_ge(ml_qT, 2 * l + 2)
                            pe.wait_ge(ml_kT, 2 * l + 2)
                        t = j % 2
                        for c in range(2):
                            if j < DA_JOBS:
                                part = slice(c * DA_DIM, (c + 1) * DA_DIM)
                                q, k = qT_da[part, j // 2, t * P:(t + 1) * P], kT_da[part, j // 2, :]
                            else:
                                hd = 2 * ((j - DA_JOBS) // 2) + c
                                q, k = qT_ml[0:ML_QK, hd, t * P:(t + 1) * P], kT_ml[0:ML_QK, hd, :]
                            ins = pe.matmul(scores[j % 2][:, c, :], q, k, start=True, stop=True)
                        ins.then_inc(scored, 1)
                    j = i - 2
                    if 0 <= j < JOBS:
                        pe.wait_ge(mix_ready, base + j + 1)
                        if j >= 2:
                            pe.wait_ge(probsT_ready, base + j - 1)
                        for c in range(1 if j < DA_JOBS else 2):
                            for kc in range(TOKS):
                                src = mixed[j % 2][:, kc * P:(kc + 1) * P] if j < DA_JOBS else probs[j % 2][:, c, kc * P:(kc + 1) * P]
                                ins = pe.transpose(bank[4 + j % 2][:, c * S + kc * P:c * S + (kc + 1) * P], src, ident[:, :])
                        ins.then_inc(probs_turned, 1)
                    j = i - 3
                    if 0 <= j < JOBS:
                        pe.wait_ge(probsT_ready, base + j + 1)
                        if j >= 2:
                            pe.wait_ge(o_ready, base + j - 1)
                        for c in range(1 if j < DA_JOBS else 2):
                            for kc in range(TOKS):
                                if j < DA_JOBS:
                                    v = v_da[:, kc, (j // 2) * DA_V:(j // 2 + 1) * DA_V]
                                else:
                                    hd = 2 * ((j - DA_JOBS) // 2) + c
                                    v = v_ml[:, kc, hd * ML_V:(hd + 1) * ML_V]
                                ins = pe.matmul(bank[6 + j % 2][:, c * P:(c + 1) * P], probsT[j % 2][:, c * S + kc * P:c * S + (kc + 1) * P],
                                                v, start=(kc == 0), stop=(kc == 1))
                        ins.then_inc(pv_ready, 1)
                parts = parts_before(2 * l) + NORM_PARTS
                turn(3 * l + 1, 0, [(h_ready, parts + 1), (h_ready, parts + 2), (o_ready, base + JOBS - 1),
                                       (o_ready, base + JOBS)])
                for n in range(2):
                    columns(place, 16 + 4 * n, hT_hi, hT_lo, TOKS, (4 + 2 * n, 5 + 2 * n), FB,
                            None if n else (tT_lo, 4 * (3 * l + 1)))
                turn_norm(3 * l + 2, 2 * l + 1, 0)

            def turn_act(count, toks, banks, chunks):
                pe.wait_ge(act_ready, count)
                for t in range(toks):
                    a = act[toks][:, t, 0:chunks * P].rearrange("p (m c) -> p c m", c=chunks)
                    for c in range(chunks):
                        ins = pe.transpose(bank[banks[t]][:, c * P:(c + 1) * P], a[:, c, :], ident[:, :])
                    ins.then_inc(act_turned, 1)

            pe.wait_ge(consts, CONSTS)
            attention(0)

            Y = (4, 5, 6, 7)

            def dense_step(place, count, cols, first, since=None):
                if not (isinstance(count, int) and count == 1):
                    pe.wait_ge(silu_ready, count - 1)
                columns(place, 0, hT_hi, hT_lo, TOKS, (0, 1), cols, since)
                if not (isinstance(count, int) and count == 1):
                    pe.wait_ge(aT_lo_ready, (count - 1) * TOKS)
                columns(place, 4, hT_hi, hT_lo, TOKS, (2, 3), cols)
                if first is not None:
                    down(place, 8, TOKS, Y, FB // P, first, False)
                turn_act(count, TOKS, (2, 3), cols // P)

            dense_step(Place(DENSE_UNIT, DENSE_TILE), 1, FB, None, (tT_lo, 4 * 2))
            dense_step(Place(DENSE_UNIT + 8, DENSE_TILE + 2), 2, FB, True)
            with pe.Fori(0, DENSE_STEPS - 3) as i:
                dense_step(Place(DENSE_UNIT + 8 + STEP_UNITS, DENSE_TILE + 2 + STEP_TILES, fb=i), i + 3, FB, False)
            last = Place(DENSE_UNIT + 8 + STEP_UNITS * (DENSE_STEPS - 2), DENSE_TILE + 2 + STEP_TILES * (DENSE_STEPS - 2))
            dense_step(last, DENSE_STEPS, DENSE_LAST, False)
            pe.wait_ge(aT_lo_ready, DENSE_STEPS * TOKS)
            down(last, 12, TOKS, Y, DENSE_LAST // P, False, True, dense_summed)
            attention(1)

            pe.wait_ge(r_split, 2)
            logits = bank[5][:, 0:TOKS * 2 * EXPERTS].rearrange("p (t n) -> p t n", t=TOKS)
            for k in range(KC):
                for t in range(TOKS):
                    if k % 4 == 0:
                        pe.wait_ge(tT_lo, 4 * 5 + k // 2 + t + 1)
                    tk = slice(t * P, (t + 1) * P)
                    pe.matmul(logits[:, t, :], hT_hi[:, k, tk], r_halves[:, k, :, :].rearrange("p i e -> p (i e)"),
                              start=(k == 0 and t == 0), stop=False, skip_group_check=True)
                    ins = pe.matmul(logits[:, t, 0:EXPERTS], hT_lo[:, k, tk], r_halves[:, k, 0, :],
                                    start=False, stop=(k == KC - 1), skip_group_check=True)
            ins.then_inc(routed_ps, 1)
            pe.wait_ge(mask_ready, 1)
            E = EXPERTS
            m = [mask[:, t, 0:E] for t in range(TOKS)]
            pe.matmul(bank[6][:, 0:E], before[:, :], m[0], start=True, stop=True)
            pe.matmul(bank[6][:, E:2 * E], ones[:, :], m[0], start=True, stop=False)
            pe.matmul(bank[6][:, E:2 * E], before[:, :], m[1], start=False, stop=True)
            pe.matmul(bank[6][:, 2 * E:3 * E], ones[:, :], m[0], start=True, stop=False)
            pe.matmul(bank[6][:, 2 * E:3 * E], ones[:, :], m[1], start=False, stop=True).then_inc(ranked_ps, 1)

            def experts(unit0, tile0, fb0, tok0, e0):
                def gather(e):
                    pe.wait_ge(pick_ready, e + (e0 + 1))
                    for g in range(4):
                        src = (h_hi, h_lo)[g % 2]
                        if isinstance(e, int) and e0 == 0 and g < 2:
                            pe.wait_ge(*((h_hi_ready, TOKS) if g == 0 else (h_split, TOKS)))
                        for c in range(4):
                            k = 4 * (g // 2) + c
                            for t in range(TOKS):
                                ins = pe.matmul(bank[GATHER_BANKS[g]][:, c * P:(c + 1) * P], src[:, t, k * P:(k + 1) * P],
                                                pick[:, t, :], start=(t == 0), stop=(t == TOKS - 1))
                        ins.then_inc(gathered, 1)

                def gate(e, place):
                    columns(place, 0, g_hi, g_lo, 1, (0,), FB, (g_ready, (e + e0) * 4))

                def turn_pick(e):
                    if isinstance(e, int) and e == e0 == 0:
                        pe.wait_ge(flag_ready, 1)
                    for t in range(TOKS):
                        pe.transpose(bank[5][:, t * P:(t + 1) * P], pick[:, t, :].bitcast(F32), ident[:, :])
                    for t in range(TOKS):
                        col = share[:, t, e:e + 1] if isinstance(e, int) else share[:, t, bass.ds(e, 1)]
                        ins = pe.matmul(bank[5][:, S:S + 1], pick[:, t, :].bitcast(F32), col, start=(t == 0), stop=(t == TOKS - 1))
                    ins.then_inc(pick_turned, 1)

                def steps(e, reg):
                    step = Place(unit0 + 8, tile0 + 2, e=reg)
                    if reg is None:
                        step = step.plus(e * EXPERT_UNITS, e * EXPERT_TILES)
                    pe.wait_ge(silu_ready, e * STEPS + (fb0 + 1))
                    columns(step, 0, g_hi, g_lo, 1, (0,), FB)
                    turn_act(e * STEPS + (fb0 + 1), 1, (2,), FB // P)
                    columns(step, 4, g_hi, g_lo, 1, (1,), FB)
                    pe.wait_ge(aT_lo_ready, e * STEPS + (tok0 + 1))
                    pe.wait_ge(pickT_ready, e + (e0 + 1))
                    pe.wait_ge(scatter_added, (e + e0) * 4 + 4)
                    down(step, 8, 1, (5, 6), FB // P, True, False)
                    turn_act(e * STEPS + (fb0 + 2), 1, (2,), FB // P)
                    with pe.Fori(0, STEPS - 2) as i:
                        step = Place(step.unit + STEP_UNITS, step.tile + STEP_TILES, e=reg, fb=i)
                        pe.wait_ge(silu_ready, e * STEPS + i + (fb0 + 2))
                        columns(step, 0, g_hi, g_lo, 1, (0,), FB)
                        columns(step, 4, g_hi, g_lo, 1, (1,), FB)
                        pe.wait_ge(aT_lo_ready, e * STEPS + i + (tok0 + 2))
                        down(step, 8, 1, (5, 6), FB // P, False, False)
                        turn_act(e * STEPS + i + (fb0 + 3), 1, (2,), FB // P)
                    return Place(step.unit + STEP_UNITS * (STEPS - 2), step.tile + STEP_TILES * (STEPS - 2), e=reg)

                def finish(e, place):
                    pe.wait_ge(aT_lo_ready, e * STEPS + (tok0 + STEPS))
                    down(place, 0, 1, (5, 6), FB // P, False, True)

                def scatter(e):
                    for g in range(4):
                        t, half = g % 2, g // 2
                        pe.wait_ge(y_lo_ready, (e + e0) * 2 + half + 1)
                        part = slice(half * 512, (half + 1) * 512)
                        pe.matmul(bank[SCATTER_BANKS[g]], pickT[:, t, :], y_hi[:, part], start=True, stop=False)
                        pe.matmul(bank[SCATTER_BANKS[g]], pickT[:, t, :], y_lo[:, part], start=False, stop=True).then_inc(scattered, 1)

                first = Place(unit0, tile0)
                gather(0)
                gate(0, first)
                columns(first, 4, g_hi, g_lo, 1, (1,), FB)
                turn_pick(0)
                with pe.Fori(0, EXPERTS - 1) as e:
                    tail = steps(e, e)
                    gather(e + 1)
                    finish(e, tail)
                    nxt = tail.plus(4, 1)
                    gate(e + 1, nxt)
                    columns(nxt, 4, g_hi, g_lo, 1, (1,), FB)
                    scatter(e)
                    turn_pick(e + 1)
                tail = steps(EXPERTS - 1, None)
                finish(EXPERTS - 1, tail)
                scatter(EXPERTS - 1)

            experts(MOE_UNIT, MOE_TILE, DENSE_STEPS, DENSE_STEPS * TOKS, 0)
            pe.wait_ge(flag_ready, 1)
            some_over = pe.value_load(over_i[0:1, 0:1], min_val=0, max_val=1)
            with pe.If(some_over == 1):
                experts(MOE_UNIT + EXPERTS * EXPERT_UNITS, MOE_TILE + EXPERTS * EXPERT_TILES,
                        DENSE_STEPS + EXPERTS * STEPS, DENSE_STEPS * TOKS + EXPERTS * STEPS, EXPERTS)


_INS = ["x", "positions", "w_in", "w_out", "norm_mix", "norm_ffn", "da_lambda_q1", "da_lambda_k1", "da_lambda_q2",
        "da_lambda_k2", "da_subln", "mla_q_norm", "mla_w_uq", "mla_kv_norm", "mla_w_ukv", "ffn_w_gate", "ffn_w_up",
        "ffn_w_down", "moe_router", "moe_w_gate", "moe_w_up", "moe_w_down", "norm_final"]


def kernel(**inputs):
    import concourse.bacc as _bacc
    from concourse.bass_utils import run_bass_kernel_spmd as _run

    nc = _bacc.Bacc("TRN2", target_bir_lowering=False, num_devices=1, dynamic_dma_scratch_size=1024)
    arrays, args = {}, []
    for name in _INS + ["rope_freqs"]:
        a = rope_freqs() if name == "rope_freqs" else np.ascontiguousarray(inputs[name])
        arrays[f"in_{name}"] = a
        args.append(nc.dram_tensor(f"in_{name}", a.shape, mybir.dt.from_np(a.dtype), kind="ExternalInput").ap())
    out = nc.dram_tensor("out_x", (1, S, D), mybir.dt.float32, kind="ExternalOutput").ap()
    encoder(nc, *args, out)
    r = _run(nc, [arrays], core_ids=[0])
    return r.results[0]["out_x"]
```
